# Optimizing a Trainium2 kernel written in Bass

```python
import numpy as np
import jax
import jax.numpy as jnp
from jax import lax

D_MODEL = 1024
BATCH = 1
SEQ = 512
DEPTH = 2
DEC_BATCH = 1
DEC_SEQ = 32
PAST_LEN = 1024

CHUNK = 64
Q_BLOCK = 128
N_MEM = 256
EPS = 1e-6
NEG_BIG = -1e30
EXP_CLIP = 80.0
FOX_HEADS = 8
FOX_DIM = 64
FOX_BIAS_INIT = 2.0
MLA_HEADS = 4
MLA_Q_RANK = 384
MLA_KV_RANK = 256
MLA_NOPE = 128
MLA_ROPE = 64
MLA_V = 128
ROPE_THETA = 10000.0
HG_HEADS = 4
HG_DK = 128
HG_DV = 128
X_HEADS = 4
X_DIM = 128
D_FF = 4 * D_MODEL
N_BRANCH = 3
BRANCH_W = 512
IN_SIZES = (FOX_HEADS * FOX_DIM, FOX_HEADS * FOX_DIM, FOX_HEADS * FOX_DIM, FOX_HEADS,
            MLA_Q_RANK, MLA_KV_RANK, MLA_ROPE,
            HG_HEADS * HG_DK, HG_HEADS * HG_DK, HG_HEADS * HG_DV, HG_HEADS * HG_DV,
            D_MODEL, D_MODEL, D_MODEL)
D_IN = sum(IN_SIZES)

kernel_name = 'hybrid_streaming_encoder_step'

def rmsnorm(x, g):
    xf = x.astype(jnp.float32)
    y = xf * lax.rsqrt(jnp.mean(xf * xf, axis=-1, keepdims=True) + EPS)
    return (y * g.astype(jnp.float32)).astype(x.dtype)

def rope(x, pos):
    half = MLA_ROPE // 2
    freq = ROPE_THETA ** (-jnp.arange(half, dtype=jnp.float32) / half)
    ang = pos.astype(jnp.float32)[:, None] * freq[None, :]
    shape = (pos.shape[0],) + (1,) * (x.ndim - 3) + (half,)
    cos, sin = jnp.cos(ang).reshape(shape), jnp.sin(ang).reshape(shape)
    x1 = x[..., :half].astype(jnp.float32)
    x2 = x[..., half:].astype(jnp.float32)
    return jnp.concatenate([x1 * cos - x2 * sin, x2 * cos + x1 * sin], axis=-1).astype(x.dtype)

def attend(q, k, v, bias, mask, scale):
    s = jnp.einsum('bthd,bshd->bhts', q, k).astype(jnp.float32) * scale
    if bias is not None:
        s = s + bias
    if mask is not None:
        s = jnp.where(mask, s, NEG_BIG)
    p = jax.nn.softmax(s, axis=-1).astype(v.dtype)
    return jnp.einsum('bhts,bshd->bthd', p, v)

def fox_block(q, k, v, cum_q, cum_k, qpos, kpos):
    bias = jnp.swapaxes(cum_q, 1, 2)[..., :, None] - jnp.swapaxes(cum_k, 1, 2)[..., None, :]
    mask = qpos[:, None] >= kpos[None, :]
    return attend(q, k, v, bias, mask, FOX_DIM ** -0.5)

def fox_prompt(q, k, v, logf):
    S = q.shape[1]
    cum = jnp.cumsum(logf.astype(jnp.float32), axis=1)
    pos = jnp.arange(S)
    outs = []
    for lo in range(0, S, Q_BLOCK):
        hi = lo + Q_BLOCK
        outs.append(fox_block(q[:, lo:hi], k[:, :hi], v[:, :hi], cum[:, lo:hi], cum[:, :hi],
                              pos[lo:hi], pos[:hi]))
    return jnp.concatenate(outs, axis=1)

def fox_sample(q, k, v, logf, c_k, c_v, c_logf):
    P, T = c_k.shape[1], q.shape[1]
    k_all = jnp.concatenate([c_k, k], axis=1)
    v_all = jnp.concatenate([c_v, v], axis=1)
    cum = jnp.cumsum(jnp.concatenate([c_logf.astype(jnp.float32), logf], axis=1), axis=1)
    return fox_block(q, k_all, v_all, cum[:, P:], cum, P + jnp.arange(T), jnp.arange(P + T))

def mla_query(c_q, pos, g_q, w_uq):
    B, T, _ = c_q.shape
    q = (rmsnorm(c_q, g_q) @ w_uq).reshape(B, T, MLA_HEADS, MLA_NOPE + MLA_ROPE)
    return jnp.concatenate([q[..., :MLA_NOPE], rope(q[..., MLA_NOPE:], pos).astype(q.dtype)], axis=-1)

def mla_keys_values(ckv_n, kpe_r, w_ukv):
    B, S, _ = ckv_n.shape
    kv = (ckv_n @ w_ukv).reshape(B, S, MLA_HEADS, MLA_NOPE + MLA_V)
    k_pe = jnp.broadcast_to(kpe_r[:, :, None, :], (B, S, MLA_HEADS, MLA_ROPE)).astype(kv.dtype)
    return jnp.concatenate([kv[..., :MLA_NOPE], k_pe], axis=-1), kv[..., MLA_NOPE:]

def mla_block(q, k, v, qpos, kpos):
    mask = (qpos[:, None] // CHUNK) >= (kpos[None, :] // CHUNK)
    return attend(q, k, v, None, mask, (MLA_NOPE + MLA_ROPE) ** -0.5)

def mla_prompt(q, k, v, pos):
    outs = []
    for lo in range(0, q.shape[1], Q_BLOCK):
        hi = lo + Q_BLOCK
        outs.append(mla_block(q[:, lo:hi], k[:, :hi], v[:, :hi], pos[lo:hi], pos[:hi]))
    return jnp.concatenate(outs, axis=1)

def hgrn_chunk(S, q, k, v, logf):
    q = q.astype(jnp.float32)
    k = k.astype(jnp.float32)
    v = v.astype(jnp.float32)
    L = q.shape[1]
    lc = jnp.cumsum(logf, axis=1)
    diff = lc[:, :, None] - lc[:, None, :]
    causal = jnp.tril(jnp.ones((L, L), dtype=bool))[None, :, :, None, None]
    decay = jnp.where(causal, jnp.exp(jnp.minimum(diff, 0.0)), 0.0)
    a = jnp.einsum('bthc,bshc,btshc->bhts', q, k, decay)
    o = jnp.einsum('bhts,bshv->bthv', a, v) + jnp.einsum('bthc,bhcv->bthv', q * jnp.exp(lc), S)
    last = lc[:, -1]
    S_new = jnp.exp(last)[..., None] * S + jnp.einsum('bshc,bshv->bhcv', k * jnp.exp(last[:, None] - lc), v)
    return S_new, o

def hgrn_prompt(q, k, v, logf):
    B, S = q.shape[:2]
    n = S // CHUNK

    def to_chunks(a):
        return a.reshape((B, n, CHUNK) + a.shape[2:]).swapaxes(0, 1)

    S0 = jnp.zeros((B, HG_HEADS, HG_DK, HG_DV), jnp.float32)
    state, o = lax.scan(lambda st, xs: hgrn_chunk(st, *xs), S0,
                        (to_chunks(q), to_chunks(k), to_chunks(v), to_chunks(logf)))
    return o.swapaxes(0, 1).reshape(B, S, HG_HEADS, HG_DV), state

def trunk_layer(x, pos, past, mem_k, mem_v, lb, w_in, b_fox, g_mla_q, w_mla_uq, g_mla_kv, w_mla_ukv,
                g_hgrn_out, w_branch, w_out, w_xq, w_xo, w_up, w_down, g_norm):
    B, T, _ = x.shape
    h = rmsnorm(x, g_norm[0])
    idx = np.cumsum(IN_SIZES)[:-1].tolist()
    (fq, fk, fv, ff, cq, ckv, kpe, hq, hf, hi, hg, ga, gb, gc) = jnp.split(h @ w_in, idx, axis=-1)
    fq = fq.reshape(B, T, FOX_HEADS, FOX_DIM)
    fk = fk.reshape(B, T, FOX_HEADS, FOX_DIM)
    fv = fv.reshape(B, T, FOX_HEADS, FOX_DIM)
    f_logf = jax.nn.log_sigmoid(ff.astype(jnp.float32) + b_fox.astype(jnp.float32))
    q_m = mla_query(cq, pos, g_mla_q, w_mla_uq)
    ckv_n = rmsnorm(ckv, g_mla_kv)
    kpe_r = rope(kpe, pos)
    zf = hf.astype(jnp.float32).reshape(B, T, HG_HEADS, HG_DK)
    lbh = lb.reshape(HG_HEADS, HG_DK)
    h_logf = jax.nn.log_sigmoid(zf) + jnp.log1p(lbh * jnp.exp(jnp.minimum(-zf, EXP_CLIP)))
    h_k = (1.0 - lbh) * jax.nn.sigmoid(-zf)
    hq = hq.reshape(B, T, HG_HEADS, HG_DK)
    hi = hi.reshape(B, T, HG_HEADS, HG_DV)
    if past is None:
        o_fox = fox_prompt(fq, fk, fv, f_logf)
        k_m, v_m = mla_keys_values(ckv_n, kpe_r, w_mla_ukv)
        o_mla = mla_prompt(q_m, k_m, v_m, pos)
        o_hg, hg_state = hgrn_prompt(hq, h_k, hi, h_logf)
    else:
        c_fk, c_fv, c_flogf, c_ckv, c_kpe, c_hg = past
        P = c_fk.shape[1]
        o_fox = fox_sample(fq, fk, fv, f_logf, c_fk, c_fv, c_flogf)
        k_m, v_m = mla_keys_values(jnp.concatenate([c_ckv, ckv_n], axis=1),
                                   jnp.concatenate([c_kpe, kpe_r], axis=1), w_mla_ukv)
        o_mla = mla_block(q_m, k_m, v_m, pos, jnp.arange(P + T))
        hg_state, o_hg = hgrn_chunk(c_hg.astype(jnp.float32), hq, h_k, hi, h_logf)
    o_hg = (rmsnorm(o_hg, g_hgrn_out) * jax.nn.sigmoid(hg.astype(jnp.float32)).reshape(B, T, HG_HEADS, HG_DV)).astype(x.dtype)
    merged = (jax.nn.sigmoid(ga) * (o_fox.reshape(B, T, BRANCH_W) @ w_branch[0])
              + jax.nn.sigmoid(gb) * (o_mla.reshape(B, T, BRANCH_W) @ w_branch[1])
              + jax.nn.sigmoid(gc) * (o_hg.reshape(B, T, BRANCH_W) @ w_branch[2]))
    x = x + rmsnorm(merged @ w_out, g_norm[1])
    h = rmsnorm(x, g_norm[2])
    qx = (h @ w_xq).reshape(B, T, X_HEADS, X_DIM)
    ox = attend(qx, mem_k, mem_v, None, None, X_DIM ** -0.5).reshape(B, T, X_HEADS * X_DIM)
    x = x + rmsnorm(ox @ w_xo, g_norm[3])
    h = rmsnorm(x, g_norm[4])
    u = jnp.square(jax.nn.relu(h @ w_up)) @ w_down
    x = x + rmsnorm(u, g_norm[5])
    return x, (fk, fv, f_logf, ckv_n, kpe_r, hg_state)

def setup_inputs(seed: int = 0) -> dict:
    key = jax.random.key(seed)
    ks = jax.random.split(key, 28)

    def nrm(i, shape, scale=1.0):
        return scale * jax.random.normal(ks[i], shape, jnp.float32)

    return {
        'x_prompt': nrm(0, (BATCH, SEQ, D_MODEL)),
        'x_sample': nrm(1, (DEC_BATCH, DEC_SEQ, D_MODEL)),
        'cache_fox_k': nrm(2, (DEPTH, DEC_BATCH, PAST_LEN, FOX_HEADS, FOX_DIM)),
        'cache_fox_v': nrm(3, (DEPTH, DEC_BATCH, PAST_LEN, FOX_HEADS, FOX_DIM)),
        'cache_fox_logf': jax.nn.log_sigmoid(nrm(4, (DEPTH, DEC_BATCH, PAST_LEN, FOX_HEADS)) + FOX_BIAS_INIT),
        'cache_mla_ckv': nrm(5, (DEPTH, DEC_BATCH, PAST_LEN, MLA_KV_RANK)),
        'cache_mla_kpe': nrm(6, (DEPTH, DEC_BATCH, PAST_LEN, MLA_ROPE)),
        'state_hgrn': nrm(7, (DEPTH, DEC_BATCH, HG_HEADS, HG_DK, HG_DV), 0.5),
        'cache_mem_k': nrm(8, (DEPTH, DEC_BATCH, N_MEM, X_HEADS, X_DIM)),
        'cache_mem_v': nrm(9, (DEPTH, DEC_BATCH, N_MEM, X_HEADS, X_DIM)),
        'mem_prompt': nrm(10, (BATCH, N_MEM, D_MODEL)),
        'w_in': nrm(11, (DEPTH, D_MODEL, D_IN), D_MODEL ** -0.5),
        'b_fox': FOX_BIAS_INIT + nrm(12, (DEPTH, FOX_HEADS), 0.1),
        'g_mla_q': 1.0 + nrm(13, (DEPTH, MLA_Q_RANK), 0.05),
        'w_mla_uq': nrm(14, (DEPTH, MLA_Q_RANK, MLA_HEADS * (MLA_NOPE + MLA_ROPE)), MLA_Q_RANK ** -0.5),
        'g_mla_kv': 1.0 + nrm(15, (DEPTH, MLA_KV_RANK), 0.05),
        'w_mla_ukv': nrm(16, (DEPTH, MLA_KV_RANK, MLA_HEADS * (MLA_NOPE + MLA_V)), MLA_KV_RANK ** -0.5),
        'g_hgrn_out': 1.0 + nrm(17, (DEPTH, HG_DV), 0.05),
        'lb_hgrn': nrm(18, (DEPTH, HG_HEADS * HG_DK), 0.1),
        'w_branch': nrm(19, (DEPTH, N_BRANCH, BRANCH_W, D_MODEL), BRANCH_W ** -0.5),
        'w_out': nrm(20, (DEPTH, D_MODEL, D_MODEL), D_MODEL ** -0.5),
        'w_xq': nrm(21, (DEPTH, D_MODEL, X_HEADS * X_DIM), D_MODEL ** -0.5),
        'w_mem_k': nrm(22, (DEPTH, D_MODEL, X_HEADS * X_DIM), D_MODEL ** -0.5),
        'w_mem_v': nrm(23, (DEPTH, D_MODEL, X_HEADS * X_DIM), D_MODEL ** -0.5),
        'w_xo': nrm(24, (DEPTH, X_HEADS * X_DIM, D_MODEL), (X_HEADS * X_DIM) ** -0.5),
        'w_up': nrm(25, (DEPTH, D_MODEL, D_FF), D_MODEL ** -0.5),
        'w_down': nrm(26, (DEPTH, D_FF, D_MODEL), D_FF ** -0.5),
        'g_norm': 1.0 + nrm(27, (DEPTH, 6, D_MODEL), 0.05),
    }

def reference(x_prompt, x_sample, cache_fox_k, cache_fox_v, cache_fox_logf, cache_mla_ckv, cache_mla_kpe,
              state_hgrn, cache_mem_k, cache_mem_v, mem_prompt, w_in, b_fox, g_mla_q, w_mla_uq, g_mla_kv,
              w_mla_ukv, g_hgrn_out, lb_hgrn, w_branch, w_out, w_xq, w_mem_k, w_mem_v, w_xo, w_up, w_down,
              g_norm):
    lb_p = jax.nn.softmax(lb_hgrn.astype(jnp.float32), axis=0)
    lb_all = jnp.cumsum(lb_p, axis=0) - lb_p[0]

    def layer(x, pos, past, mk, mv, l):
        return trunk_layer(x, pos, past, mk, mv, lb_all[l], w_in[l], b_fox[l], g_mla_q[l], w_mla_uq[l],
                           g_mla_kv[l], w_mla_ukv[l], g_hgrn_out[l], w_branch[l], w_out[l], w_xq[l],
                           w_xo[l], w_up[l], w_down[l], g_norm[l])

    Bp, Sp, _ = x_prompt.shape
    pos_p = jnp.arange(Sp)
    x = x_prompt
    p_states = []
    for l in range(DEPTH):
        mk = (mem_prompt @ w_mem_k[l]).reshape(Bp, N_MEM, X_HEADS, X_DIM)
        mv = (mem_prompt @ w_mem_v[l]).reshape(Bp, N_MEM, X_HEADS, X_DIM)
        x, st = layer(x, pos_p, None, mk, mv, l)
        p_states.append(st + (mk, mv))
    y_prompt = x
    (p_fox_k, p_fox_v, p_fox_logf, p_mla_ckv, p_mla_kpe, p_hgrn_state, p_mem_k,
     p_mem_v) = [jnp.stack(a) for a in zip(*p_states)]

    past_len = cache_fox_k.shape[2]
    pos_s = past_len + jnp.arange(x_sample.shape[1])
    x = x_sample
    s_states = []
    for l in range(DEPTH):
        past = (cache_fox_k[l], cache_fox_v[l], cache_fox_logf[l], cache_mla_ckv[l], cache_mla_kpe[l],
                state_hgrn[l])
        x, st = layer(x, pos_s, past, cache_mem_k[l], cache_mem_v[l], l)
        s_states.append(st)
    y_sample = x
    (s_fox_k, s_fox_v, s_fox_logf, s_mla_ckv, s_mla_kpe,
     s_hgrn_state) = [jnp.stack(a) for a in zip(*s_states)]

    return (y_prompt, y_sample, p_fox_k, p_fox_v, p_fox_logf, p_mla_ckv, p_mla_kpe, p_hgrn_state,
            p_mem_k, p_mem_v, s_fox_k, s_fox_v, s_fox_logf, s_mla_ckv, s_mla_kpe, s_hgrn_state)


_drawn_inputs = setup_inputs


def setup_inputs(seed=0):
    import zlib

    import numpy as np

    out = dict(_drawn_inputs(seed))
    spreads = {}
    factors = {'g_mla_q': 6.738}
    for name, (base, spread) in spreads.items():
        noise = np.random.default_rng([zlib.crc32(name.encode()), seed]).standard_normal(out[name].shape)
        drawn = base * np.exp(spread * noise) if base else spread * noise
        out[name] = jnp.asarray(drawn.astype(out[name].dtype))
    for name, factor in factors.items():
        out[name] = (out[name] * factor).astype(out[name].dtype)
    return out
```

```python
from contextlib import ExitStack

import numpy as np

import concourse.bass as bass
from concourse import mybir

F32 = mybir.dt.float32
F32R = mybir.dt.float32r
U8 = mybir.dt.uint8
ALU = mybir.AluOpType
ACT = mybir.ActivationFunctionType
AX = mybir.AxisListType

P = 128
D_MODEL, SEQ, DEPTH, DEC_SEQ, PAST_LEN = 1024, 512, 2, 32, 1024
CHUNK, N_MEM, EPS, NEG_BIG, EXP_CLIP = 64, 256, 1e-6, -1e30, 80.0
FOX_HEADS, FOX_DIM = 8, 64
MLA_HEADS, MLA_Q_RANK, MLA_KV_RANK, MLA_NOPE, MLA_ROPE, MLA_V = 4, 384, 256, 128, 64, 128
ROPE_THETA = 10000.0
HG_HEADS, HG_DIM = 4, 128
X_HEADS, X_DIM = 4, 128
D_FF = 4 * D_MODEL
BRANCH_W = 512

NT = SEQ + DEC_SEQ
HALF = NT // 2
TB = SEQ // P
KT = D_MODEL // P
MT = MLA_KV_RANK // P
QT = MLA_Q_RANK // P
MB = N_MEM // P
CB = PAST_LEN // P
CACHED = PAST_LEN + DEC_SEQ
RAW, SPLIT = 4, 2
MLP_GROUPS = D_FF // D_MODEL

C_FQ, C_FK, C_FV, C_FF = 0, 512, 1024, 1536
C_CQ = C_FF + FOX_HEADS
C_CKV = C_CQ + MLA_Q_RANK
C_KPE = C_CKV + MLA_KV_RANK
C_HQ = C_KPE + MLA_ROPE
C_HF, C_HI, C_HG = C_HQ + 512, C_HQ + 1024, C_HQ + 1536
C_GATE = C_HQ + 2048

K_ID, K_ONES, K_CAUSAL, K_CHUNK, K_SAMPLE, K_ROT = 0, 128, 256, 384, 512, 544
K_COS, K_SIN, K_RESET, K_SEL = 672, 672 + NT, 672 + 2 * NT, 672 + 3 * NT
K_HEAD = K_SEL + 256
K_END = K_HEAD + FOX_HEADS
V_NORM, V_CQ, V_CKV, V_HG, V_LB, V_ROWS = 0, 48, 51, 53, 54, 62

LEVELS = [64, 32, 16, 8, 4, 2, 1]
NL = len(LEVELS) + 1
LOW_ROWS = 32
BIG, SMALL = 2.0 ** 60, 2.0 ** -60
assert PAST_LEN % CHUNK == 0 and DEC_SEQ <= CHUNK


class Turns:

    def __init__(self):
        self.fills, self.uses, self.of = {}, {}, {}

    def add(self, bank, name, parts=1):
        assert name not in self.of, name
        fills, uses = self.fills.get(bank, 0), self.uses.get(bank, 0)
        self.fills[bank], self.uses[bank] = fills + parts, uses + 1
        self.of[name] = (bank, fills, uses, parts)


def weight_slots():
    s = []

    def w_in(col, n, name):
        s.extend(("w_in", 0, KT, col + P * i, P, [(name, i)]) for i in range(n))

    def branch(b):
        for j in range(KT // 2):
            for n in (2 * j, 2 * j + 1):
                s.append(("w_in", 0, KT, C_GATE + D_MODEL * b + P * n, P, [("gate", b, n)]))
            s.append((f"w_branch{b}", 0, 4, 256 * j, 256, [("br", b, 2 * j), ("br", b, 2 * j + 1)]))

    w_in(C_FQ, 4, "fq"), w_in(C_FK, 4, "fk"), w_in(C_FV, 4, "fv"), w_in(C_FF, 1, "ff")
    branch(0)
    w_in(C_CQ, QT, "cq"), w_in(C_CKV, MT, "ckv")
    s.append(("kpe", 0, KT, C_KPE, MLA_ROPE, [("kpe", 0)]))
    branch(1)
    w_in(C_HF, 4, "hf"), w_in(C_HG, 4, "hg"), w_in(C_HQ, 4, "hq"), w_in(C_HI, 4, "hi")
    branch(2)
    s.extend(("w_out", 0, KT, P * n, P, [("out", n)]) for n in range(KT))
    s.extend(("w_mem_k", 0, KT, P * n, P, [("memk", n)]) for n in range(4))
    s.extend(("w_mem_v", 0, KT, P * n, P, [("memv", n)]) for n in range(4))
    s.extend(("w_xq", 0, KT, P * n, P, [("xq", n)]) for n in range(4))
    s.extend(("w_xo", 0, 4, 256 * j, 256, [("xo", 2 * j), ("xo", 2 * j + 1)]) for j in range(4))
    for g in range(1):
        s.extend(("w_up", 0, KT, P * n, P, [("up", n)]) for n in range(KT))
        s.extend(("w_down", 0, KT, P * n, P, [("down", n)]) for n in range(KT))
    return s


SLOTS = weight_slots()
SLOT_OF = {name: n for n, s in enumerate(SLOTS) for name in s[5]}
MLP0 = SLOT_OF["up", 0]
MLP_N = 2 * KT
HG_STEP_U, HG_STEP_O = 0, 2


def prompt_units(heads, causal):
    return [(qb, h) for qb in range(TB) for h in range(heads)]


def plan_layer():
    t = Turns()
    count = {"g": 0, "t": 0}

    def gemm(*names):
        for n in names:
            t.add(f"G{count['g'] % 2}", n)
            count["g"] += 1

    def tr(name):
        t.add("TO"[count["t"] % 2], name)
        count["t"] += 1

    def stat(k):
        t.add("A0", ("stat", k, 0)), t.add("A1", ("stat", k, 1))

    def tokens(kind):
        for tb in range(TB + 1):
            tr((kind, "tok", tb))

    def attention(kind, heads):
        n = TB * heads
        for i in range(n + 2):
            if i < n:
                t.add(f"A{i % 2}", (kind, "S", i))
            if 1 <= i <= n:
                gemm((kind, "PT", i - 1))
            if i >= 2 and (i - 2) % heads == 0:
                t.add("O", (kind, "O", (i - 2) // heads), heads)

    def sample(kind, banks=("A0", "A1", "T"), batches=3):
        for b in banks:
            t.add(b, (kind, "S", b))
        for j in range(batches):
            tr((kind, "PT", j))
        t.add("A0", (kind, "PV"))

    def to_features(kind):
        for f in range(4):
            tr((kind, "feat", f))

    def branch(b):
        for j in range(KT // 2):
            gemm(("gate", b, 2 * j), ("gate", b, 2 * j + 1), ("br", b, 2 * j), ("br", b, 2 * j + 1))

    tr(("vec",))
    stat(0)
    gemm(*[("fq", n) for n in range(4)], *[("fk", n) for n in range(4)], *[("fv", n) for n in range(4)])
    gemm(("ff", 0))
    tokens("fk"), tokens("fv")
    for tb in range(TB + 1):
        tr(("flogf", tb))
    tr(("clogf", 0)), tr(("clogf", 1))
    attention("fox", FOX_HEADS)
    for g in range(2):
        for j in range(4):
            tr(("foxs", g, "KT", j))
        sample(("foxs", g))
    to_features("fox")
    branch(0)
    gemm(*[("cq", n) for n in range(QT)])
    gemm(*[("ckv", n) for n in range(MT)], ("kpe", 0))
    stat(1), stat(2)
    t.add("A0", ("rot", 0, 0)), t.add("A1", ("rot", 0, 1))
    gemm(*[("qn", h) for h in range(4)], ("qpe", 0), ("qpe", 1))
    for j in (1, 2):
        t.add("A0", ("rot", j, 0)), t.add("A1", ("rot", j, 1))
    tokens("ckv")
    for h in range(4):
        gemm(("kn", h))
    for tb in range(TB):
        gemm(("vm", tb))
    attention("mla", MLA_HEADS)
    for j in range(4):
        tr(("mlas", "ckvT", j))
    for j in range(2):
        tr(("mlas", "kpeT", j))
    for j in range(2):
        tr(("mlas", "wukT", j))
    t.add("A0", ("mlas", "qabs"))
    sample("mlas")
    t.add("A1", ("mlas", "o"))
    to_features("mla")
    branch(1)
    gemm(*[(k, n) for k in ("hf", "hg", "hq", "hi") for n in range(4)])
    tokens("hi")
    for h in range(HG_HEADS + 1):
        for lv in range(NL):
            if h < HG_HEADS:
                gemm(("hgA", h, lv))
            if h and lv == HG_STEP_U:
                t.add("A0", ("hg", "U", h - 1)), t.add("A1", ("hg", "Us", h - 1))
            if h and lv == HG_STEP_O:
                tr(("hg", "O", h - 1)), tr(("hg", "Os", h - 1))
        if h < HG_HEADS:
            tr(("hg", "kdT", h)), tr(("hg", "kdTs", h))
    for f in range(4):
        tr(("hg", "feat", f)), tr(("hg", "feats", f))
    branch(2)
    gemm(*[("out", n) for n in range(KT)])
    stat(3)
    for j in range(4):
        tr(("memT", j))
    gemm(*[("memk", n) for n in range(4)], *[("memv", n) for n in range(4)])
    for b in range(MB):
        tr(("memk", "tok", b))
    for b in range(MB):
        tr(("memv", "tok", b))
    stat(4)
    gemm(*[("xq", n) for n in range(4)])
    attention("x", X_HEADS)
    for j in range(2):
        tr(("xs", "KT", j))
    sample("xs", ("A0",), 1)
    to_features("x")
    gemm(*[("xo", n) for n in range(KT)])
    stat(5)
    stat(6)
    t.mlp = count["g"]
    gemm(*[("up", n) for n in range(KT)], *[("down", n) for n in range(KT)])
    for b in ("G0", "G1"):
        t.fills[b] += (MLP_GROUPS - 1) * MLP_N // 2
        t.uses[b] += (MLP_GROUPS - 1) * MLP_N // 2
    stat(7)
    return t


def plan_ends(kind):
    t = Turns()
    if kind == "in":
        for f in range(KT):
            t.add("TO"[f % 2], ("x", f)), t.add(f"A{f % 2}", ("xs", f))
    else:
        for j in range(2 * (TB + 1)):
            t.add("TO"[j % 2], ("y", j))
    return t


def hybrid_encoder(nc, A, O):
    with ExitStack() as ctx:
        def sb(name, shape, dt=F32):
            return ctx.enter_context(nc.sbuf_tensor(name, shape, dt))

        def sem(name):
            return ctx.enter_context(nc.semaphore(name))

        def alternatives(limit, *groups):
            made = {}
            for group in groups:
                size = sum(int(np.prod(shape[1:])) * 4 for _, shape, _ in group)
                assert limit is None or size <= limit, (group[0][0], size, limit)
                with ExitStack() as inner:
                    for name, shape, dt in group:
                        made[name] = inner.enter_context(nc.sbuf_tensor(name, shape, dt))
            return made

        x = sb("x", [P, KT, NT])
        h_hi, h_lo = sb("h_hi", [P, KT, NT], F32R), sb("h_lo", [P, KT, NT], F32R)
        raw = sb("w_raw", [P, RAW, KT * P])
        w_hi, w_lo = sb("w_hi", [P, SPLIT, KT * P], F32R), sb("w_lo", [P, SPLIT, KT * P], F32R)
        cst = sb("constants", [P, K_END])
        masks = sb("level_masks", [P, NL, P], U8)
        vecs = sb("vecs", [64, P])
        gT = sb("vectors", [P, 64])
        lbsel = sb("lb_select", [P, DEPTH])
        small = sb("small", [P, 32])
        bfox = sb("b_fox_col", [FOX_HEADS, 1])
        eps, zero = sb("eps", [P, 1]), sb("zero", [P, 1])
        head_rows = sb("head_rows", [P, FOX_HEADS], F32R)
        acc_rs = sb("square_sum_and_rs", [P, 2, NT])
        acc, rs, PT = acc_rs[:, 0, :], acc_rs[:, 1, :], acc_rs
        eg = sb("gate_exp", [P, 2, NT])
        negmax, rsum, rinv = sb("negmax", [P, 64]), sb("row_sum", [P, 64]), sb("row_inv", [P, 64])

        RW = 8 * NT
        M = alternatives(
            4 * RW,
            [("U", [P, KT, NT], F32)],
            [("fk_s", [DEC_SEQ, 512], F32), ("fo_tok", [P, TB, 512], F32), ("ncums", [FOX_HEADS, CACHED], F32),
             ("ncum_parts", [P, SEQ], F32R)])
        m_area = sb("m_area", [P, RW])
        R = alternatives(
            8 * RW,
            [("r_hi", [P, KT, NT], F32R), ("r_lo", [P, KT, NT], F32R)],
            [("sq", [P, KT, NT], F32)],
            [("mask32", [P, NL, P], F32)],
            [("fvT", [P, 4, NT], F32)],
            [("fKc", [P, CB, 256], F32), ("fKT", [P, 2, PAST_LEN], F32), ("fVc", [P, CB, 256], F32),
             ("fPs", [P, CACHED], F32), ("fPTs", [P, CB + 1, P], F32)],
            [("ckvc", [P, CB, 256], F32), ("ckvT", [P, MT, PAST_LEN], F32), ("kpec", [P, CB, 128], F32),
             ("kpeT", [P, PAST_LEN], F32), ("wukT", [P, 4, 256], F32), ("qabs", [P, MT, P], F32),
             ("lat", [P, MT, P], F32), ("kpe", [P, NT], F32)],
            [("hgap0", [P, 2176], F32), ("ho_tok", [P, TB, 512], F32), ("hsq", [P, HG_DIM], F32),
             ("hST", [P, TB, P], F32), ("hS0", [P, HG_HEADS, P], F32),
             ("hSf", [P, HG_HEADS, P], F32), ("hAT", [P, 2, TB, P], F32),
             ("hATs", [DEC_SEQ, 2, DEC_SEQ], F32), ("hkd", [P, NT], F32), ("hkdT", [P, TB, P], F32), ("hkdTs", [DEC_SEQ, P], F32),
             ("hqd", [P, NT], F32)],
            [("hviT", [P, 4, NT], F32)],
            [("mgap", [P, KT, NT], F32), ("m_hi", [P, KT, N_MEM], F32R), ("m_lo", [P, KT, N_MEM], F32R)],
        )
        r_area = sb("r_area", [P, 2 * RW])
        S = alternatives(
            None,
            [("x_tok", [P, TB, D_MODEL], F32), ("xs_tok", [DEC_SEQ, D_MODEL], F32)],
            [("fq", [P, FOX_HEADS, NT], F32), ("fk", [P, 4, NT], F32), ("fv_tok", [P, TB, 512], F32),
             ("fv_s", [DEC_SEQ, 512], F32), ("fk_tok", [P, TB, 512], F32),
             ("foS", [P, 4, DEC_SEQ], F32), ("fq_new", [P, FOX_HEADS, DEC_SEQ], F32),
             ("flogT", [FOX_HEADS, NT], F32), ("flogf", [P, TB + 1, FOX_HEADS], F32), ("clogf", [P, CB, FOX_HEADS], F32)],
            [("ckv", [P, MT, NT], F32), ("wukv", [P, MT, 1024], F32),
             ("qn", [P, 4, NT], F32), ("qpe", [P, 2, NT], F32), ("kn", [P, 4, SEQ], F32),
             ("vm", [P, TB, 512], F32), ("ckv_s", [DEC_SEQ, 512], F32), ("moS", [P, 4, DEC_SEQ], F32),
             ("mo_tok", [P, TB, 512], F32)],
            [("z0", [P, MT, NT], F32), ("z2", [P, MT, 1024], F32),
             ("z3", [P, 4, NT], F32), ("z4", [P, 2, NT], F32), ("msP", [P, CACHED], F32),
             ("msPT", [P, CB + 1, P], F32)],
            [("z5", [P, MT, NT], F32), ("z7", [P, MT, 1024], F32),
             ("z8", [P, 4, NT], F32), ("z9", [P, 2, NT], F32),
             ("wuqn", [P, QT, 4, P], F32), ("wuqp", [P, QT, 4, 64], F32), ("cq", [P, QT, NT], F32),
             ("msq", [P, QT, NT], F32)],
            [("hq", [P, 4, NT], F32), ("hf", [P, 4, NT], F32), ("hk", [P, 4, NT], F32), ("hg", [P, 4, NT], F32),
             ("hv", [P, TB, 512], F32), ("hv_s", [DEC_SEQ, 512], F32), ("ho_s", [DEC_SEQ, 512], F32),
             ("hE", [P, 2, NT], F32)],
            [("xq", [P, 4, NT], F32), ("mkT", [P, 4, N_MEM], F32), ("mvT", [P, 4, N_MEM], F32),
             ("mk_tok", [P, MB, 512], F32), ("mv_tok", [P, MB, 512], F32), ("xo_tok", [P, TB, 512], F32),
             ("xoS", [P, 4, DEC_SEQ], F32), ("xsK", [P, MB, 512], F32), ("xsV", [P, MB, 512], F32),
             ("xsKT", [P, 4, N_MEM], F32)],
            [("y0", [P, 4, NT], F32), ("y1", [P, 4, N_MEM], F32), ("y2", [P, 4, N_MEM], F32),
             ("y3", [P, MB, 512], F32), ("y4", [P, MB, 512], F32), ("mem_tok", [P, MB, D_MODEL], F32)],
            [("y5", [P, 4, NT], F32), ("xsP", [P, N_MEM], F32), ("xsPT", [P, MB, P], F32)],
            [("sqx", [P, KT, NT], F32)],
            [("t1", [P, 2, NT], F32), ("t2", [P, 2, NT], F32)],
        )

        psum = ctx.enter_context(nc.psum_tensor("psum", [P, 8, 512], F32))
        BANK = {"G0": psum[:, 0:2, :], "G1": psum[:, 2:4, :], "A0": psum[:, 4, :], "A1": psum[:, 5, :],
                "T": psum[:, 6, :], "O": psum[:, 7, :]}
        SCORES = psum[:, 4:7, :].rearrange("p a b -> p (a b)")
        ident, ones = cst[:, K_ID:K_ID + P], cst[:, K_ONES:K_ONES + P]
        COS, SIN = cst[:, K_COS:K_COS + NT], cst[:, K_SIN:K_SIN + NT]
        SEL = cst[0:FOX_HEADS, K_SEL:K_SEL + 256]
        sq = R["sq"]

        FILLED = {b: sem(f"filled_{b}") for b in BANK}
        EMPTIED = {b: sem(f"emptied_{b}") for b in BANK}
        raw_arrived = [sem(f"raw_arrived_{r}") for r in range(RAW)]
        high_split, weights_split = sem("high_split"), sem("weights_split")
        vector_chain, scalar_chain = sem("vector_chain"), sem("scalar_chain")
        square_ready, square_sum_ready, rs_ready = sem("square_ready"), sem("square_sum_ready"), sem("rs_ready")
        h32_ready, h_hi_ready, h_lo_ready = sem("h32_ready"), sem("h_hi_ready"), sem("h_lo_ready")
        x_ready, u_ready, cqn_ready, rope_ready = sem("x_ready"), sem("u_ready"), sem("cqn_ready"), sem("rope_ready")
        row_max, sample_probs, o_hi_ready = sem("row_max"), sem("sample_probs"), sem("o_hi_ready")
        ff_vector, ff_scalar, ncum_ready = sem("ff_vector"), sem("ff_scalar"), sem("ncum_ready")
        hz_vector, hz_scalar = sem("hz_vector"), sem("hz_scalar")
        hl_diff, hl_exp, hl_scaled = sem("hl_diff"), sem("hl_exp"), sem("hl_scaled")
        hd_diff, hd_exp, hd_scaled = sem("hd_diff"), sem("hd_exp"), sem("hd_scaled")
        zeros_ready = sem("zeros_ready")
        r32_ready, r_hi_ready, r_lo_ready = sem("r32_ready"), sem("r_hi_ready"), sem("r_lo_ready")
        DMA = {n: sem("dma_" + n) for n in (
            "vecs", "state", "foxc", "wuq", "wukv", "mlac", "mem", "xsc", "clogf",
            "k_out", "v_out", "ckv_out", "mem_out", "out", "y_out")}
        CLEARED = [*FILLED.values(), *EMPTIED.values(), *raw_arrived, high_split, weights_split, vector_chain,
                   scalar_chain, square_ready, square_sum_ready, rs_ready, h32_ready, h_hi_ready, h_lo_ready,
                   x_ready, u_ready, cqn_ready, rope_ready, row_max, sample_probs, o_hi_ready, ff_vector,
                   ff_scalar, ncum_ready, hz_vector, hz_scalar, hl_diff, hl_exp, hl_scaled, hd_diff, hd_exp,
                   hd_scaled, zeros_ready, r32_ready, r_hi_ready, r_lo_ready, *DMA.values()]
        consts_loaded, phase_done, phase_go = sem("consts_loaded"), sem("phase_done"), sem("phase_go")

        plan = plan_layer()

        def filled(eng, name, part=None, t=plan, plus=0):
            bank, fills, _, parts = t.of[name]
            eng.wait_ge(FILLED[bank], fills + (parts if part is None else part) + plus)

        def emptied(eng, name, t=plan, plus=0):
            bank, _, uses, _ = t.of[name]
            eng.wait_ge(EMPTIED[bank], uses + 1 + plus)

        def bank_free(pe, name, t=plan, plus=0):
            bank, _, uses, _ = t.of[name]
            if uses:
                pe.wait_ge(EMPTIED[bank], uses + plus)
            return BANK[bank]

        def bank_of(name, t=plan):
            return BANK[t.of[name][0]]

        def one_bank(bank):
            return bank[:, 0, :] if len(bank.shape) == 3 else bank

        def fill_sem(name, t=plan):
            return FILLED[t.of[name][0]]

        def empty_sem(name, t=plan):
            return EMPTIED[t.of[name][0]]

        def both(tile):
            return tile.rearrange("p (a n) -> p a n", a=2)

        def g_tile(name, rows=P):
            return bank_of(name)[0:rows, :, 0:HALF]

        def end_of_phase(eng, n):
            eng.nop().then_inc(phase_done, 1)
            eng.wait_ge(phase_go, n)

        def end_of_phase_sp(sp):
            sp.wait_ge(phase_done, 4)
            for s in [phase_done, *CLEARED]:
                sp.sem_clear(s)
            sp.nop().then_inc(phase_go, 1)

        NORMS = [KT, QT, MT, KT, KT, KT, KT, KT]
        SQ0 = [sum(NORMS[:k]) for k in range(len(NORMS))]
        OHI = {"fox": 0, "mla": 5, "hg": 10, "x": 14, "mem": 19}
        RMAX = {"fox": 0, ("foxs", 0): 32, ("foxs", 1): 33, "mla": 34, "mlas": 50, "x": 51, "xs": 67}
        SPROB = {("foxs", 0): 1, ("foxs", 1): 2, "mlas": 3, "xs": 4}
        HEADS = {"fox": FOX_HEADS, "mla": MLA_HEADS, "x": X_HEADS}
        SCALE = {"fox": 1.0, "mla": (MLA_NOPE + MLA_ROPE) ** -0.5, "x": X_DIM ** -0.5}
        SCALE[("foxs", 0)] = SCALE[("foxs", 1)] = 1.0
        SCALE["mlas"], SCALE["xs"] = SCALE["mla"], SCALE["x"]
        O_TOK = {"fox": M["fo_tok"], "mla": S["mo_tok"], "x": S["xo_tok"], "hg": R["ho_tok"]}
        O_S = {"fox": S["foS"], "mla": S["moS"], "x": S["xoS"]}
        r_hi, r_lo, U = R["r_hi"], R["r_lo"], M["U"]

        VECS = 7 * 16
        SBUF_P = {("foxs", 0): (R["fPs"], R["fPTs"]), ("foxs", 1): (R["fPs"], R["fPTs"]),
                  "mlas": (S["msP"], S["msPT"]), "xs": (S["xsP"], S["xsPT"])}

        def keys(kind, qb):
            return N_MEM if kind == "x" else P * (qb + 1)

        def source(l, matrix, row, kt, col, cols):
            if matrix.startswith("w_branch"):
                w = A["w_branch"][bass.ds(l, 1), int(matrix[-1])]
            else:
                w = A["w_in" if matrix == "kpe" else matrix][bass.ds(l, 1)]
            w = w.rearrange("a r c -> (a r) c")
            return w[row if not isinstance(row, int) else slice(row, row + P * kt), col:col + cols] \
                .rearrange("(k p) c -> p k c", p=P)

        def load_slot(sp, l, s, row=0):
            matrix, _, kt, col, cols, _ = SLOTS[s]
            r = s % RAW
            if s >= RAW:
                sp.wait_ge(weights_split, s - RAW + 1)
            dst = raw[:, r, :].rearrange("p (k c) -> p k c", k=kt)
            src = source(l, matrix, row, kt, col, cols)
            if matrix == "kpe":
                sp.dma_start(dst[:, :, 0:MLA_ROPE], src).then_inc(raw_arrived[r], 16)
                sp.dma_start(dst[:, :, MLA_ROPE:P], src).then_inc(raw_arrived[r], 16)
            else:
                sp.dma_start(dst, src).then_inc(raw_arrived[r], 16)

        def raw_value(s):
            kpe = SLOT_OF["kpe", 0]
            return 16 * (s // RAW + 1) + (16 if s >= kpe and s % RAW == kpe % RAW else 0)

        def sp_layer(sp, l):
            for s in range(MLP0):
                load_slot(sp, l, s)
            with sp.Fori(0, MLP_GROUPS) as g:
                for j in range(MLP_N):
                    s = MLP0 + j
                    matrix, _, kt, col, cols, _ = SLOTS[s]
                    sp.wait_ge(weights_split, g * MLP_N + (s - RAW + 1))
                    w = A[matrix][bass.ds(l, 1)].rearrange("a r c -> (a r) c")
                    if matrix == "w_up":
                        src = w[:, bass.ds(g * D_MODEL + col, P)]
                    else:
                        src = w[bass.ds(g * D_MODEL, D_MODEL), col:col + P]
                    sp.dma_start(raw[:, s % RAW, :].rearrange("p (k c) -> p k c", k=KT),
                                 src.rearrange("(k p) c -> p k c", p=P)).then_inc(raw_arrived[s % RAW], 16)

        def split_slot(pool, s, plus_s=0, plus_t=0, mlp=False):
            pool.wait_ge(raw_arrived[s % RAW], raw_value(s) + plus_s * (16 // RAW))
            if mlp:
                filled(pool, SLOTS[s][5][0], part=0, plus=plus_t)
            elif s >= SPLIT:
                filled(pool, SLOTS[s - SPLIT][5][-1])
            nc.gpsimd.tensor_tensor(w_hi[:, s % SPLIT, :], raw[:, s % RAW, :],
                                    zero[:, 0:1].to_broadcast([P, KT * P]), ALU.add).then_inc(high_split, 1)
            pool.wait_ge(high_split, s + 1 + plus_s)
            nc.gpsimd.tensor_tensor(w_lo[:, s % SPLIT, :], raw[:, s % RAW, :],
                                    w_hi[:, s % SPLIT, :].bitcast(F32), ALU.subtract).then_inc(weights_split, 1)

        def level_view(tile, lv):
            w = 2 * LEVELS[lv]
            return tile[:, 0:SEQ if w > DEC_SEQ else NT].rearrange("p (b w) -> p b w", w=w)

        def hg_difference(eng, i):
            h, lv = i // len(LEVELS), i % len(LEVELS)
            half = LEVELS[lv]
            e, w = level_view(S["hE"][:, i % 2, :], lv), level_view(S["hf"][:, h, :], lv)
            eng.tensor_tensor(e, w, w[:, :, half - 1:half].to_broadcast(list(e.shape)), ALU.subtract) \
                .then_inc(hl_diff, 1)

        def pool_hgrn(pool):
            emptied(pool, ("br", 1, KT - 1)), emptied(pool, ("br", 1, KT - 2))
            nc.gpsimd.memset(R["hAT"][:, :, :, :], 0.0).then_inc(zeros_ready, 1)
            nc.gpsimd.memset(R["hATs"][:, :, :], 0.0).then_inc(zeros_ready, 1)
            pool.wait_ge(hz_vector, 1 + 3 * HG_HEADS)
            nc.gpsimd.memset(eg[:, :, :], 0.0).then_inc(zeros_ready, 1)
            nc.gpsimd.memset(acc_rs[:, :, :], 0.0).then_inc(zeros_ready, 1)
            for i in range(2, HG_HEADS * len(LEVELS)):
                pool.wait_ge(hl_scaled, i - 1)
                hg_difference(nc.gpsimd, i)

        def pool_layer(pool):
            for s in range(MLP0):
                split_slot(pool, s)
                if s == SLOT_OF["gate", 2, SPLIT - 1]:
                    pool_hgrn(pool)
            with pool.Fori(0, MLP_GROUPS) as g:
                for j in range(MLP_N):
                    split_slot(pool, MLP0 + j, plus_s=g * MLP_N, plus_t=g * (MLP_N // 2), mlp=True)

        def gemm(pe, name, hi, lo, cols=(0, NT), plus_s=0, plus_t=0, wait_h=None, kts=None, wait_r=None):
            s = SLOT_OF[name]
            _, _, kt, _, ccols, results = SLOTS[s]
            c = P * results.index(name)
            G = bank_free(pe, name, plus=plus_t)
            if c == 0:
                pe.wait_ge(weights_split, s + 1 + plus_s)
            whi = w_hi[:, s % SPLIT, :].rearrange("p (k c) -> p k c", k=kt)[:, :, c:c + P]
            wlo = w_lo[:, s % SPLIT, :].rearrange("p (k c) -> p k c", k=kt)[:, :, c:c + P]
            n = cols[1] - cols[0]
            parts = [(0, HALF), (HALF, NT)] if n == NT else [cols]
            for a, (c0, c1) in enumerate(parts):
                for k in range(kt):
                    if a == 0 and wait_h is not None:
                        pe.wait_ge(h_lo_ready, wait_h + k + 1)
                    if a == 0 and wait_r is not None:
                        pe.wait_ge(r_lo_ready, wait_r + (k + 1))
                    dst = G[:, a, 0:c1 - c0]
                    pe.matmul(dst, whi[:, k, :], hi[:, k, c0:c1], start=k == 0, stop=False)
                    pe.matmul(dst, whi[:, k, :], lo[:, k, c0:c1], start=False, stop=False)
                    last = pe.matmul(dst, wlo[:, k, :], hi[:, k, c0:c1], start=False, stop=k == kt - 1)
            last.then_inc(fill_sem(name), 1)

        def stat(pe, k):
            pe.wait_ge(square_sum_ready, k + 1)
            for a in range(2):
                dst = bank_free(pe, ("stat", k, a))
                pe.matmul(dst[:, 0:HALF], ones, acc[:, a * HALF:(a + 1) * HALF], start=True, stop=True) \
                    .then_inc(fill_sem(("stat", k, a)), 1)

        def transposes(pe, name, pieces, t=plan):
            bank = one_bank(bank_free(pe, name, t=t))
            for tile, at in pieces:
                rows, cols = tile.shape[0], tile.shape[1]
                last = pe.transpose(bank[0:cols, at:at + rows], tile, ident[0:rows, 0:rows])
            last.then_inc(fill_sem(name, t), 1)

        def tokens(pe, kind, tiles):
            for tb in range(TB + 1):
                c0, c1 = (P * tb, P * tb + P) if tb < TB else (SEQ, NT)
                bank = bank_free(pe, (kind, "tok", tb))
                at = 0
                for tile in tiles:
                    rows = tile.shape[0]
                    last = pe.transpose(bank[0:c1 - c0, at:at + rows], tile[:, c0:c1], ident[0:rows, 0:rows])
                    at += rows
                last.then_inc(fill_sem((kind, "tok", tb)), 1)

        def attention(pe, kind, scores, values, dv):
            units = prompt_units(HEADS[kind], kind != "x")
            for i in range(len(units) + 2):
                if i < len(units):
                    qb, h = units[i]
                    dst = bank_free(pe, (kind, "S", i))[:, 0:keys(kind, qb)]
                    scores(pe, qb, h, dst).then_inc(fill_sem((kind, "S", i)), 1)
                if 1 <= i <= len(units):
                    u = i - 1
                    emptied(pe, (kind, "S", u))
                    n = keys(kind, units[u][0])
                    transposes(pe, (kind, "PT", u), [(eg[:, u % 2, b:b + P], b) for b in range(0, n, P)])
                if i >= 2:
                    u = i - 2
                    qb, h = units[u]
                    emptied(pe, (kind, "PT", u))
                    name = (kind, "O", qb)
                    dst = bank_free(pe, name) if h == 0 else bank_of(name)
                    nb = keys(kind, qb) // P
                    for b in range(nb):
                        last = pe.matmul(dst[:, h * dv:(h + 1) * dv], PT[:, u % 2, b * P:(b + 1) * P],
                                         values(b, h), start=b == 0, stop=b == nb - 1)
                    last.then_inc(fill_sem(name), 1)

        def sample_transposes(pe, kind, n_keys):
            Ps, _ = SBUF_P[kind]
            pe.wait_ge(sample_probs, SPROB[kind])
            for j, b0 in enumerate(range(0, n_keys, 512)):
                blocks = [(Ps[:, b:min(b + P, n_keys)], b - b0) for b in range(b0, min(b0 + 512, n_keys), P)]
                bank = bank_free(pe, (kind, "PT", j))
                for tile, at in blocks:
                    cols = tile.shape[1]
                    last = pe.transpose(bank[0:cols, at:at + P], tile, ident)
                last.then_inc(fill_sem((kind, "PT", j)), 1)
            emptied(pe, (kind, "PT", (n_keys - 1) // 512))

        def to_features(pe, kind):
            emptied(pe, (kind, "O", TB - 1))
            for f in range(4):
                transposes(pe, (kind, "feat", f),
                           [(O_TOK[kind][:, tb, P * f:P * f + P], P * tb) for tb in range(TB)])

        def branch(pe, b):
            for n in range(0, KT, 2):
                gemm(pe, ("gate", b, n), h_hi, h_lo)
                gemm(pe, ("gate", b, n + 1), h_hi, h_lo)
                if n == 0 and b < 2:
                    emptied(pe, (("fox", "mla")[b], "feat", 3))
                elif n == 0:
                    pe.wait_ge(r_lo_ready, 4)
                gemm(pe, ("br", b, n), r_hi, r_lo)
                gemm(pe, ("br", b, n + 1), r_hi, r_lo)

        def chunks(name_banks):
            return list(zip(name_banks, (0, 512, 1024), (512, 1024, CACHED)))

        def pe_fox(pe):
            fq, fk = S["fq"], S["fk"]
            for n in range(4):
                gemm(pe, ("fq", n), h_hi, h_lo, wait_h=0 if n == 0 else None)
            for n in range(4):
                gemm(pe, ("fk", n), h_hi, h_lo)
            for n in range(4):
                gemm(pe, ("fv", n), h_hi, h_lo)
            gemm(pe, ("ff", 0), h_hi, h_lo)
            emptied(pe, ("fk", 3))
            tokens(pe, "fk", [fk[:, n, :] for n in range(4)])
            emptied(pe, ("fv", 3))
            tokens(pe, "fv", [R["fvT"][:, n, :] for n in range(4)])
            pe.wait_ge(ff_vector, 2)
            for tb in range(TB + 1):
                c0, c1 = (P * tb, P * tb + P) if tb < TB else (SEQ, NT)
                name = ("flogf", tb)
                pe.matmul(bank_free(pe, name)[0:c1 - c0, 0:FOX_HEADS], S["flogT"][:, c0:c1],
                          ident[0:FOX_HEADS, 0:FOX_HEADS], start=True, stop=True).then_inc(fill_sem(name), 1)
            pe.wait_ge(DMA["clogf"], 16)
            for j in range(2):
                name = ("clogf", j)
                bank = bank_free(pe, name)
                for b in range(4):
                    last = pe.matmul(bank[0:FOX_HEADS, P * b:P * b + P], S["clogf"][:, 4 * j + b, :], ident,
                                     start=True, stop=True)
                last.then_inc(fill_sem(name), 1)
            pe.wait_ge(ncum_ready, 1)
            emptied(pe, ("fv", "tok", TB))

            def scores(pe, qb, h, dst):
                n = dst.shape[1]
                pe.matmul(dst, head_rows[:, h:h + 1].to_broadcast([P, P]), M["ncum_parts"][:, 0:n],
                          start=True, stop=True)
                return pe.matmul(dst, fq[:, h, P * qb:P * qb + P], fk[:, h // 2, 0:n],
                                 start=False, stop=True, skip_group_check=True)

            attention(pe, "fox", scores, lambda b, h: S["fv_tok"][:, b, 64 * h:64 * h + 64], FOX_DIM)
            for g in range(2):
                kind = ("foxs", g)
                pe.wait_ge(DMA["foxc"], 32 * (g + 1))
                for j in range(4):
                    f, half = j // 2, j % 2
                    transposes(pe, (kind[0], g, "KT", j),
                               [(R["fKc"][:, 4 * half + b, P * f:P * f + P], P * b) for b in range(4)])
                emptied(pe, ("foxs", g, "KT", 3))
                emptied(pe, ("foxs", g, "KT", 2))
                for bank, c0, c1 in chunks(("A0", "A1", "T")):
                    dst = bank_free(pe, (kind, "S", bank))
                    pe.matmul(dst[:, 0:c1 - c0], SEL[:, P * g:P * g + P], M["ncums"][:, c0:c1],
                              start=True, stop=True)
                    for f in range(2):
                        k = R["fKT"][:, f, c0:c1] if c0 < PAST_LEN else fk[:, 2 * g + f, SEQ:NT]
                        q = S["fq_new"][:, :, :].rearrange("p h n -> p (h n)")
                        q = q[:, 64 * (2 * g + f):64 * (2 * g + f) + 64]
                        last = pe.matmul(dst[64 * f:64 * f + 64, 0:c1 - c0], q, k,
                                         start=False, stop=True, skip_group_check=True)
                    last.then_inc(fill_sem((kind, "S", bank)), 1)
                sample_transposes(pe, kind, CACHED)
                dst = bank_free(pe, (kind, "PV"))
                PTs = R["fPTs"]
                for j in range(4):
                    r, f = 64 * (j % 2), j // 2
                    out = dst[r:r + 64, 32 * f:32 * f + 32]
                    for b in range(CB):
                        pe.matmul(out, R["fVc"][:, b, 64 * j:64 * j + 64], PTs[:, b, 32 * j:32 * j + 32],
                                  start=b == 0, stop=False)
                    c = 256 * g + 64 * j
                    last = pe.matmul(out, S["fv_s"][:, c:c + 64], PTs[0:DEC_SEQ, CB, 32 * j:32 * j + 32],
                                     start=False, stop=True)
                last.then_inc(fill_sem((kind, "PV")), 1)
            to_features(pe, "fox")
            branch(pe, 0)

        def rot(pe, j, tile):
            for a in range(2):
                name = ("rot", j, a)
                pe.matmul(bank_free(pe, name)[:, 0:HALF], cst[:, K_ROT:K_ROT + P], tile[:, a * HALF:(a + 1) * HALF],
                          start=True, stop=True).then_inc(fill_sem(name), 1)

        def pe_mla(pe):
            ckv, kpe, wukv, qn, qpe = S["ckv"], R["kpe"], S["wukv"], S["qn"], S["qpe"]
            cq, kn, vm = S["cq"], S["kn"], S["vm"]
            for n in range(QT):
                gemm(pe, ("cq", n), h_hi, h_lo)
            for n in range(MT):
                gemm(pe, ("ckv", n), h_hi, h_lo)
            gemm(pe, ("kpe", 0), h_hi, h_lo)
            stat(pe, 1)
            stat(pe, 2)
            emptied(pe, ("kpe", 0))
            rot(pe, 0, kpe)
            pe.wait_ge(cqn_ready, 1)
            pe.wait_ge(DMA["wuq"], 32 * QT)
            for n in range(6):
                name = ("qn", n) if n < 4 else ("qpe", n - 4)
                G = bank_free(pe, name)
                for a in range(2):
                    for k in range(QT):
                        w = S["wuqn"][:, k, n, :] if n < 4 else \
                            S["wuqp"][:, k, 2 * (n - 4):2 * (n - 4) + 2, :].rearrange("p a b -> p (a b)")
                        last = pe.matmul(G[:, a, 0:HALF], w, cq[:, k, a * HALF:(a + 1) * HALF],
                                         start=k == 0, stop=k == QT - 1)
                last.then_inc(fill_sem(name), 1)
            emptied(pe, ("qpe", 0))
            rot(pe, 1, qpe[:, 0, :])
            emptied(pe, ("qpe", 1))
            rot(pe, 2, qpe[:, 1, :])
            pe.wait_ge(rope_ready, 3)
            tokens(pe, "ckv", [ckv[:, 0, :], ckv[:, 1, :], kpe[0:MLA_ROPE, :]])
            pe.wait_ge(DMA["wukv"], 16)
            for h in range(4):
                G = bank_free(pe, ("kn", h))
                for c in range(MT):
                    last = pe.matmul(G[:, 0, :], wukv[:, c, 256 * h:256 * h + P], ckv[:, c, 0:SEQ],
                                     start=c == 0, stop=c == MT - 1)
                last.then_inc(fill_sem(("kn", h)), 1)
            for tb in range(TB):
                G = bank_free(pe, ("vm", tb))
                for c in range(MT):
                    wv = wukv[:, c, :].rearrange("p (h t d) -> p h t d", h=4, t=2)[:, :, 1, :]
                    last = pe.matmul(G[:, 0, :].rearrange("p (h d) -> p h d", h=4), ckv[:, c, P * tb:P * tb + P], wv,
                                     start=c == 0, stop=c == MT - 1)
                last.then_inc(fill_sem(("vm", tb)), 1)
            emptied(pe, ("kn", 3)), emptied(pe, ("vm", 3)), emptied(pe, ("vm", 2))

            def scores(pe, qb, h, dst):
                r, n = 64 * (h % 2), dst.shape[1]
                pe.matmul(dst, qn[:, h, P * qb:P * qb + P], kn[:, h, 0:n], start=True, stop=False)
                return pe.matmul(dst, qpe[r:r + 64, h // 2, P * qb:P * qb + P], kpe[r:r + 64, 0:n],
                                 start=False, stop=True)

            attention(pe, "mla", scores, lambda b, h: vm[:, b, P * h:P * h + P], MLA_V)
            pe.wait_ge(DMA["mlac"], 48)
            for j in range(4):
                c, half = j // 2, j % 2
                transposes(pe, ("mlas", "ckvT", j),
                           [(R["ckvc"][:, 4 * half + b, P * c:P * c + P], P * b) for b in range(4)])
            for j in range(2):
                transposes(pe, ("mlas", "kpeT", j), [(R["kpec"][:, 4 * j + b, :], P * b) for b in range(4)])
            for c in range(2):
                transposes(pe, ("mlas", "wukT", c), [(wukv[:, c, 256 * h:256 * h + P], P * h) for h in range(4)])
            emptied(pe, ("mlas", "wukT", 0)), emptied(pe, ("mlas", "wukT", 1))
            name = ("mlas", "qabs")
            dst = bank_free(pe, name)
            for c in range(MT):
                for h in range(4):
                    last = pe.matmul(dst[:, P * c + 32 * h:P * c + 32 * h + 32], R["wukT"][:, h, P * c:P * c + P],
                                     qn[:, h, SEQ:NT], start=True, stop=True)
            last.then_inc(fill_sem(name), 1)
            emptied(pe, name)
            for bank, c0, c1 in chunks(("A0", "A1", "T")):
                dst = bank_free(pe, ("mlas", "S", bank))
                old = c0 < PAST_LEN
                for c in range(MT):
                    k = R["ckvT"][:, c, c0:c1] if old else ckv[:, c, SEQ:NT]
                    pe.matmul(dst[:, 0:c1 - c0], R["qabs"][:, c, :], k, start=c == 0, stop=c == MT - 1)
                for j in range(4):
                    r = 64 * (j % 2)
                    k = R["kpeT"][r:r + 64, c0:c1] if old else kpe[r:r + 64, SEQ:NT]
                    last = pe.matmul(dst[32 * j:32 * j + 32, 0:c1 - c0], qpe[r:r + 64, j // 2, SEQ:NT], k,
                                     start=False, stop=True, skip_group_check=True)
                last.then_inc(fill_sem(("mlas", "S", bank)), 1)
            sample_transposes(pe, "mlas", CACHED)
            dst = bank_free(pe, ("mlas", "PV"))
            for c in range(MT):
                for b in range(CB):
                    pe.matmul(dst[:, P * c:P * c + P], R["ckvc"][:, b, P * c:P * c + P], S["msPT"][:, b, :],
                              start=b == 0, stop=False)
                last = pe.matmul(dst[:, P * c:P * c + P], S["ckv_s"][:, P * c:P * c + P],
                                 S["msPT"][0:DEC_SEQ, CB, :], start=False, stop=True)
            last.then_inc(fill_sem(("mlas", "PV")), 1)
            emptied(pe, ("mlas", "PV"))
            dst = bank_free(pe, ("mlas", "o"))
            for h in range(4):
                for c in range(MT):
                    last = pe.matmul(dst[:, 32 * h:32 * h + 32], wukv[:, c, 256 * h + P:256 * h + 2 * P],
                                     R["lat"][:, c, 32 * h:32 * h + 32], start=c == 0, stop=c == MT - 1)
            last.then_inc(fill_sem(("mlas", "o")), 1)
            to_features(pe, "mla")
            branch(pe, 1)

        def pe_hgrn(pe):
            hq, lc, hk = S["hq"], S["hf"], S["hk"]
            for kind in ("hf", "hg", "hq", "hi"):
                for n in range(4):
                    gemm(pe, (kind, n), h_hi, h_lo)
            emptied(pe, ("hi", 3)), emptied(pe, ("hi", 2))
            tokens(pe, "hi", [R["hviT"][:, n, :] for n in range(4)])
            emptied(pe, ("hi", "tok", TB)), emptied(pe, ("hi", "tok", TB - 1))
            def products(h, lv):
                name = ("hgA", h, lv)
                G = bank_free(pe, name)
                diagonal = lv == NL - 1
                if not diagonal:
                    i = h * len(LEVELS) + lv
                    pe.wait_ge(hl_scaled, i + 1)
                    q, k = eg[:, i % 2, :], acc_rs[:, i % 2, :]
                else:
                    q, k = hq[:, h, :], hk[:, h, :]
                for tb in range(TB):
                    last = pe.matmul(G[:, 0, P * tb:P * tb + P], k[:, P * tb:P * tb + P], q[:, P * tb:P * tb + P],
                                     start=True, stop=True)
                if diagonal or LEVELS[lv] < DEC_SEQ:
                    last = pe.matmul(G[0:DEC_SEQ, 1, 0:DEC_SEQ], k[:, SEQ:NT], q[:, SEQ:NT], start=True, stop=True)
                last.then_inc(fill_sem(name), 1)

            def state_updates(h):
                emptied(pe, ("hg", "kdTs", h)), emptied(pe, ("hg", "kdT", h))
                dst = bank_free(pe, ("hg", "U", h))
                for tb in range(TB):
                    last = pe.matmul(dst[:, P * tb:P * tb + P], R["hkdT"][:, tb, :], S["hv"][:, tb, P * h:P * h + P],
                                     start=True, stop=True)
                last.then_inc(fill_sem(("hg", "U", h)), 1)
                dst = bank_free(pe, ("hg", "Us", h))
                pe.matmul(dst[:, 0:P], R["hkdTs"][:, :], S["hv_s"][:, P * h:P * h + P], start=True, stop=True) \
                    .then_inc(fill_sem(("hg", "Us", h)), 1)

            def outputs(h):
                emptied(pe, ("hgA", h, NL - 1))
                emptied(pe, ("hg", "U", h))
                dst = bank_free(pe, ("hg", "O", h))
                for tb in range(TB):
                    out = dst[:, P * tb:P * tb + P]
                    last = pe.matmul(out, R["hAT"][:, h % 2, tb, :], S["hv"][:, tb, P * h:P * h + P],
                                     start=True, stop=tb == 0)
                    if tb:
                        last = pe.matmul(out, R["hqd"][:, P * tb:P * tb + P], R["hST"][:, tb - 1, :],
                                         start=False, stop=True)
                last.then_inc(fill_sem(("hg", "O", h)), 1)
                if h == 0:
                    pe.wait_ge(DMA["state"], 16)
                dst = bank_free(pe, ("hg", "Os", h))
                pe.matmul(dst[0:DEC_SEQ, 0:P], R["hATs"][:, h % 2, :], S["hv_s"][:, P * h:P * h + P],
                          start=True, stop=False)
                pe.matmul(dst[0:DEC_SEQ, 0:P], R["hqd"][:, SEQ:NT], R["hS0"][:, h, :], start=False, stop=True) \
                    .then_inc(fill_sem(("hg", "Os", h)), 1)

            for h in range(HG_HEADS + 1):
                for lv in range(NL):
                    if h < HG_HEADS:
                        products(h, lv)
                    if h and lv == HG_STEP_U:
                        state_updates(h - 1)
                    if h and lv == HG_STEP_O:
                        outputs(h - 1)
                if h < HG_HEADS:
                    pe.wait_ge(hd_scaled, h + 1)
                    kd = R["hkd"]
                    transposes(pe, ("hg", "kdT", h), [(kd[:, P * tb:P * tb + P], P * tb) for tb in range(TB)])
                    transposes(pe, ("hg", "kdTs", h), [(kd[:, SEQ:NT], 0)])
            for f in range(4):
                emptied(pe, ("hg", "O", f)), emptied(pe, ("hg", "Os", f))
                transposes(pe, ("hg", "feat", f),
                           [(R["ho_tok"][:, tb, P * f:P * f + P], P * tb) for tb in range(TB)])
                transposes(pe, ("hg", "feats", f), [(S["ho_s"][:, P * f:P * f + P], 0)])
            branch(pe, 2)

        def pe_layer(pe):
            pe.wait_ge(DMA["vecs"], VECS)
            transposes(pe, ("vec",), [(vecs[0:V_ROWS, :], 0)])
            stat(pe, 0)
            pe_fox(pe)
            pe_mla(pe)
            pe_hgrn(pe)
            for n in range(KT):
                gemm(pe, ("out", n), h_hi, h_lo, wait_h=KT if n == 0 else None)
            stat(pe, 3)
            pe.wait_ge(DMA["mem"], 16)
            for j in range(4):
                transposes(pe, ("memT", j), [(S["mem_tok"][:, b, P * (2 * j + f):P * (2 * j + f) + P], 256 * f + P * b)
                                             for f in range(2) for b in range(MB)])
            emptied(pe, ("memT", 3)), emptied(pe, ("memT", 2))
            for kind in ("memk", "memv"):
                for n in range(4):
                    gemm(pe, (kind, n), R["m_hi"], R["m_lo"], cols=(0, N_MEM))
            for kind, tile in (("memk", S["mkT"]), ("memv", S["mvT"])):
                emptied(pe, (kind, 3)), emptied(pe, (kind, 2))
                for b in range(MB):
                    transposes(pe, (kind, "tok", b), [(tile[:, n, P * b:P * b + P], P * n) for n in range(4)])
            stat(pe, 4)
            for n in range(4):
                gemm(pe, ("xq", n), h_hi, h_lo, wait_h=2 * KT if n == 0 else None)
            xq = S["xq"]
            emptied(pe, ("memv", "tok", 1)), emptied(pe, ("memv", "tok", 0))
            emptied(pe, ("xq", 3)), emptied(pe, ("xq", 2))

            def scores(pe, qb, h, dst):
                return pe.matmul(dst, xq[:, h, P * qb:P * qb + P], S["mkT"][:, h, :], start=True, stop=True)

            attention(pe, "x", scores, lambda b, h: S["mv_tok"][:, b, P * h:P * h + P], X_DIM)
            pe.wait_ge(DMA["xsc"], 32)
            for j in range(2):
                transposes(pe, ("xs", "KT", j), [(S["xsK"][:, b, P * (2 * j + f):P * (2 * j + f) + P], 256 * f + P * b)
                                                 for f in range(2) for b in range(MB)])
            emptied(pe, ("xs", "KT", 0)), emptied(pe, ("xs", "KT", 1))
            dst = bank_free(pe, ("xs", "S", "A0"))
            for j in range(4):
                last = pe.matmul(dst[32 * j:32 * j + 32, 0:N_MEM], xq[:, j, SEQ:NT], S["xsKT"][:, j, :],
                                 start=True, stop=True)
            last.then_inc(fill_sem(("xs", "S", "A0")), 1)
            sample_transposes(pe, "xs", N_MEM)
            dst = bank_free(pe, ("xs", "PV"))
            for j in range(4):
                for b in range(MB):
                    last = pe.matmul(dst[:, 32 * j:32 * j + 32], S["xsV"][:, b, P * j:P * j + P],
                                     S["xsPT"][:, b, 32 * j:32 * j + 32], start=b == 0, stop=b == MB - 1)
            last.then_inc(fill_sem(("xs", "PV")), 1)
            to_features(pe, "x")
            emptied(pe, ("x", "feat", 3))
            for n in range(KT):
                gemm(pe, ("xo", n), r_hi, r_lo)
            stat(pe, 5)
            stat(pe, 6)
            for k in range(KT):
                pe.wait_ge(h_lo_ready, 3 * KT + k + 1)
            with pe.Fori(0, MLP_GROUPS) as g:
                for n in range(KT):
                    gemm(pe, ("up", n), h_hi, h_lo, plus_s=g * MLP_N, plus_t=g * (MLP_N // 2))
                for n in range(KT):
                    gemm(pe, ("down", n), r_hi, r_lo, plus_s=g * MLP_N, plus_t=g * (MLP_N // 2),
                         wait_r=4 + g * KT if n == 0 else None)
            stat(pe, 7)

        def act_code():
            n = [0]

            def chain(ins):
                ins.then_inc(scalar_chain, 1)
                n[0] += 1

            def wait_chain(act):
                act.wait_ge(scalar_chain, n[0])

            copy = nc.scalar.copy

            def exp(out, in_, **kw):
                return nc.scalar.activation(out, in_, ACT.Exp, **kw)

            def rs_of(act, k, features):
                for a in range(2):
                    name = ("stat", k, a)
                    filled(act, name)
                    nc.scalar.activation(acc[:, a * HALF:(a + 1) * HALF], bank_of(name)[:, 0:HALF], ACT.Ln,
                                         bias=eps[:, 0:1], scale=1.0 / features).then_inc(empty_sem(name), 1)
                emptied(act, ("stat", k, 1)), emptied(act, ("stat", k, 0))
                exp(rs, acc, scale=-0.5).then_inc(rs_ready, 1)

            def h_high(act, base):
                for t in range(KT):
                    act.wait_ge(h32_ready, base + t + 1)
                    copy(h_hi[:, t, :], sq[:, t, :]).then_inc(h_hi_ready, 1)

            def evacuate(act, name, out):
                filled(act, name)
                copy(out, g_tile(name, out.shape[0])).then_inc(empty_sem(name), 1)

            def square_and_keep(act, name, sq_tile, keep):
                filled(act, name)
                nc.scalar.activation(both(sq_tile), g_tile(name), ACT.Square).then_inc(square_ready, 1)
                copy(both(keep), g_tile(name)).then_inc(empty_sem(name), 1)

            def attention(act, kind):
                units = prompt_units(HEADS[kind], kind != "x")
                for i in range(len(units) + 1):
                    if i < len(units):
                        nk = keys(kind, units[i][0])
                        act.wait_ge(row_max, RMAX[kind] + i + 1)
                        if i >= 2:
                            filled(act, (kind, "PT", i - 2))
                        exp(eg[:, i % 2, 0:nk], bank_of((kind, "S", i))[:, 0:nk], bias=negmax[:, i:i + 1],
                            scale=SCALE[kind], accum_out=rsum[:, i:i + 1]).then_inc(empty_sem((kind, "S", i)), 1)
                    if i >= 1:
                        u = i - 1
                        nk = keys(kind, units[u][0])
                        filled(act, (kind, "PT", u))
                        if u >= 2:
                            qb, h = units[u - 2]
                            filled(act, (kind, "O", qb), part=h + 1)
                        copy(PT[:, u % 2, 0:nk], one_bank(bank_of((kind, "PT", u)))[:, 0:nk]) \
                            .then_inc(empty_sem((kind, "PT", u)), 1)

            def sample(act, kind, n_keys, o_out):
                Ps, PTs = SBUF_P[kind]
                act.wait_ge(row_max, RMAX[kind] + 1)
                for j, c0 in enumerate(range(0, n_keys, 512)):
                    c1 = min(c0 + 512, n_keys)
                    name = (kind, "S", ("A0", "A1", "T")[j])
                    exp(Ps[:, c0:c1], SCORES[:, c0:c1], bias=negmax[:, 63:64], scale=SCALE[kind],
                        accum_out=rsum[:, 60 + j:61 + j]).then_inc(empty_sem(name), 1)
                for j, c0 in enumerate(range(0, n_keys, 512)):
                    name = (kind, "PT", j)
                    filled(act, name)
                    nb = (min(c0 + 512, n_keys) - c0) // P
                    if nb:
                        copy(PTs[:, 4 * j:4 * j + nb, :], bank_of(name)[:, 0:nb * P].rearrange("p (b c) -> p b c", b=nb)) \
                            .then_inc(empty_sem(name), 1)
                    else:
                        copy(PTs[0:DEC_SEQ, 4 * j, :], bank_of(name)[0:DEC_SEQ, 0:P]).then_inc(empty_sem(name), 1)
                name = (kind, "PV")
                filled(act, name)
                n_cols = o_out.shape[1] * o_out.shape[2]
                copy(o_out, bank_of(name)[:, 0:n_cols].rearrange("p (a b) -> p a b", a=o_out.shape[1])) \
                    .then_inc(empty_sem(name), 1)

            def o_high(act, kind):
                copy(r_hi[:, 0:4, SEQ:NT], O_S[kind][:, :, :]).then_inc(o_hi_ready, 1)
                for f in range(4):
                    name = (kind, "feat", f)
                    filled(act, name)
                    copy(r_hi[:, f, 0:SEQ], bank_of(name)).then_inc(o_hi_ready, 1)

            def gates(act, b):
                for m in range(KT):
                    filled(act, ("gate", b, m))
                    if m >= 2:
                        emptied(act, ("br", b, m - 2))
                    exp(both(eg[:, m % 2, :]), g_tile(("gate", b, m)), scale=-1.0) \
                        .then_inc(empty_sem(("gate", b, m)), 1)

            def load(act, dst, src, key):
                act.dma_start(dst, src).then_inc(DMA[key], 16)

            def layer_of(name, l):
                return A[name][bass.ds(l, 1)]

            def store(act, name, l, prompt, sample, key="out"):
                if prompt is not None:
                    dst = O["p_" + name][bass.ds(l, 1), 0]
                    dst = dst.rearrange("a s h d -> (a s) (h d)") if len(dst.shape) == 4 else \
                        dst.rearrange("a s c -> (a s) c")
                    act.dma_start(dst.rearrange("(b p) c -> p b c", p=P), prompt).then_inc(DMA[key], 16)
                if sample is not None:
                    dst = O["s_" + name][bass.ds(l, 1), 0]
                    dst = dst.rearrange("a s h d -> (a s) (h d)") if len(dst.shape) == 4 else \
                        dst.rearrange("a s c -> (a s) c")
                    act.dma_start(dst, sample).then_inc(DMA[key], 16)

            def act_vectors(act, l):
                v = layer_of("g_norm", l).rearrange("a g (t p) -> (a g t) p", p=P)
                load(act, vecs[V_NORM:V_CQ, :], v, "vecs")
                load(act, vecs[V_CQ:V_CKV, :], layer_of("g_mla_q", l).rearrange("a (t p) -> (a t) p", p=P), "vecs")
                load(act, vecs[V_CKV:V_HG, :], layer_of("g_mla_kv", l).rearrange("a (t p) -> (a t) p", p=P), "vecs")
                load(act, vecs[V_HG:V_LB, :], layer_of("g_hgrn_out", l), "vecs")
                load(act, vecs[V_LB:V_ROWS, :], A["lb_hgrn"].rearrange("l (t p) -> (l t) p", p=P), "vecs")
                load(act, bfox[:, :], layer_of("b_fox", l).rearrange("a h -> h a"), "vecs")
                load(act, lbsel[:, :], A["lb_select"][bass.ds(l, 1)].rearrange("a p d -> (a p) d"), "vecs")
                clog = layer_of("cache_fox_logf", l)[:, 0].rearrange("a s h -> (a s) h")
                load(act, S["clogf"][:, :, :], clog.rearrange("(b p) h -> p b h", p=P), "clogf")

            def act_lb(act):
                act.wait_ge(hz_vector, 1)
                exp(small[:, 8:16], small[:, 0:8]).then_inc(hz_scalar, 1)

            def cached(name, l, c0, c1):
                src = layer_of(name, l)[:, 0]
                src = src.rearrange("a s h d -> (a s) (h d)") if len(src.shape) == 4 else \
                    src.rearrange("a s c -> (a s) c")
                return src[:, c0:c1].rearrange("(b p) c -> p b c", p=P)

            def act_fox(act, l):
                for m in range(4):
                    filled(act, ("fq", m))
                    for j in range(2):
                        r = slice(64 * j, 64 * j + 64)
                        ins = nc.scalar.activation(both(S["fq"][r, 2 * m + j, :]), g_tile(("fq", m))[r], ACT.Copy,
                                                   scale=FOX_DIM ** -0.5)
                        ins.then_inc(empty_sem(("fq", m)), 1) if j else chain(ins)
                for m in range(4):
                    evacuate(act, ("fk", m), both(S["fk"][:, m, :]))
                for m in range(4):
                    evacuate(act, ("fv", m), both(R["fvT"][:, m, :]))
                name = ("ff", 0)
                filled(act, name)
                act.wait_ge(DMA["vecs"], VECS)
                nc.scalar.activation(both(S["flogT"][:, :]), g_tile(name, FOX_HEADS), ACT.Identity,
                                     bias=bfox[:, 0:1]).then_inc(empty_sem(name), 1)
                act.wait_ge(ff_vector, 1)
                chain(exp(eg[0:FOX_HEADS, 0, :], eg[0:FOX_HEADS, 0, :], scale=-1.0))
                wait_chain(act)
                nc.scalar.activation(eg[0:FOX_HEADS, 1, :], eg[0:FOX_HEADS, 0, :], ACT.Ln, bias=1.0) \
                    .then_inc(ff_scalar, 1)
                emptied(act, ("fk", "tok", TB)), emptied(act, ("fk", "tok", TB - 1))
                store(act, "fox_k", l, S["fk_tok"][:, :, :], M["fk_s"][:, :], "k_out")
                emptied(act, ("fv", "tok", TB)), emptied(act, ("fv", "tok", TB - 1))
                store(act, "fox_v", l, S["fv_tok"][:, :, :], S["fv_s"][:, :], "k_out")
                load(act, R["fKc"][:, :, :], cached("cache_fox_k", l, 0, 256), "foxc")
                load(act, R["fVc"][:, :, :], cached("cache_fox_v", l, 0, 256), "foxc")
                emptied(act, ("flogf", TB)), emptied(act, ("flogf", TB - 1))
                store(act, "fox_logf", l, S["flogf"][:, 0:TB, :], S["flogf"][0:DEC_SEQ, TB, :], "k_out")
                attention(act, "fox")
                for g in range(2):
                    for j in range(4):
                        name = ("foxs", g, "KT", j)
                        filled(act, name)
                        copy(R["fKT"][:, j // 2, 512 * (j % 2):512 * (j % 2) + 512], bank_of(name)) \
                            .then_inc(empty_sem(name), 1)
                    sample(act, ("foxs", g), CACHED, S["foS"][:, 2 * g:2 * g + 2, :])
                    if g == 0:
                        load(act, R["fKc"][:, :, :], cached("cache_fox_k", l, 256, 512), "foxc")
                        load(act, R["fVc"][:, :, :], cached("cache_fox_v", l, 256, 512), "foxc")
                emptied(act, (("foxs", 1), "PV"))
                o_high(act, "fox")
                emptied(act, ("fox", "feat", 3))
                act.wait_ge(DMA["k_out"], 96)
                for k in range(QT):
                    uq = layer_of("w_mla_uq", l).rearrange("a r (h c) -> (a r) h c", h=4)[P * k:P * k + P]
                    load(act, S["wuqn"][:, k, :, :], uq[:, :, 0:MLA_NOPE], "wuq")
                    load(act, S["wuqp"][:, k, :, :], uq[:, :, MLA_NOPE:], "wuq")
                load(act, S["wukv"][:, :, :], layer_of("w_mla_ukv", l).rearrange("a r c -> (a r) c")
                     .rearrange("(k p) c -> p k c", p=P), "wukv")
                gates(act, 0)

            def act_mla(act, l):
                for m in range(QT):
                    square_and_keep(act, ("cq", m), S["msq"][:, m, :], S["cq"][:, m, :])
                act.wait_ge(square_sum_ready, 2)
                for m in range(MT):
                    square_and_keep(act, ("ckv", m), S["msq"][:, m, :], S["ckv"][:, m, :])
                emptied(act, ("br", 0, KT - 1))
                emptied(act, ("br", 0, KT - 2))
                evacuate(act, ("kpe", 0), both(R["kpe"][:, :]))
                load(act, R["ckvc"][:, :, :], cached("cache_mla_ckv", l, 0, 256), "mlac")
                kp = R["kpec"][:, :, :].rearrange("p b (t c) -> p b t c", t=2)
                for t in range(2):
                    load(act, kp[:, :, t, :], cached("cache_mla_kpe", l, 0, 64), "mlac")
                rs_of(act, 1, MLA_Q_RANK)
                rs_of(act, 2, MLA_KV_RANK)
                for m in range(6):
                    name = ("qn", m) if m < 4 else ("qpe", m - 4)
                    evacuate(act, name, both(S["qn"][:, m, :] if m < 4 else S["qpe"][:, m - 4, :]))
                for kind, tile in (("kn", S["kn"]), ("vm", S["vm"])):
                    for m in range(4):
                        filled(act, (kind, m))
                        copy(tile[:, m, :], bank_of((kind, m))[:, 0, :]).then_inc(empty_sem((kind, m)), 1)
                emptied(act, ("ckv", "tok", TB)), emptied(act, ("ckv", "tok", TB - 1))
                o = S["mo_tok"]
                store(act, "mla_ckv", l, o[:, :, 0:256], S["ckv_s"][:, 0:256], "ckv_out")
                store(act, "mla_kpe", l, o[:, :, 256:320], S["ckv_s"][:, 256:320], "ckv_out")
                attention(act, "mla")
                for j in range(4):
                    name = ("mlas", "ckvT", j)
                    filled(act, name)
                    copy(R["ckvT"][:, j // 2, 512 * (j % 2):512 * (j % 2) + 512], bank_of(name)) \
                        .then_inc(empty_sem(name), 1)
                for j in range(2):
                    name = ("mlas", "kpeT", j)
                    filled(act, name)
                    copy(R["kpeT"][:, 512 * j:512 * j + 512], bank_of(name)).then_inc(empty_sem(name), 1)
                for c in range(2):
                    name = ("mlas", "wukT", c)
                    filled(act, name)
                    copy(R["wukT"][:, :, P * c:P * c + P], bank_of(name).rearrange("p (h c) -> p h c", h=4)) \
                        .then_inc(empty_sem(name), 1)
                name = ("mlas", "qabs")
                filled(act, name)
                copy(R["qabs"][:, :, :], bank_of(name)[:, 0:256].rearrange("p (c n) -> p c n", c=2)) \
                    .then_inc(empty_sem(name), 1)
                sample(act, "mlas", CACHED, R["lat"][:, :, :])
                name = ("mlas", "o")
                filled(act, name)
                copy(S["moS"][:, :, :], bank_of(name)[:, 0:P].rearrange("p (h n) -> p h n", h=4)) \
                    .then_inc(empty_sem(name), 1)
                emptied(act, name)
                o_high(act, "mla")
                gates(act, 1)

            def act_hgrn(act, l):
                hf, hk, hE = S["hf"], S["hk"], S["hE"]
                emptied(act, ("mla", "feat", 3))
                act.wait_ge(DMA["ckv_out"], 64)
                for m in range(4):
                    evacuate(act, ("hf", m), both(hf[:, m, :]))

                def other(kind, m):
                    if kind == "hq":
                        evacuate(act, ("hq", m), both(S["hq"][:, m, :]))
                    elif kind == "hi":
                        if m == 0:
                            emptied(act, ("br", 1, KT - 1)), emptied(act, ("br", 1, KT - 2))
                        evacuate(act, ("hi", m), both(R["hviT"][:, m, :]))
                    else:
                        filled(act, ("hg", m))
                        exp(both(S["hg"][:, m, :]), g_tile(("hg", m)), scale=-1.0).then_inc(empty_sem(("hg", m)), 1)

                others = [(kind, m) for kind in ("hg", "hq", "hi") for m in range(4)]
                ta, tb_, tc, td, te = eg[:, 0, :], eg[:, 1, :], acc, rs, hE[:, 0, :]
                for h in range(HG_HEADS):
                    act.wait_ge(hz_vector, 2 + 3 * h)
                    chain(exp(ta, ta, scale=-1.0))
                    wait_chain(act)
                    chain(nc.scalar.activation(tb_, ta, ACT.Ln, bias=1.0))
                    exp(tc, tc).then_inc(hz_scalar, 1)
                    other(*others[3 * h])
                    act.wait_ge(hz_vector, 3 + 3 * h)
                    chain(nc.scalar.activation(tc, tc, ACT.Ln))
                    chain(nc.scalar.activation(td, td, ACT.Ln))
                    exp(hk[:, h, :], te, scale=-1.0).then_inc(hz_scalar, 1)
                    other(*others[3 * h + 1])
                    other(*others[3 * h + 2])
                load(act, R["hS0"][:, :, :], layer_of("state_hgrn", l)[:, 0].rearrange("a h c v -> (a h) c v")
                     .rearrange("h c v -> c h v"), "state")

                def keep_kd(h):
                    name = ("hg", "kdT", h)
                    filled(act, name)
                    copy(R["hkdT"][:, :, :], bank_of(name).rearrange("p (b c) -> p b c", b=TB)) \
                        .then_inc(empty_sem(name), 1)
                    name = ("hg", "kdTs", h)
                    filled(act, name)
                    copy(R["hkdTs"][:, :], bank_of(name)[0:DEC_SEQ, 0:P]).then_inc(empty_sem(name), 1)

                def keep_outputs(h):
                    prompt, new = ("hg", "O", h), ("hg", "Os", h)
                    filled(act, prompt), filled(act, new)
                    blocks = [(bank_of(prompt)[:, P * tb:P * tb + P], P) for tb in range(TB)] + \
                        [(bank_of(new)[0:DEC_SEQ, 0:P], DEC_SEQ)]
                    for tb, (o, rows) in enumerate(blocks):
                        chain(nc.scalar.activation(R["hsq"][0:rows, :], o, ACT.Square,
                                                   accum_out=small[0:rows, tb:tb + 1]))
                        wait_chain(act)
                    for rows, c0, c1 in ((P, 0, TB), (DEC_SEQ, TB, TB + 1)):
                        rms = small[0:rows, c0:c1]
                        chain(nc.scalar.activation(rms, rms, ACT.Ln, bias=eps[0:rows, 0:1], scale=1.0 / HG_DIM))
                    wait_chain(act)
                    for rows, c0, c1 in ((P, 0, TB), (DEC_SEQ, TB, TB + 1)):
                        chain(exp(small[0:rows, c0:c1], small[0:rows, c0:c1], scale=-0.5))
                    wait_chain(act)
                    for tb, (o, rows) in enumerate(blocks):
                        out = R["ho_tok"][:, tb, P * h:P * h + P] if tb < TB else S["ho_s"][:, P * h:P * h + P]
                        ins = nc.scalar.activation(out, o, ACT.Copy, scale=small[0:rows, tb:tb + 1])
                        if tb < TB - 1:
                            chain(ins)
                        else:
                            ins.then_inc(empty_sem(prompt if tb < TB else new), 1)

                for h in range(HG_HEADS):
                    for lv, half in enumerate(LEVELS):
                        i = h * len(LEVELS) + lv
                        n_tok = SEQ if 2 * half > DEC_SEQ else NT
                        e = hE[:, i % 2, 0:n_tok].rearrange("p (b w) -> p b w", w=2 * half)
                        act.wait_ge(hl_diff, i + 1)
                        chain(exp(e[:, :, half:], e[:, :, half:]))
                        exp(e[:, :, 0:half], e[:, :, 0:half], scale=-1.0).then_inc(hl_exp, 1)
                        if h and lv == 1:
                            keep_kd(h - 1)
                        if h and lv == 4:
                            keep_outputs(h - 1)
                        if lv == 5:
                            act.wait_ge(hd_diff, h + 1)
                            chain(exp(R["hqd"][:, :], hf[:, h, :]))
                            chain(exp(R["hkd"][:, :], R["hkd"][:, :], scale=-1.0))
                            lcp = hf[:, h, 0:SEQ].rearrange("p (b w) -> p b w", w=P)
                            chain(exp(small[:, 16:16 + TB], lcp[:, :, P - 1]))
                            exp(small[:, 16 + TB:17 + TB], hf[:, h, NT - 1:NT]).then_inc(hd_exp, 1)
                keep_kd(HG_HEADS - 1)
                keep_outputs(HG_HEADS - 1)
                emptied(act, ("hg", "Us", HG_HEADS - 1))
                src = R["hSf"][:, :, :]
                act.dma_start(O["p_hgrn_state"][bass.ds(l, 1), 0].rearrange("a h c v -> (a h) c v")
                              .rearrange("h c v -> c h v"), src).then_inc(DMA["out"], 16)
                act.dma_start(O["s_hgrn_state"][bass.ds(l, 1), 0].rearrange("a h c v -> (a h) c v")
                              .rearrange("h c v -> c h v"), R["hS0"][:, :, :]).then_inc(DMA["out"], 16)
                for f in range(4):
                    act.wait_ge(r32_ready, f + 1)
                    copy(r_hi[:, f, :], hE[:, f % 2, :]).then_inc(r_hi_ready, 1)
                gates(act, 2)

            def act_cross(act, l):
                act.wait_ge(r_lo_ready, 4)
                load(act, S["mem_tok"][:, :, :], A["mem_prompt"][0].rearrange("(b p) c -> p b c", p=P), "mem")
                load(act, S["xsK"][:, :, :], cached("cache_mem_k", l, 0, 512), "xsc")
                load(act, S["xsV"][:, :, :], cached("cache_mem_v", l, 0, 512), "xsc")
                filled(act, ("gate", 2, KT - 1)), filled(act, ("br", 2, KT - 1))
                for m in range(KT):
                    emptied(act, ("br", 2, m))
                    copy(h_hi[:, m, :], U[:, m, :]).then_inc(h_hi_ready, 1)
                for m in range(KT):
                    square_and_keep(act, ("out", m), sq[:, m, :], U[:, m, :])
                rs_of(act, 3, D_MODEL)
                for j in range(4):
                    name = ("memT", j)
                    filled(act, name)
                    copy(R["m_hi"][:, 2 * j:2 * j + 2, :], bank_of(name).rearrange("p (f n) -> p f n", f=2)) \
                        .then_inc(o_hi_ready, 1)
                for kind, tile in (("memk", S["mkT"]), ("memv", S["mvT"])):
                    for m in range(4):
                        filled(act, (kind, m))
                        copy(tile[:, m, :], bank_of((kind, m))[:, 0, 0:N_MEM]).then_inc(empty_sem((kind, m)), 1)
                for kind, tile in (("mem_k", S["mk_tok"]), ("mem_v", S["mv_tok"])):
                    emptied(act, (kind.replace("_", ""), "tok", 1)), emptied(act, (kind.replace("_", ""), "tok", 0))
                    store(act, kind, l, tile[:, :, :], None, "mem_out")
                x_squares(act, 4, 0)
                rs_of(act, 4, D_MODEL)
                h_high(act, KT)
                for m in range(4):
                    evacuate(act, ("xq", m), both(S["xq"][:, m, :]))
                attention(act, "x")
                for j in range(2):
                    name = ("xs", "KT", j)
                    filled(act, name)
                    copy(S["xsKT"][:, 2 * j:2 * j + 2, :], bank_of(name).rearrange("p (f n) -> p f n", f=2)) \
                        .then_inc(empty_sem(name), 1)
                sample(act, "xs", N_MEM, S["xoS"][:, :, :])
                emptied(act, ("xs", "PV"))
                o_high(act, "x")
                emptied(act, ("x", "feat", 3))
                act.wait_ge(DMA["mem_out"], 32)
                for m in range(KT):
                    square_and_keep(act, ("xo", m), S["sqx"][:, m, :], U[:, m, :])
                rs_of(act, 5, D_MODEL)
                x_squares(act, 6, KT)
                rs_of(act, 6, D_MODEL)
                h_high(act, 2 * KT)

            def x_squares(act, k, base):
                for t in range(KT):
                    act.wait_ge(x_ready, base + t + 1)
                    nc.scalar.activation(sq[:, t, :], x[:, t, :], ACT.Square).then_inc(square_ready, 1)

            def act_mlp(act):
                with act.Fori(0, MLP_GROUPS) as g:
                    plus = g * (MLP_N // 2)
                    for m in range(KT):
                        name = ("up", m)
                        filled(act, name, plus=plus)
                        if m >= 2:
                            act.wait_ge(r32_ready, 4 + g * KT + m - 1)
                        else:
                            act.wait_ge(r32_ready, 4 + g * KT)
                        nc.scalar.activation(both(S["t1"][:, m % 2, :]), g_tile(name), ACT.Relu) \
                            .then_inc(empty_sem(name), 1)
                        if m >= 1:
                            act.wait_ge(r32_ready, 4 + g * KT + m)
                            copy(r_hi[:, m - 1, :], S["t2"][:, (m - 1) % 2, :]).then_inc(r_hi_ready, 1)
                    act.wait_ge(r32_ready, 4 + g * KT + KT)
                    copy(r_hi[:, KT - 1, :], S["t2"][:, (KT - 1) % 2, :]).then_inc(r_hi_ready, 1)
                for t in range(KT):
                    act.wait_ge(u_ready, 1)
                    nc.scalar.activation(sq[:, t, :], U[:, t, :], ACT.Square).then_inc(square_ready, 1)
                rs_of(act, 7, D_MODEL)

            def layer(act, l):
                n[0] = 0
                act_vectors(act, l)
                for t in range(KT):
                    nc.scalar.activation(sq[:, t, :], x[:, t, :], ACT.Square).then_inc(square_ready, 1)
                act_lb(act)
                rs_of(act, 0, D_MODEL)
                h_high(act, 0)
                act_fox(act, l)
                act_mla(act, l)
                act_hgrn(act, l)
                act_cross(act, l)
                act_mlp(act)
                wait_chain(act)

            return layer

        def dve_code():
            n = [0]
            V = nc.vector

            def step(v, ins):
                n[0] += 1
                ins.then_inc(vector_chain, 1)
                v.wait_ge(vector_chain, n[0])

            def square_sum(v, k, tiles):
                base = SQ0[k]
                for t in range(1, NORMS[k]):
                    v.wait_ge(square_ready, base + t + 1)
                    first = tiles[:, 0, :] if t == 1 else acc
                    ins = V.tensor_tensor(acc, first, tiles[:, t, :], ALU.add)
                    if t < NORMS[k] - 1:
                        step(v, ins)
                    else:
                        ins.then_inc(square_sum_ready, 1)

            def low(v, t, base, src):
                v.wait_ge(h_hi_ready, base + t + 1)
                V.tensor_tensor(h_lo[:, t, :], src[:, t, :], h_hi[:, t, :].bitcast(F32), ALU.subtract) \
                    .then_inc(h_lo_ready, 1)

            def post(v, k, gcol, tmp, last=False):
                v.wait_ge(rs_ready, k + 1)
                for t in range(KT):
                    step(v, V.scalar_tensor_tensor(tmp[:, t, :], U[:, t, :], gT[:, gcol + t:gcol + t + 1], rs,
                                                   ALU.mult, ALU.mult))
                    V.tensor_tensor(x[:, t, :], x[:, t, :], tmp[:, t, :], ALU.add).then_inc(x_ready, 1)

            def to_tokens(v, kind, prompt, sample, cols):
                for tb in range(TB + 1):
                    name = (kind, "tok", tb)
                    filled(v, name)
                    dst = prompt[:, tb, 0:cols] if tb < TB else sample[:, 0:cols]
                    V.tensor_copy(dst, bank_of(name)[0:dst.shape[0], 0:cols]).then_inc(empty_sem(name), 1)

            def attention(v, kind, mask, dv):
                heads = HEADS[kind]
                units = prompt_units(heads, kind != "x")

                def outputs(qb):
                    name = (kind, "O", qb)
                    filled(v, name)
                    inv = rinv[:, qb * heads:(qb + 1) * heads]
                    step(v, V.reciprocal(inv, rsum[:, qb * heads:(qb + 1) * heads]))
                    V.tensor_tensor(O_TOK[kind][:, qb, :].rearrange("p (h d) -> p h d", h=heads),
                                    bank_of(name).rearrange("p (h d) -> p h d", h=heads),
                                    inv.unsqueeze(2).to_broadcast([P, heads, dv]), ALU.mult) \
                        .then_inc(empty_sem(name), 1)

                for i, (qb, h) in enumerate(units):
                    name = (kind, "S", i)
                    filled(v, name)
                    bank, nk = bank_of(name), keys(kind, qb)
                    if mask is not None:
                        diag = bank[:, nk - P:nk]
                        step(v, V.tensor_tensor(diag, diag, mask, ALU.add))
                    ins = V.tensor_reduce(negmax[:, i:i + 1], bank[:, 0:nk], AX.X, ALU.max, negate=True)
                    if SCALE[kind] != 1.0:
                        step(v, ins)
                        ins = V.tensor_scalar_mul(negmax[:, i:i + 1], negmax[:, i:i + 1], SCALE[kind])
                    ins.then_inc(row_max, 1)
                    if h == 1 and qb:
                        outputs(qb - 1)
                outputs(TB - 1)

            def sample(v, kind, n_keys, masked):
                banks = ("A0", "A1", "T")[:-(-n_keys // 512)]
                for b in banks:
                    filled(v, (kind, "S", b))
                if masked:
                    new = SCORES[:, PAST_LEN:CACHED]
                    step(v, V.tensor_tensor(new, new, cst[:, K_SAMPLE:K_SAMPLE + DEC_SEQ], ALU.add))
                ins = V.tensor_reduce(negmax[:, 63:64], SCORES[:, 0:n_keys], AX.X, ALU.max, negate=True)
                if SCALE[kind] != 1.0:
                    step(v, ins)
                    ins = V.tensor_scalar_mul(negmax[:, 63:64], negmax[:, 63:64], SCALE[kind])
                ins.then_inc(row_max, 1)
                for b in banks:
                    emptied(v, (kind, "S", b))
                step(v, V.tensor_reduce(rinv[:, 62:63], rsum[:, 60:60 + len(banks)], AX.X, ALU.add))
                step(v, V.reciprocal(rinv[:, 63:64], rinv[:, 62:63]))
                Ps = SBUF_P[kind][0]
                V.tensor_scalar_mul(Ps[:, 0:n_keys], Ps[:, 0:n_keys], rinv[:, 63:64]).then_inc(sample_probs, 1)

            def o_low(v, kind):
                v.wait_ge(o_hi_ready, OHI[kind] + 1)
                step(v, V.tensor_tensor(r_lo[:, 0:4, SEQ:NT], O_S[kind][:, :, :], r_hi[:, 0:4, SEQ:NT].bitcast(F32),
                                        ALU.subtract))
                for f in range(4):
                    name = (kind, "feat", f)
                    v.wait_ge(o_hi_ready, OHI[kind] + f + 2)
                    V.tensor_tensor(r_lo[:, f, 0:SEQ], bank_of(name), r_hi[:, f, 0:SEQ].bitcast(F32), ALU.subtract) \
                        .then_inc(empty_sem(name), 1)

            def merge(v, b):
                for m in range(KT):
                    e = eg[:, m % 2, :]
                    emptied(v, ("gate", b, m))
                    step(v, V.tensor_scalar_add(e, e, 1.0))
                    step(v, V.reciprocal(e, e))
                    name = ("br", b, m)
                    filled(v, name)
                    if b == 0:
                        V.tensor_tensor(both(U[:, m, :]), g_tile(name), both(e), ALU.mult).then_inc(empty_sem(name), 1)
                    else:
                        step(v, V.tensor_tensor(both(e), g_tile(name), both(e), ALU.mult))
                        V.tensor_tensor(U[:, m, :], U[:, m, :], e, ALU.add).then_inc(empty_sem(name), 1)

            def vectors(v):
                name = ("vec",)
                filled(v, name)
                V.tensor_copy(gT[:, 0:V_ROWS], bank_of(name)[:, 0:V_ROWS]).then_inc(empty_sem(name), 1)
                emptied(v, name)
                l0, l1 = gT[:, V_LB:V_LB + 4], gT[:, V_LB + 4:V_LB + 8]
                step(v, V.tensor_tensor(small[:, 16:20], l0, l1, ALU.max))
                step(v, V.tensor_tensor(small[:, 0:4], l0, small[:, 16:20], ALU.subtract))
                V.tensor_tensor(small[:, 4:8], l1, small[:, 16:20], ALU.subtract).then_inc(hz_vector, 1)
                v.wait_ge(hz_scalar, 1)
                step(v, V.tensor_tensor(small[:, 16:20], small[:, 8:12], small[:, 12:16], ALU.add))
                step(v, V.reciprocal(small[:, 20:24], small[:, 16:20]))
                step(v, V.tensor_tensor(small[:, 8:12], small[:, 8:12], small[:, 20:24], ALU.mult))
                step(v, V.tensor_tensor(small[:, 12:16], small[:, 12:16], small[:, 20:24], ALU.mult))
                step(v, V.tensor_scalar(small[:, 16:20], small[:, 8:12], lbsel[:, 0:1], None, ALU.mult))
                step(v, V.scalar_tensor_tensor(small[:, 24:28], small[:, 12:16], lbsel[:, 1:2], small[:, 16:20],
                                               ALU.mult, ALU.add))
                step(v, V.tensor_scalar(small[:, 28:32], small[:, 24:28], -1.0, 1.0, ALU.mult, ALU.add))

            def dve_fox(v):
                e0, e1, flog = eg[0:FOX_HEADS, 0, :], eg[0:FOX_HEADS, 1, :], S["flogT"][:, :]
                for j in range(2):
                    r = slice(64 - 64 * j, 128 - 64 * j)
                    step(v, V.memset(S["fq"][r, :, :].rearrange("p (m t) n -> p m t n", t=2)[:, :, j, :], 0.0))
                step(v, V.memset(M["ncum_parts"][:, :].bitcast(F32), 0.0))
                emptied(v, ("ff", 0))
                V.scalar_tensor_tensor(e0, flog, -1.0, flog, ALU.mult, ALU.max).then_inc(ff_vector, 1)
                v.wait_ge(ff_scalar, 1)
                V.scalar_tensor_tensor(flog, flog, 0.0, e1, ALU.min, ALU.subtract).then_inc(ff_vector, 1)
                to_tokens(v, "fk", S["fk_tok"], M["fk_s"], 512)
                to_tokens(v, "fv", S["fv_tok"], S["fv_s"], 512)
                for tb in range(TB + 1):
                    rows = P if tb < TB else DEC_SEQ
                    name = ("flogf", tb)
                    filled(v, name)
                    V.tensor_copy(S["flogf"][0:rows, tb, :], bank_of(name)[0:rows, 0:FOX_HEADS]) \
                        .then_inc(empty_sem(name), 1)
                v.wait_ge(ff_vector, 2)
                step(v, V.memset(e0, 1.0))
                parts, ncums = M["ncum_parts"], M["ncums"]
                step(v, V.tensor_tensor_scan(e1[:, 0:SEQ], e0[:, 0:SEQ], flog[:, 0:SEQ], 0.0, ALU.mult, ALU.subtract))
                high = parts[0:FOX_HEADS, :]
                step(v, V.tensor_copy(high, e1[:, 0:SEQ]))
                step(v, V.tensor_tensor(parts[LOW_ROWS:LOW_ROWS + FOX_HEADS, :], e1[:, 0:SEQ], high.bitcast(F32),
                                        ALU.subtract))
                emptied(v, ("fq", 3)), emptied(v, ("fq", 2))
                step(v, V.tensor_copy(S["fq_new"][:, :, :], S["fq"][:, :, SEQ:NT]))
                for j in range(2):
                    name = ("clogf", j)
                    filled(v, name)
                    init = 0.0 if j == 0 else ncums[:, 511:512]
                    V.tensor_tensor_scan(ncums[:, 512 * j:512 * j + 512], e0[:, 0:512], bank_of(name)[0:FOX_HEADS, :],
                                         init, ALU.mult, ALU.subtract).then_inc(empty_sem(name), 1)
                    emptied(v, name)
                V.tensor_tensor_scan(ncums[:, PAST_LEN:CACHED], e0[:, 0:DEC_SEQ], flog[:, SEQ:NT],
                                     ncums[:, PAST_LEN - 1:PAST_LEN], ALU.mult, ALU.subtract).then_inc(ncum_ready, 1)
                attention(v, "fox", cst[:, K_CAUSAL:K_CAUSAL + P], FOX_DIM)
                for g in range(2):
                    sample(v, ("foxs", g), CACHED, True)
                o_low(v, "fox")
                merge(v, 0)

            def rope(v, j, tile):
                t = eg[:, 0, :]
                for a in range(2):
                    name = ("rot", j, a)
                    c = slice(a * HALF, (a + 1) * HALF)
                    filled(v, name)
                    V.tensor_tensor(t[:, c], bank_of(name)[:, 0:HALF], SIN[:, c], ALU.mult).then_inc(empty_sem(name), 1)
                    emptied(v, name)
                step(v, V.tensor_tensor(tile, tile, COS, ALU.mult))
                V.tensor_tensor(tile, tile, t, ALU.add).then_inc(rope_ready, 1)
                v.wait_ge(rope_ready, j + 1)

            def dve_mla(v):
                cq, ckv = S["cq"], S["ckv"]
                for k, nt, tile, col in ((1, QT, cq, V_CQ), (2, MT, ckv, V_CKV)):
                    square_sum(v, k, S["msq"])
                    v.wait_ge(rs_ready, k + 1)
                    for t in range(nt):
                        ins = V.scalar_tensor_tensor(tile[:, t, :], tile[:, t, :], gT[:, col + t:col + t + 1], rs,
                                                     ALU.mult, ALU.mult)
                        if k == 1 and t == nt - 1:
                            ins.then_inc(cqn_ready, 1)
                        else:
                            step(v, ins)
                rope(v, 0, R["kpe"][:, :])
                rope(v, 1, S["qpe"][:, 0, :])
                rope(v, 2, S["qpe"][:, 1, :])
                to_tokens(v, "ckv", S["mo_tok"], S["ckv_s"], 320)
                v.wait_ge(DMA["ckv_out"], 64)
                attention(v, "mla", cst[:, K_CHUNK:K_CHUNK + P], MLA_V)
                sample(v, "mlas", CACHED, False)
                o_low(v, "mla")
                merge(v, 1)

            def dve_hgrn(v):
                hq, hf, hk, hg, hE = S["hq"], S["hf"], S["hk"], S["hg"], S["hE"]
                ta, tb_, tc, td, te = eg[:, 0, :], eg[:, 1, :], acc, rs, hE[:, 0, :]
                for h in range(HG_HEADS):
                    z = hf[:, h, :]
                    emptied(v, ("hf", h))
                    step(v, V.scalar_tensor_tensor(ta, z, -1.0, z, ALU.mult, ALU.max))
                    V.tensor_scalar(tc, z, -1.0, EXP_CLIP, ALU.mult, ALU.min).then_inc(hz_vector, 1)
                    v.wait_ge(hz_scalar, 2 + 2 * h)
                    lb, one_less = small[:, 24 + h:25 + h], small[:, 28 + h:29 + h]
                    step(v, V.tensor_scalar(tc, tc, lb, 1.0, ALU.mult, ALU.add))
                    step(v, V.tensor_scalar(td, tc, SMALL, 1.0, ALU.mult, ALU.max))
                    step(v, V.tensor_scalar_min(tc, tc, BIG))
                    V.scalar_tensor_tensor(te, z, 0.0, tb_, ALU.max, ALU.add).then_inc(hz_vector, 1)
                    v.wait_ge(hz_scalar, 3 + 2 * h)
                    step(v, V.tensor_scalar(hk[:, h, :], hk[:, h, :], one_less, None, ALU.mult))
                    step(v, V.scalar_tensor_tensor(z, z, 0.0, tb_, ALU.min, ALU.subtract))
                    step(v, V.tensor_tensor(z, z, tc, ALU.add))
                    step(v, V.tensor_tensor(z, z, td, ALU.add))
                    V.tensor_tensor_scan(te, cst[:, K_RESET:K_RESET + NT], z, 0.0, ALU.mult, ALU.add) \
                        .then_inc(hz_vector, 1)
                    v.wait_ge(hz_vector, 4 + 3 * h)
                    step(v, V.tensor_copy(z, te))
                    for m in ((), (0,), (1, 2), (3,))[h]:
                        emptied(v, ("hg", m))
                        step(v, V.tensor_scalar_add(hg[:, m, :], hg[:, m, :], 1.0))
                        step(v, V.reciprocal(hg[:, m, :], hg[:, m, :]))
                AT, ATs = R["hAT"], R["hATs"]
                items = [(h, lv) for h in range(HG_HEADS) for lv in range(len(LEVELS))]

                def scale(i):
                    h, lv = items[i]
                    half = LEVELS[lv]
                    v.wait_ge(hl_exp, i + 1)
                    if i >= 2:
                        filled(v, ("hgA", *items[i - 2]))
                    e = level_view(hE[:, i % 2, :], lv)
                    step(v, V.tensor_tensor(level_view(eg[:, i % 2, :], lv)[:, :, half:], level_view(hq[:, h, :], lv)[:, :, half:],
                                            e[:, :, half:], ALU.mult))
                    V.tensor_tensor(level_view(acc_rs[:, i % 2, :], lv)[:, :, 0:half], level_view(hk[:, h, :], lv)[:, :, 0:half],
                                    e[:, :, 0:half], ALU.mult).then_inc(hl_scaled, 1)
                    v.wait_ge(hl_scaled, i + 1)

                def choose(h, lv):
                    name = ("hgA", h, lv)
                    filled(v, name)
                    G = bank_of(name)
                    mask = masks[:, lv, :].unsqueeze(1).to_broadcast([P, TB, P])
                    ins = V.copy_predicated(AT[:, h % 2, :, :], mask, G[:, 0, :].rearrange("p (b t) -> p b t", b=TB))
                    if lv == NL - 1 or LEVELS[lv] < DEC_SEQ:
                        step(v, ins)
                        ins = V.copy_predicated(ATs[:, h % 2, :], masks[0:DEC_SEQ, lv, 0:DEC_SEQ],
                                                G[0:DEC_SEQ, 1, 0:DEC_SEQ])
                    ins.then_inc(empty_sem(name), 1)
                    emptied(v, name)

                def decay_differences(h):
                    kd, lc = R["hkd"], hf[:, h, :]
                    if h:
                        filled(v, ("hg", "kdT", h - 1)), filled(v, ("hg", "kdTs", h - 1))
                    ends = lc[:, 0:SEQ].rearrange("p (b w) -> p b w", w=P)
                    step(v, V.tensor_tensor(kd[:, 0:SEQ].rearrange("p (b w) -> p b w", w=P), ends,
                                            ends[:, :, P - 1:P].to_broadcast([P, TB, P]), ALU.subtract))
                    V.tensor_scalar(kd[:, SEQ:NT], lc[:, SEQ:NT], lc[:, NT - 1:NT], None, ALU.subtract) \
                        .then_inc(hd_diff, 1)

                def decay_scale(h):
                    v.wait_ge(hd_exp, h + 1)
                    step(v, V.tensor_tensor(R["hqd"][:, :], hq[:, h, :], R["hqd"][:, :], ALU.mult))
                    V.tensor_tensor(R["hkd"][:, :], hk[:, h, :], R["hkd"][:, :], ALU.mult).then_inc(hd_scaled, 1)

                def states(h):
                    name = ("hg", "U", h)
                    filled(v, name)
                    bank, ST = bank_of(name), R["hST"]
                    step(v, V.tensor_copy(ST[:, 0, :], bank[:, 0:P]))
                    for tb in range(1, TB - 1):
                        step(v, V.scalar_tensor_tensor(ST[:, tb, :], ST[:, tb - 1, :], small[:, 16 + tb:17 + tb],
                                                       bank[:, P * tb:P * tb + P], ALU.mult, ALU.add))
                    V.scalar_tensor_tensor(R["hSf"][:, h, :], ST[:, TB - 2, :], small[:, 15 + TB:16 + TB],
                                           bank[:, P * (TB - 1):P * TB], ALU.mult, ALU.add) \
                        .then_inc(empty_sem(name), 1)

                def new_state(h):
                    filled(v, ("hg", "Os", h))
                    name = ("hg", "Us", h)
                    filled(v, name)
                    V.scalar_tensor_tensor(R["hS0"][:, h, :], R["hS0"][:, h, :], small[:, 16 + TB:17 + TB],
                                           bank_of(name)[:, 0:P], ALU.mult, ALU.add).then_inc(empty_sem(name), 1)

                hg_difference(V, 0), hg_difference(V, 1)
                to_tokens(v, "hi", S["hv"], S["hv_s"], 512)
                v.wait_ge(zeros_ready, 4)
                for i, (h, lv) in enumerate(items):
                    scale(i)
                    if lv:
                        choose(h, lv - 1)
                    elif h:
                        choose(h - 1, len(LEVELS) - 1)
                        choose(h - 1, NL - 1)
                    if h and lv == HG_STEP_U + 1:
                        states(h - 1)
                    if h and lv == HG_STEP_O + 1:
                        new_state(h - 1)
                    if lv == 4:
                        decay_differences(h)
                    if lv == len(LEVELS) - 1:
                        decay_scale(h)
                h = HG_HEADS - 1
                choose(h, len(LEVELS) - 1)
                choose(h, NL - 1)
                states(h)
                new_state(h)
                emptied(v, ("hg", "Us", h))
                for f in range(4):
                    g = gT[:, V_HG:V_HG + 1]
                    e = hE[:, f % 2, :]
                    name = ("hg", "feat", f)
                    filled(v, name)
                    if f >= 2:
                        v.wait_ge(r_hi_ready, f - 1)
                    V.scalar_tensor_tensor(e[:, 0:SEQ], bank_of(name), g, hg[:, f, 0:SEQ], ALU.mult, ALU.mult) \
                        .then_inc(empty_sem(name), 1)
                    name = ("hg", "feats", f)
                    filled(v, name)
                    V.scalar_tensor_tensor(e[:, SEQ:NT], bank_of(name)[:, 0:DEC_SEQ], g, hg[:, f, SEQ:NT],
                                           ALU.mult, ALU.mult).then_inc(empty_sem(name), 1)
                    emptied(v, name)
                    V.engine_nop().then_inc(r32_ready, 1)
                    v.wait_ge(r_hi_ready, f + 1)
                    if f == 0:
                        v.wait_ge(DMA["out"], 32)
                    V.tensor_tensor(r_lo[:, f, :], e, r_hi[:, f, :].bitcast(F32), ALU.subtract).then_inc(r_lo_ready, 1)
                merge(v, 2)

            def dve_cross(v):
                for t in range(KT):
                    low(v, t, KT, U)
                square_sum(v, 3, sq)
                post(v, 3, V_NORM + KT, sq)
                for j in range(4):
                    name = ("memT", j)
                    v.wait_ge(o_hi_ready, 11 + j)
                    V.tensor_tensor(R["m_lo"][:, 2 * j:2 * j + 2, :], bank_of(name).rearrange("p (f n) -> p f n", f=2),
                                    R["m_hi"][:, 2 * j:2 * j + 2, :].bitcast(F32), ALU.subtract) \
                        .then_inc(empty_sem(name), 1)
                for kind, tile in (("memk", S["mk_tok"]), ("memv", S["mv_tok"])):
                    for b in range(MB):
                        name = (kind, "tok", b)
                        filled(v, name)
                        V.tensor_copy(tile[:, b, :], bank_of(name)).then_inc(empty_sem(name), 1)
                square_sum(v, 4, sq)
                h_pre(v, 4, 2 * KT, V_NORM + 2 * KT)
                attention(v, "x", None, X_DIM)
                sample(v, "xs", N_MEM, False)
                o_low(v, "x")
                square_sum(v, 5, S["sqx"])
                post(v, 5, V_NORM + 3 * KT, S["sqx"])
                square_sum(v, 6, sq)
                h_pre(v, 6, 3 * KT, V_NORM + 4 * KT)

            def h_pre(v, k, base, gcol):
                v.wait_ge(rs_ready, k + 1)
                done = {0: 0, 2 * KT: KT, 3 * KT: 2 * KT}[base]
                for t in range(KT + 1):
                    if t < KT:
                        V.scalar_tensor_tensor(sq[:, t, :], x[:, t, :], gT[:, gcol + t:gcol + t + 1], rs,
                                               ALU.mult, ALU.mult).then_inc(h32_ready, 1)
                        v.wait_ge(h32_ready, done + t + 1)
                    if t:
                        low(v, t - 1, base, sq)

            def dve_mlp(v):
                for t in range(KT):
                    step(v, V.memset(U[:, t, :], 0.0))
                with v.Fori(0, MLP_GROUPS) as g:
                    plus = g * (MLP_N // 2)
                    for m in range(KT):
                        name = ("up", m)
                        emptied(v, name, plus=plus)
                        t2 = S["t2"][:, m % 2, :]
                        if m >= 2:
                            v.wait_ge(r_lo_ready, 4 + g * KT + m - 1)
                        V.tensor_tensor(t2, S["t1"][:, m % 2, :], S["t1"][:, m % 2, :], ALU.mult).then_inc(r32_ready, 1)
                        v.wait_ge(r_hi_ready, 4 + g * KT + m + 1)
                        V.tensor_tensor(r_lo[:, m, :], t2, r_hi[:, m, :].bitcast(F32), ALU.subtract) \
                            .then_inc(r_lo_ready, 1)
                    for m in range(KT):
                        name = ("down", m)
                        filled(v, name, plus=plus)
                        V.tensor_tensor(both(U[:, m, :]), both(U[:, m, :]), g_tile(name), ALU.add) \
                            .then_inc(empty_sem(name), 1)
                    emptied(v, ("down", KT - 1), plus=plus), emptied(v, ("down", KT - 2), plus=plus)
                V.engine_nop().then_inc(u_ready, 1)
                square_sum(v, 7, sq)
                post(v, 7, V_NORM + 5 * KT, sq)
                v.wait_ge(x_ready, 3 * KT)

            def layer(v):
                n[0] = 0
                vectors(v)
                square_sum(v, 0, sq)
                h_pre(v, 0, 0, V_NORM)
                dve_fox(v)
                dve_mla(v)
                dve_hgrn(v)
                dve_cross(v)
                dve_mlp(v)

            return layer

        ends_in, ends_out = plan_ends("in"), plan_ends("out")
        block = ctx.enter_context(nc.Block())

        @block.sync
        def _(sp):
            sp.dma_start(cst[:, :], A["constants"]).then_inc(consts_loaded, 16)
            sp.dma_start(R["mask32"][:, :, :], A["level_masks"]).then_inc(consts_loaded, 16)
            end_of_phase_sp(sp)
            with sp.Fori(0, DEPTH) as l:
                sp_layer(sp, l)
                end_of_phase_sp(sp)
            t = ends_out
            for c in range(2):
                for tb in range(TB + 1):
                    emptied(sp, ("y", c * (TB + 1) + tb), t=t)
            sp.dma_start(O["y_prompt"][0].rearrange("(b p) c -> p b c", p=P), S["x_tok"][:, :, :])                 .then_inc(DMA["y_out"], 16)
            sp.dma_start(O["y_sample"][0], S["xs_tok"][:, :]).then_inc(DMA["y_out"], 16)
            sp.wait_ge(DMA["y_out"], 32)

        @block.gpsimd
        def _(pool):
            end_of_phase(pool, 1)
            with pool.Fori(0, DEPTH) as l:
                pool_layer(pool)
                end_of_phase(pool, l + 2)

        @block.tensor
        def _(pe):
            pe.wait_ge(consts_loaded, 32)
            pe.wait_ge(DMA["mem"], 32)
            for f in range(KT):
                transposes(pe, ("x", f), [(S["x_tok"][:, tb, P * f:P * f + P], P * tb) for tb in range(TB)], t=ends_in)
                transposes(pe, ("xs", f), [(S["xs_tok"][:, P * f:P * f + P], 0)], t=ends_in)
            end_of_phase(pe, 1)
            with pe.Fori(0, DEPTH) as l:
                pe_layer(pe)
                end_of_phase(pe, l + 2)
            for c in range(2):
                for tb in range(TB + 1):
                    c0, c1 = (P * tb, P * tb + P) if tb < TB else (SEQ, NT)
                    name = ("y", c * (TB + 1) + tb)
                    bank = bank_free(pe, name, t=ends_out)
                    for f in range(4):
                        last = pe.transpose(bank[0:c1 - c0, P * f:P * f + P], x[:, 4 * c + f, c0:c1], ident)
                    last.then_inc(fill_sem(name, ends_out), 1)

        @block.scalar
        def _(act):
            act.preload_act_table_set("natural_log_exp_and_others")
            act.dma_start(S["x_tok"][:, :, :], A["x_prompt"][0].rearrange("(b p) c -> p b c", p=P))                 .then_inc(DMA["mem"], 16)
            act.dma_start(S["xs_tok"][:, :], A["x_sample"][0]).then_inc(DMA["mem"], 16)
            end_of_phase(act, 1)
            layer = act_code()
            with act.Fori(0, DEPTH) as l:
                layer(act, l)
                end_of_phase(act, l + 2)

        @block.vector
        def _(v):
            nc.vector.memset(eps[:, :], EPS).then_inc(vector_chain, 1)
            nc.vector.memset(zero[:, :], 0.0).then_inc(vector_chain, 1)
            v.wait_ge(consts_loaded, 32)
            nc.vector.tensor_copy(masks[:, :, :], R["mask32"][:, :, :]).then_inc(vector_chain, 1)
            nc.vector.tensor_copy(head_rows[:, :], cst[:, K_HEAD:K_HEAD + FOX_HEADS]).then_inc(vector_chain, 1)
            for f in range(KT):
                for name, dst in ((("x", f), x[:, f, 0:SEQ]), (("xs", f), x[:, f, SEQ:NT])):
                    filled(v, name, t=ends_in)
                    nc.vector.tensor_copy(dst, bank_of(name, ends_in)[:, 0:dst.shape[1]])                         .then_inc(empty_sem(name, ends_in), 1)
            emptied(v, ("x", KT - 1), t=ends_in), emptied(v, ("xs", KT - 1), t=ends_in)
            end_of_phase(v, 1)
            layer = dve_code()
            with v.Fori(0, DEPTH) as l:
                layer(v)
                end_of_phase(v, l + 2)
            for c in range(2):
                for tb in range(TB + 1):
                    name = ("y", c * (TB + 1) + tb)
                    filled(v, name, t=ends_out)
                    dst = S["x_tok"][:, tb, 512 * c:512 * c + 512] if tb < TB else S["xs_tok"][:, 512 * c:512 * c + 512]
                    nc.vector.tensor_copy(dst, bank_of(name, ends_out)[0:dst.shape[0], :])                         .then_inc(empty_sem(name, ends_out), 1)


_INS = ["x_prompt", "x_sample", "cache_fox_k", "cache_fox_v", "cache_fox_logf", "cache_mla_ckv", "cache_mla_kpe",
        "state_hgrn", "cache_mem_k", "cache_mem_v", "mem_prompt", "w_in", "b_fox", "g_mla_q", "w_mla_uq",
        "g_mla_kv", "w_mla_ukv", "g_hgrn_out", "lb_hgrn", "w_branch", "w_out", "w_xq", "w_mem_k", "w_mem_v",
        "w_xo", "w_up", "w_down", "g_norm"]
_OUTS = {
    "y_prompt": (1, SEQ, D_MODEL), "y_sample": (1, DEC_SEQ, D_MODEL),
    "p_fox_k": (DEPTH, 1, SEQ, FOX_HEADS, FOX_DIM), "p_fox_v": (DEPTH, 1, SEQ, FOX_HEADS, FOX_DIM),
    "p_fox_logf": (DEPTH, 1, SEQ, FOX_HEADS), "p_mla_ckv": (DEPTH, 1, SEQ, MLA_KV_RANK),
    "p_mla_kpe": (DEPTH, 1, SEQ, MLA_ROPE), "p_hgrn_state": (DEPTH, 1, HG_HEADS, HG_DIM, HG_DIM),
    "p_mem_k": (DEPTH, 1, N_MEM, X_HEADS, X_DIM), "p_mem_v": (DEPTH, 1, N_MEM, X_HEADS, X_DIM),
    "s_fox_k": (DEPTH, 1, DEC_SEQ, FOX_HEADS, FOX_DIM), "s_fox_v": (DEPTH, 1, DEC_SEQ, FOX_HEADS, FOX_DIM),
    "s_fox_logf": (DEPTH, 1, DEC_SEQ, FOX_HEADS), "s_mla_ckv": (DEPTH, 1, DEC_SEQ, MLA_KV_RANK),
    "s_mla_kpe": (DEPTH, 1, DEC_SEQ, MLA_ROPE), "s_hgrn_state": (DEPTH, 1, HG_HEADS, HG_DIM, HG_DIM),
}


def shape_constants():
    c = np.zeros((P, K_END), np.float32)
    i = np.arange(P)
    c[:, K_ID:K_ID + P] = np.eye(P)
    c[:, K_ONES:K_ONES + P] = 1.0
    c[:, K_CAUSAL:K_CAUSAL + P] = np.where(i[:, None] >= i[None, :], 0.0, NEG_BIG)
    c[:, K_CHUNK:K_CHUNK + P] = np.where(i[:, None] // CHUNK >= i[None, :] // CHUNK, 0.0, NEG_BIG)
    j = np.arange(DEC_SEQ)
    c[:, K_SAMPLE:K_SAMPLE + DEC_SEQ] = np.where((i % DEC_SEQ)[:, None] >= j[None, :], 0.0, NEG_BIG)
    half = MLA_ROPE // 2
    for m in range(P):
        if m % MLA_ROPE < half:
            c[m + half, K_ROT + m] = -1.0
        else:
            c[m - half, K_ROT + m] = 1.0
    freq = np.float32(ROPE_THETA) ** (-np.arange(half, dtype=np.float32) / np.float32(half))
    pos = np.concatenate([np.arange(SEQ), PAST_LEN + np.arange(DEC_SEQ)]).astype(np.float32)
    ang = (pos[None, :] * freq[:, None]).astype(np.float32)
    c[:, K_COS:K_COS + NT] = np.tile(np.cos(ang), (P // half, 1))
    c[:, K_SIN:K_SIN + NT] = np.tile(np.sin(ang), (P // half, 1))
    c[:, K_RESET:K_RESET + NT] = (np.arange(NT) % P != 0)
    for g in range(2):
        for h in range(4):
            c[4 * g + h, K_SEL + P * g + 32 * h:K_SEL + P * g + 32 * h + 32] = 1.0
    for h in range(FOX_HEADS):
        c[[h, LOW_ROWS + h], K_HEAD + h] = 1.0
    masks = np.zeros((P, NL, P), np.float32)
    s, t = i[:, None], i[None, :]
    for n, w in enumerate(LEVELS):
        masks[:, n, :] = (s // (2 * w) == t // (2 * w)) & (s % (2 * w) < w) & (t % (2 * w) >= w)
    masks[:, NL - 1, :] = s == t
    select = np.zeros((DEPTH, P, DEPTH), np.float32)
    for l in range(DEPTH):
        select[l, :, 1:l + 1] = 1.0
    return {"constants": c, "level_masks": masks, "lb_select": select}


def kernel(**inputs):
    import numpy as _np
    import concourse.bacc as _bacc
    from concourse import mybir as _mybir
    from concourse.bass_utils import run_bass_kernel_spmd as _run

    nc = _bacc.Bacc("TRN2", target_bir_lowering=False, num_devices=1)
    arrays, A, O = {}, {}, {}
    given = {n: _np.ascontiguousarray(inputs[n]) for n in _INS}
    given.update(shape_constants())
    for name, a in given.items():
        arrays[f"in_{name}"] = a
        A[name] = nc.dram_tensor(f"in_{name}", a.shape, _mybir.dt.from_np(a.dtype), kind="ExternalInput").ap()
    for name, shape in _OUTS.items():
        O[name] = nc.dram_tensor(f"out_{name}", shape, _mybir.dt.float32, kind="ExternalOutput").ap()
    hybrid_encoder(nc, A, O)
    r = _run(nc, [arrays], core_ids=[0])
    return tuple(r.results[0][f"out_{name}"] for name in _OUTS)
```

```python
from contextlib import ExitStack

import numpy as np

import concourse.bass as bass
from concourse import mybir

F32 = mybir.dt.float32
F32R = mybir.dt.float32r
U8 = mybir.dt.uint8
ALU = mybir.AluOpType
ACT = mybir.ActivationFunctionType
AX = mybir.AxisListType

P = 128
D_MODEL, SEQ, DEPTH, DEC_SEQ, PAST_LEN = 1024, 512, 2, 32, 1024
CHUNK, N_MEM, EPS, NEG_BIG, EXP_CLIP = 64, 256, 1e-6, -1e30, 80.0
FOX_HEADS, FOX_DIM = 8, 64
MLA_HEADS, MLA_Q_RANK, MLA_KV_RANK, MLA_NOPE, MLA_ROPE, MLA_V = 4, 384, 256, 128, 64, 128
ROPE_THETA = 10000.0
HG_HEADS, HG_DIM = 4, 128
X_HEADS, X_DIM = 4, 128
D_FF = 4 * D_MODEL

NT = SEQ + DEC_SEQ
HALF = NT // 2
TB = SEQ // P
KT = D_MODEL // P
MT = MLA_KV_RANK // P
QT = MLA_Q_RANK // P
MB = N_MEM // P
CB = PAST_LEN // P
CACHED = PAST_LEN + DEC_SEQ
RAW, SPLIT = 4, 2
MLP_GROUPS = D_FF // D_MODEL

C_FQ, C_FK, C_FV, C_FF = 0, 512, 1024, 1536
C_CQ = C_FF + FOX_HEADS
C_CKV = C_CQ + MLA_Q_RANK
C_KPE = C_CKV + MLA_KV_RANK
C_HQ = C_KPE + MLA_ROPE
C_HF, C_HI, C_HG = C_HQ + 512, C_HQ + 1024, C_HQ + 1536
C_GATE = C_HQ + 2048

K_ID, K_ONES, K_CAUSAL, K_CHUNK, K_SAMPLE, K_ROT = 0, 128, 256, 384, 512, 544
K_COS, K_SIN, K_RESET, K_SEL = 672, 672 + NT, 672 + 2 * NT, 672 + 3 * NT
K_HEAD = K_SEL + 256
K_END = K_HEAD + FOX_HEADS
V_NORM, V_CQ, V_CKV, V_HG, V_LB, V_ROWS = 0, 48, 51, 53, 54, 62

LEVELS = [64, 32, 16, 8, 4, 2, 1]
NL = len(LEVELS) + 1
LOW_ROWS = 32
BIG, SMALL = 2.0 ** 60, 2.0 ** -60
assert PAST_LEN % CHUNK == 0 and DEC_SEQ <= CHUNK


class Turns:

    def __init__(self):
        self.fills, self.uses, self.of = {}, {}, {}

    def add(self, bank, name, parts=1):
        assert name not in self.of, name
        fills, uses = self.fills.get(bank, 0), self.uses.get(bank, 0)
        self.fills[bank], self.uses[bank] = fills + parts, uses + 1
        self.of[name] = (bank, fills, uses, parts)


def weight_slots():
    s = []

    def w_in(col, n, name):
        s.extend(("w_in", 0, KT, col + P * i, P, [(name, i)]) for i in range(n))

    def branch(b):
        for j in range(KT // 2):
            for n in (2 * j, 2 * j + 1):
                s.append(("w_in", 0, KT, C_GATE + D_MODEL * b + P * n, P, [("gate", b, n)]))
            s.append((f"w_branch{b}", 0, 4, 256 * j, 256, [("br", b, 2 * j), ("br", b, 2 * j + 1)]))

    w_in(C_FF, 1, "ff"), w_in(C_FQ, 4, "fq"), w_in(C_FK, 4, "fk"), w_in(C_FV, 4, "fv")
    branch(0)
    w_in(C_CQ, QT, "cq"), w_in(C_CKV, MT, "ckv")
    s.append(("kpe", 0, KT, C_KPE, MLA_ROPE, [("kpe", 0)]))
    branch(1)
    w_in(C_HF, 4, "hf"), w_in(C_HG, 4, "hg"), w_in(C_HQ, 4, "hq"), w_in(C_HI, 4, "hi")
    branch(2)
    s.extend(("w_out", 0, KT, P * n, P, [("out", n)]) for n in range(KT))
    s.extend(("w_mem_k", 0, KT, P * n, P, [("memk", n)]) for n in range(4))
    s.extend(("w_mem_v", 0, KT, P * n, P, [("memv", n)]) for n in range(4))
    s.extend(("w_xq", 0, KT, P * n, P, [("xq", n)]) for n in range(4))
    s.extend(("w_xo", 0, 4, 256 * j, 256, [("xo", 2 * j), ("xo", 2 * j + 1)]) for j in range(4))
    for g in range(1):
        s.extend(("w_up", 0, KT, P * n, P, [("up", n)]) for n in range(KT))
        s.extend(("w_down", 0, KT, P * n, P, [("down", n)]) for n in range(KT))
    return s


SLOTS = weight_slots()
SLOT_OF = {name: n for n, s in enumerate(SLOTS) for name in s[5]}
MLP0 = SLOT_OF["up", 0]
MLP_N = 2 * KT
HG_STEP_U, HG_STEP_O = 0, 2


PREPARED = {
    "fox": {8 + 6 * j: ("foxs", 0, "KT", j) for j in range(4)},
    "mla": dict(zip((2, 4, 6, 8, 10, 12, 14, 16, 17), [("mlas", "ckvT", j) for j in range(4)] +
                    [("mlas", "kpeT", j) for j in range(2)] + [("mlas", "wukT", j) for j in range(2)] +
                    [("mlas", "qabs")])),
    "x": {4: ("xs", "KT", 0), 8: ("xs", "KT", 1)},
}


def prompt_units(heads):
    return [(qb, h) for qb in range(TB) for h in range(heads)]


def plan_layer():
    t = Turns()
    count = {"g": 0, "t": 0}

    def gemm(*names):
        for n in names:
            t.add(f"G{count['g'] % 2}", n)
            count["g"] += 1

    def tr(name):
        t.add("TO"[count["t"] % 2], name)
        count["t"] += 1

    def stat(k):
        t.add("A0", ("stat", k, 0)), t.add("A1", ("stat", k, 1))

    def tokens(kind):
        for tb in range(TB + 1):
            tr((kind, "tok", tb))

    def attention(kind, heads):
        n = TB * heads
        for i in range(n + 2):
            if i < n:
                t.add(f"A{i % 2}", (kind, "S", i))
            if 1 <= i <= n:
                gemm((kind, "PT", i - 1))
            if i >= 2 and (i - 2) % heads == 0:
                t.add("O", (kind, "O", (i - 2) // heads), heads)
            if i in PREPARED[kind]:
                t.add("T", PREPARED[kind][i])

    def sample(kind, banks=("A0", "A1", "T"), batches=3):
        for b in banks:
            t.add(b, (kind, "S", b))
        for j in range(batches):
            tr((kind, "PT", j))
        t.add("A0", (kind, "PV"))

    def to_features(kind):
        for f in range(4):
            tr((kind, "feat", f))

    def branch(b):
        for j in range(KT // 2):
            gemm(("gate", b, 2 * j), ("gate", b, 2 * j + 1), ("br", b, 2 * j), ("br", b, 2 * j + 1))

    tr(("vec",))
    stat(0)
    gemm(("ff", 0), *[("fq", n) for n in range(4)])
    for tb in range(TB + 1):
        tr(("flogf", tb))
    tr(("clogf", 0)), tr(("clogf", 1))
    gemm(*[("fk", n) for n in range(4)], ("fv", 0))
    tokens("fk")
    gemm(*[("fv", n) for n in range(1, 4)])
    tokens("fv")
    attention("fox", FOX_HEADS)
    for g in range(2):
        for b in ("A0", "A1", "T"):
            t.add(b, (("foxs", g), "S", b))
        if g == 0:
            gemm(*[("foxs", 1, "KT", j) for j in range(4)])
        for j in range(3):
            tr((("foxs", g), "PT", j))
        t.add("A0", (("foxs", g), "PV"))
    to_features("fox")
    branch(0)
    gemm(*[("cq", n) for n in range(QT)])
    gemm(("ckv", 0))
    stat(1)
    gemm(*[("ckv", n) for n in range(1, MT)], ("kpe", 0))
    stat(2)
    t.add("A0", ("rot", 0, 0)), t.add("A1", ("rot", 0, 1))
    gemm(*[("qn", h) for h in range(4)], ("qpe", 0), ("qpe", 1))
    for j in (1, 2):
        t.add("A0", ("rot", j, 0)), t.add("A1", ("rot", j, 1))
    tokens("ckv")
    for h in range(4):
        gemm(("kn", h))
    for tb in range(TB):
        gemm(("vm", tb))
    attention("mla", MLA_HEADS)
    sample("mlas")
    t.add("A1", ("mlas", "o"))
    to_features("mla")
    branch(1)
    gemm(*[(k, n) for k in ("hf", "hg", "hq", "hi") for n in range(4)])
    tokens("hi")
    for h in range(HG_HEADS + 1):
        for lv in range(NL):
            if h < HG_HEADS:
                gemm(("hgA", h, lv))
            if h and lv == HG_STEP_U:
                t.add("A0", ("hg", "U", h - 1)), t.add("A1", ("hg", "Us", h - 1))
            if h and lv == HG_STEP_O:
                tr(("hg", "O", h - 1)), tr(("hg", "Os", h - 1))
        if h < HG_HEADS:
            tr(("hg", "kdT", h)), tr(("hg", "kdTs", h))
    gemm(*[("hg", "feat", f) for f in range(4)])
    branch(2)
    tr(("memT", 0)), tr(("memT", 1))
    gemm(*[("out", n) for n in range(KT // 2)])
    tr(("memT", 2)), tr(("memT", 3))
    gemm(*[("out", n) for n in range(KT // 2, KT)])
    gemm(("memk", 0))
    stat(3)
    gemm(*[("memk", n) for n in range(1, 4)], ("memv", 0), ("memv", 1))
    stat(4)
    gemm(("memv", 2), ("memv", 3))
    gemm(("xq", 0))
    for kind in ("memk", "memv"):
        for b in range(MB):
            tr((kind, "tok", b))
    gemm(*[("xq", n) for n in range(1, 4)])
    attention("x", X_HEADS)
    sample("xs", ("A0",), 1)
    to_features("x")
    gemm(*[("xo", n) for n in range(KT)])
    stat(5)
    stat(6)
    gemm(*[("up", n) for n in range(KT)], *[("down", n) for n in range(KT)])
    for b in ("G0", "G1"):
        t.fills[b] += (MLP_GROUPS - 1) * MLP_N // 2
        t.uses[b] += (MLP_GROUPS - 1) * MLP_N // 2
    stat(7)
    return t


def plan_ends(kind):
    t = Turns()
    if kind == "in":
        for f in range(KT):
            t.add("TO"[f % 2], ("x", f)), t.add(f"A{f % 2}", ("xs", f))
    else:
        for j in range(2 * (TB + 1)):
            t.add("TO"[j % 2], ("y", j))
    return t


def hybrid_encoder(nc, A, O):
    with ExitStack() as ctx:
        def sb(name, shape, dt=F32):
            return ctx.enter_context(nc.sbuf_tensor(name, shape, dt))

        def sem(name):
            return ctx.enter_context(nc.semaphore(name))

        def alternatives(limit, *groups):
            made = {}
            for group in groups:
                size = sum(int(np.prod(shape[1:])) * 4 for _, shape, _ in group)
                assert limit is None or size <= limit, (group[0][0], size, limit)
                with ExitStack() as inner:
                    for name, shape, dt in group:
                        made[name] = inner.enter_context(nc.sbuf_tensor(name, shape, dt))
            return made

        x = sb("x", [P, KT, NT])
        h_hi, h_lo = sb("h_hi", [P, KT, NT], F32R), sb("h_lo", [P, KT, NT], F32R)
        raw = sb("w_raw", [P, RAW, KT * P])
        w_hi, w_lo = sb("w_hi", [P, SPLIT, KT * P], F32R), sb("w_lo", [P, SPLIT, KT * P], F32R)
        cst = sb("constants", [P, K_END])
        masks = sb("level_masks", [P, NL, P], U8)
        vecs = sb("vecs", [64, P])
        gT = sb("vectors", [P, 64])
        lbsel = sb("lb_select", [P, DEPTH])
        small = sb("small", [P, 32])
        bfox = sb("b_fox_col", [FOX_HEADS, 1])
        eps, zero = sb("eps", [P, 1]), sb("zero", [P, 1])
        head_rows = sb("head_rows", [P, FOX_HEADS], F32R)
        acc_rs = sb("square_sum_and_rs", [P, 2, NT])
        acc, rs, PT = acc_rs[:, 0, :], acc_rs[:, 1, :], acc_rs
        eg = sb("gate_exp", [P, 2, NT])
        negmax, rsum, rinv = sb("negmax", [P, 64]), sb("row_sum", [P, 64]), sb("row_inv", [P, 64])

        RW = 8 * NT
        M = alternatives(
            4 * RW,
            [("U", [P, KT, NT], F32)],
            [("fk_s", [DEC_SEQ, 512], F32), ("fo_tok", [P, TB, 512], F32), ("ncums", [FOX_HEADS, CACHED], F32),
             ("ncum_parts", [P, SEQ], F32R)])
        m_area = sb("m_area", [P, RW])
        R = alternatives(
            8 * RW,
            [("r_hi", [P, KT, NT], F32R), ("r_lo", [P, KT, NT], F32R)],
            [("sq", [P, KT, NT], F32)],
            [("mask32", [P, NL, P], F32)],
            [("fvT", [P, 4, NT], F32)],
            [("fKc", [P, CB, 256], F32), ("fKT", [P, 2, PAST_LEN], F32), ("fVc", [P, CB, 256], F32),
             ("fPs", [P, CACHED], F32), ("fPTs", [P, CB + 1, P], F32)],
            [("ckvc", [P, CB, 256], F32), ("ckvT", [P, MT, PAST_LEN], F32), ("kpec", [P, CB, 128], F32),
             ("kpeT", [P, PAST_LEN], F32), ("wukT", [P, 4, 256], F32), ("qabs", [P, MT, P], F32),
             ("lat", [P, MT, P], F32), ("kpe", [P, NT], F32)],
            [("hgap0", [P, 2176], F32), ("ho_tok", [P, TB, 512], F32), ("hsq", [P, HG_DIM], F32),
             ("hST", [P, TB, P], F32), ("hS0", [P, HG_HEADS, P], F32),
             ("hSf", [P, HG_HEADS, P], F32), ("hAT", [P, 2, TB, P], F32),
             ("hATs", [DEC_SEQ, 2, DEC_SEQ], F32), ("hkd", [P, NT], F32), ("hkdT", [P, TB, P], F32), ("hkdTs", [DEC_SEQ, P], F32),
             ("hqd", [P, NT], F32)],
            [("hviT", [P, 4, NT], F32)],
            [("mgap", [P, KT, NT], F32), ("m_hi", [P, KT, N_MEM], F32R), ("m_lo", [P, KT, N_MEM], F32R)],
        )
        r_area = sb("r_area", [P, 2 * RW])
        S = alternatives(
            None,
            [("x_tok", [P, TB, D_MODEL], F32), ("xs_tok", [DEC_SEQ, D_MODEL], F32)],
            [("fq", [P, FOX_HEADS, NT], F32), ("fk", [P, 4, NT], F32), ("fv_tok", [P, TB, 512], F32),
             ("fv_s", [DEC_SEQ, 512], F32), ("fk_tok", [P, TB, 512], F32),
             ("foS", [P, 4, DEC_SEQ], F32), ("fq_new", [P, FOX_HEADS, DEC_SEQ], F32),
             ("flogT", [FOX_HEADS, NT], F32), ("flogf", [P, TB + 1, FOX_HEADS], F32), ("clogf", [P, CB, FOX_HEADS], F32)],
            [("ckv", [P, MT, NT], F32), ("wukv", [P, MT, 1024], F32),
             ("qn", [P, 4, NT], F32), ("qpe", [P, 2, NT], F32), ("kn", [P, 4, SEQ], F32),
             ("vm", [P, TB, 512], F32), ("ckv_s", [DEC_SEQ, 512], F32), ("moS", [P, 4, DEC_SEQ], F32),
             ("mo_tok", [P, TB, 512], F32)],
            [("z0", [P, MT, NT], F32), ("z2", [P, MT, 1024], F32),
             ("z3", [P, 4, NT], F32), ("z4", [P, 2, NT], F32), ("msP", [P, CACHED], F32),
             ("msPT", [P, CB + 1, P], F32)],
            [("z5", [P, MT, NT], F32), ("z7", [P, MT, 1024], F32),
             ("z8", [P, 4, NT], F32), ("z9", [P, 2, NT], F32),
             ("wuqn", [P, QT, 4, P], F32), ("wuqp", [P, QT, 4, 64], F32), ("cq", [P, QT, NT], F32),
             ("msq", [P, QT, NT], F32)],
            [("hq", [P, 4, NT], F32), ("hf", [P, 4, NT], F32), ("hk", [P, 4, NT], F32), ("hg", [P, 4, NT], F32),
             ("hv", [P, TB, 512], F32), ("hv_s", [DEC_SEQ, 512], F32), ("ho_s", [DEC_SEQ, 512], F32),
             ("hE", [P, 2, NT], F32)],
            [("xq", [P, 4, NT], F32), ("mkT", [P, 4, N_MEM], F32), ("mvT", [P, 4, N_MEM], F32),
             ("mk_tok", [P, MB, 512], F32), ("mv_tok", [P, MB, 512], F32), ("xo_tok", [P, TB, 512], F32),
             ("xoS", [P, 4, DEC_SEQ], F32), ("xsK", [P, MB, 512], F32), ("xsV", [P, MB, 512], F32),
             ("xsKT", [P, 4, N_MEM], F32)],
            [("y0", [P, 4, NT], F32), ("y1", [P, 4, N_MEM], F32), ("y2", [P, 4, N_MEM], F32),
             ("y3", [P, MB, 512], F32), ("y4", [P, MB, 512], F32), ("mem_tok", [P, MB, D_MODEL], F32)],
            [("y5", [P, 4, NT], F32), ("xsP", [P, N_MEM], F32), ("xsPT", [P, MB, P], F32)],
            [("sqx", [P, KT, NT], F32)],
            [("t1", [P, 2, NT], F32), ("t2", [P, 2, NT], F32)],
        )

        psum = ctx.enter_context(nc.psum_tensor("psum", [P, 8, 512], F32))
        BANK = {"G0": psum[:, 0:2, :], "G1": psum[:, 2:4, :], "A0": psum[:, 4, :], "A1": psum[:, 5, :],
                "T": psum[:, 6, :], "O": psum[:, 7, :]}
        SCORES = psum[:, 4:7, :].rearrange("p a b -> p (a b)")
        ident, ones = cst[:, K_ID:K_ID + P], cst[:, K_ONES:K_ONES + P]
        COS, SIN = cst[:, K_COS:K_COS + NT], cst[:, K_SIN:K_SIN + NT]
        SEL = cst[0:FOX_HEADS, K_SEL:K_SEL + 256]
        sq = R["sq"]

        FILLED = {b: sem(f"filled_{b}") for b in BANK}
        EMPTIED = {b: sem(f"emptied_{b}") for b in BANK}
        raw_arrived = [sem(f"raw_arrived_{r}") for r in range(RAW)]
        high_split, weights_split = sem("high_split"), sem("weights_split")
        vector_chain, scalar_chain = sem("vector_chain"), sem("scalar_chain")
        square_ready, square_sum_ready, rs_ready = sem("square_ready"), sem("square_sum_ready"), sem("rs_ready")
        h32_ready, h_hi_ready, h_lo_ready = sem("h32_ready"), sem("h_hi_ready"), sem("h_lo_ready")
        x_ready, u_ready, cqn_ready, rope_ready = sem("x_ready"), sem("u_ready"), sem("cqn_ready"), sem("rope_ready")
        row_max, sample_probs, o_hi_ready = sem("row_max"), sem("sample_probs"), sem("o_hi_ready")
        ff_vector, ff_scalar, ncum_ready = sem("ff_vector"), sem("ff_scalar"), sem("ncum_ready")
        hz_vector, hz_scalar = sem("hz_vector"), sem("hz_scalar")
        hl_diff, hl_exp, hl_scaled = sem("hl_diff"), sem("hl_exp"), sem("hl_scaled")
        hd_diff, hd_exp, hd_scaled = sem("hd_diff"), sem("hd_exp"), sem("hd_scaled")
        zeros_ready, pool_products = sem("zeros_ready"), sem("pool_products")
        r32_ready, r_hi_ready, r_lo_ready = sem("r32_ready"), sem("r_hi_ready"), sem("r_lo_ready")
        DMA = {n: sem("dma_" + n) for n in (
            "vecs", "state", "foxc", "wuq", "wukv", "mlac", "mem", "xsc", "clogf",
            "k_out", "v_out", "ckv_out", "mem_out", "out", "y_out")}
        CLEARED = [*FILLED.values(), *EMPTIED.values(), *raw_arrived, high_split, weights_split, vector_chain,
                   scalar_chain, square_ready, square_sum_ready, rs_ready, h32_ready, h_hi_ready, h_lo_ready,
                   x_ready, u_ready, cqn_ready, rope_ready, row_max, sample_probs, o_hi_ready, ff_vector,
                   ff_scalar, ncum_ready, hz_vector, hz_scalar, hl_diff, hl_exp, hl_scaled, hd_diff, hd_exp,
                   hd_scaled, zeros_ready, pool_products, r32_ready, r_hi_ready, r_lo_ready, *DMA.values()]
        consts_loaded, phase_done, phase_go = sem("consts_loaded"), sem("phase_done"), sem("phase_go")

        plan = plan_layer()

        def filled(eng, name, part=None, t=plan, plus=0):
            bank, fills, _, parts = t.of[name]
            eng.wait_ge(FILLED[bank], fills + (parts if part is None else part) + plus)

        def emptied(eng, name, t=plan, plus=0):
            bank, _, uses, _ = t.of[name]
            eng.wait_ge(EMPTIED[bank], uses + 1 + plus)

        def bank_free(pe, name, t=plan, plus=0):
            bank, _, uses, _ = t.of[name]
            if uses:
                pe.wait_ge(EMPTIED[bank], uses + plus)
            return BANK[bank]

        def bank_of(name, t=plan):
            return BANK[t.of[name][0]]

        def one_bank(bank):
            return bank[:, 0, :] if len(bank.shape) == 3 else bank

        def fill_sem(name, t=plan):
            return FILLED[t.of[name][0]]

        def empty_sem(name, t=plan):
            return EMPTIED[t.of[name][0]]

        def both(tile):
            return tile.rearrange("p (a n) -> p a n", a=2)

        def g_tile(name, rows=P):
            return bank_of(name)[0:rows, :, 0:HALF]

        def end_of_phase(eng, n):
            eng.nop().then_inc(phase_done, 1)
            eng.wait_ge(phase_go, n)

        def end_of_phase_sp(sp):
            sp.wait_ge(phase_done, 4)
            for s in [phase_done, *CLEARED]:
                sp.sem_clear(s)
            sp.nop().then_inc(phase_go, 1)

        NORMS = [KT, QT, MT, KT, KT, KT, KT, KT]
        SQ0 = [sum(NORMS[:k]) for k in range(len(NORMS))]
        PE_SUMS = 6
        OHI = {"fox": 0, "mla": 5, "hg": 10, "x": 14, "mem": 19}
        RMAX = {"fox": 0, ("foxs", 0): 32, ("foxs", 1): 33, "mla": 34, "mlas": 50, "x": 51, "xs": 67}
        SPROB = {("foxs", 0): 1, ("foxs", 1): 2, "mlas": 3, "xs": 4}
        HEADS = {"fox": FOX_HEADS, "mla": MLA_HEADS, "x": X_HEADS}
        SCALE = {"fox": 1.0, "mla": (MLA_NOPE + MLA_ROPE) ** -0.5, "x": X_DIM ** -0.5}
        SCALE[("foxs", 0)] = SCALE[("foxs", 1)] = 1.0
        SCALE["mlas"], SCALE["xs"] = SCALE["mla"], SCALE["x"]
        O_TOK = {"fox": M["fo_tok"], "mla": S["mo_tok"], "x": S["xo_tok"], "hg": R["ho_tok"]}
        O_S = {"fox": S["foS"], "mla": S["moS"], "x": S["xoS"]}
        r_hi, r_lo, U = R["r_hi"], R["r_lo"], M["U"]

        VECS = 7 * 16
        SBUF_P = {("foxs", 0): (R["fPs"], R["fPTs"]), ("foxs", 1): (R["fPs"], R["fPTs"]),
                  "mlas": (S["msP"], S["msPT"]), "xs": (S["xsP"], S["xsPT"])}

        def keys(kind, qb):
            return N_MEM if kind == "x" else P * (qb + 1)

        def source(l, matrix, row, kt, col, cols):
            if matrix.startswith("w_branch"):
                w = A["w_branch"][bass.ds(l, 1), int(matrix[-1])]
            else:
                w = A["w_in" if matrix == "kpe" else matrix][bass.ds(l, 1)]
            w = w.rearrange("a r c -> (a r) c")
            return w[row if not isinstance(row, int) else slice(row, row + P * kt), col:col + cols] \
                .rearrange("(k p) c -> p k c", p=P)

        def load_slot(sp, l, s, row=0):
            matrix, _, kt, col, cols, _ = SLOTS[s]
            r = s % RAW
            if s >= RAW:
                sp.wait_ge(weights_split, s - RAW + 1)
            dst = raw[:, r, :].rearrange("p (k c) -> p k c", k=kt)
            src = source(l, matrix, row, kt, col, cols)
            if matrix == "kpe":
                sp.dma_start(dst[:, :, 0:MLA_ROPE], src).then_inc(raw_arrived[r], 16)
                sp.dma_start(dst[:, :, MLA_ROPE:P], src).then_inc(raw_arrived[r], 16)
            else:
                sp.dma_start(dst, src).then_inc(raw_arrived[r], 16)

        def raw_value(s):
            kpe = SLOT_OF["kpe", 0]
            return 16 * (s // RAW + 1) + (16 if s >= kpe and s % RAW == kpe % RAW else 0)

        def load(eng, dst, src, key):
            eng.dma_start(dst, src).then_inc(DMA[key], 16)

        def layer_of(name, l):
            return A[name][bass.ds(l, 1)]

        def sp_vectors(sp, l):
            v = layer_of("g_norm", l).rearrange("a g (t p) -> (a g t) p", p=P)
            load(sp, vecs[V_NORM:V_CQ, :], v, "vecs")
            load(sp, vecs[V_CQ:V_CKV, :], layer_of("g_mla_q", l).rearrange("a (t p) -> (a t) p", p=P), "vecs")
            load(sp, vecs[V_CKV:V_HG, :], layer_of("g_mla_kv", l).rearrange("a (t p) -> (a t) p", p=P), "vecs")
            load(sp, vecs[V_HG:V_LB, :], layer_of("g_hgrn_out", l), "vecs")
            load(sp, vecs[V_LB:V_ROWS, :], A["lb_hgrn"].rearrange("l (t p) -> (l t) p", p=P), "vecs")
            load(sp, bfox[:, :], layer_of("b_fox", l).rearrange("a h -> h a"), "vecs")
            load(sp, lbsel[:, :], A["lb_select"][bass.ds(l, 1)].rearrange("a p d -> (a p) d"), "vecs")
            clog = layer_of("cache_fox_logf", l)[:, 0].rearrange("a s h -> (a s) h")
            load(sp, S["clogf"][:, :, :], clog.rearrange("(b p) h -> p b h", p=P), "clogf")

        def sp_layer(sp, l):
            for s in range(MLP0):
                if s == SPLIT:
                    sp_vectors(sp, l)
                load_slot(sp, l, s)
            with sp.Fori(0, MLP_GROUPS) as g:
                for j in range(MLP_N):
                    s = MLP0 + j
                    matrix, _, kt, col, cols, _ = SLOTS[s]
                    sp.wait_ge(weights_split, g * MLP_N + (s - RAW + 1))
                    w = A[matrix][bass.ds(l, 1)].rearrange("a r c -> (a r) c")
                    if matrix == "w_up":
                        src = w[:, bass.ds(g * D_MODEL + col, P)]
                    else:
                        src = w[bass.ds(g * D_MODEL, D_MODEL), col:col + P]
                    sp.dma_start(raw[:, s % RAW, :].rearrange("p (k c) -> p k c", k=KT),
                                 src.rearrange("(k p) c -> p k c", p=P)).then_inc(raw_arrived[s % RAW], 16)

        def split_slot(pool, s, plus_s=0, plus_t=0, mlp=False):
            pool.wait_ge(raw_arrived[s % RAW], raw_value(s) + plus_s * (16 // RAW))
            if mlp:
                filled(pool, SLOTS[s][5][0], part=0, plus=plus_t)
            elif s >= SPLIT:
                filled(pool, SLOTS[s - SPLIT][5][-1])
            nc.gpsimd.tensor_tensor(w_hi[:, s % SPLIT, :], raw[:, s % RAW, :],
                                    zero[:, 0:1].to_broadcast([P, KT * P]), ALU.add).then_inc(high_split, 1)
            pool.wait_ge(high_split, s + 1 + plus_s)
            nc.gpsimd.tensor_tensor(w_lo[:, s % SPLIT, :], raw[:, s % RAW, :],
                                    w_hi[:, s % SPLIT, :].bitcast(F32), ALU.subtract).then_inc(weights_split, 1)

        def level_view(tile, lv):
            w = 2 * LEVELS[lv]
            return tile[:, 0:SEQ if w > DEC_SEQ else NT].rearrange("p (b w) -> p b w", w=w)

        def hg_difference(eng, i):
            h, lv = i // len(LEVELS), i % len(LEVELS)
            half = LEVELS[lv]
            e, w = level_view(S["hE"][:, i % 2, :], lv), level_view(S["hf"][:, h, :], lv)
            eng.tensor_tensor(e, w, w[:, :, half - 1:half].to_broadcast(list(e.shape)), ALU.subtract) \
                .then_inc(hl_diff, 1)

        def pool_hgrn(pool):
            emptied(pool, ("br", 1, KT - 1)), emptied(pool, ("br", 1, KT - 2))
            nc.gpsimd.memset(R["hAT"][:, :, :, :], 0.0).then_inc(zeros_ready, 1)
            nc.gpsimd.memset(R["hATs"][:, :, :], 0.0).then_inc(zeros_ready, 1)
            pool.wait_ge(hz_vector, 1 + 3 * HG_HEADS)
            nc.gpsimd.memset(eg[:, :, :], 0.0).then_inc(zeros_ready, 1)
            nc.gpsimd.memset(acc_rs[:, :, :], 0.0).then_inc(zeros_ready, 1)
            for i in range(2, HG_HEADS * len(LEVELS)):
                pool.wait_ge(hl_scaled, i - 1)
                hg_difference(nc.gpsimd, i)

        POOL_FROM = 3
        POOL_POSTS = {5: 0, 7: KT - POOL_FROM}

        def pool_post(pool, k, tmp):
            pool.wait_ge(rs_ready, k + 1)
            for t in range(POOL_FROM, KT):
                nc.gpsimd.tensor_tensor(tmp[:, t, :], U[:, t, :], rs, ALU.mult).then_inc(pool_products, 1)

        def pool_layer(pool):
            for s in range(MLP0):
                split_slot(pool, s)
                if s == SLOT_OF["gate", 2, SPLIT - 1]:
                    pool_hgrn(pool)
            pool_post(pool, 5, S["sqx"])
            with pool.Fori(0, MLP_GROUPS) as g:
                for j in range(MLP_N):
                    split_slot(pool, MLP0 + j, plus_s=g * MLP_N, plus_t=g * (MLP_N // 2), mlp=True)
            pool_post(pool, 7, sq)

        def gemm(pe, name, hi, lo, cols=(0, NT), plus_s=0, plus_t=0, wait_h=None, kts=None, wait_r=None):
            s = SLOT_OF[name]
            _, _, kt, _, ccols, results = SLOTS[s]
            c = P * results.index(name)
            G = bank_free(pe, name, plus=plus_t)
            if c == 0:
                pe.wait_ge(weights_split, s + 1 + plus_s)
            whi = w_hi[:, s % SPLIT, :].rearrange("p (k c) -> p k c", k=kt)[:, :, c:c + P]
            wlo = w_lo[:, s % SPLIT, :].rearrange("p (k c) -> p k c", k=kt)[:, :, c:c + P]
            n = cols[1] - cols[0]
            parts = [(0, HALF), (HALF, NT)] if n == NT else [cols]
            order = [(k, a) for a in range(len(parts)) for k in range(kt)]
            if wait_h is not None or wait_r is not None:
                order = [(k, a) for k in range(kt) for a in range(len(parts))]
            for k, a in order:
                c0, c1 = parts[a]
                if a == 0 and wait_h is not None:
                    pe.wait_ge(h_lo_ready, wait_h + k + 1)
                if a == 0 and wait_r is not None:
                    pe.wait_ge(r_lo_ready, wait_r + (k + 1))
                dst = G[:, a, 0:c1 - c0]
                pe.matmul(dst, whi[:, k, :], hi[:, k, c0:c1], start=k == 0, stop=False)
                pe.matmul(dst, whi[:, k, :], lo[:, k, c0:c1], start=False, stop=False)
                last = pe.matmul(dst, wlo[:, k, :], hi[:, k, c0:c1], start=False, stop=k == kt - 1)
            last.then_inc(fill_sem(name), 1)

        def stat(pe, k):
            if k == PE_SUMS:
                for t in range(KT):
                    pe.wait_ge(square_ready, SQ0[k] + t + 1)
                    for a in range(2):
                        name = ("stat", k, a)
                        dst = bank_free(pe, name) if t == 0 else bank_of(name)
                        last = pe.matmul(dst[:, 0:HALF], ones, sq[:, t, a * HALF:(a + 1) * HALF],
                                         start=t == 0, stop=t == KT - 1)
                        if t == KT - 1:
                            last.then_inc(fill_sem(name), 1)
                return
            pe.wait_ge(square_sum_ready, k + 1 - (k > PE_SUMS))
            for a in range(2):
                dst = bank_free(pe, ("stat", k, a))
                pe.matmul(dst[:, 0:HALF], ones, acc[:, a * HALF:(a + 1) * HALF], start=True, stop=True) \
                    .then_inc(fill_sem(("stat", k, a)), 1)

        def transposes(pe, name, pieces, t=plan):
            bank = one_bank(bank_free(pe, name, t=t))
            for tile, at in pieces:
                rows, cols = tile.shape[0], tile.shape[1]
                last = pe.transpose(bank[0:cols, at:at + rows], tile, ident[0:rows, 0:rows])
            last.then_inc(fill_sem(name, t), 1)

        def tokens(pe, kind, tiles):
            for tb in range(TB + 1):
                c0, c1 = (P * tb, P * tb + P) if tb < TB else (SEQ, NT)
                bank = bank_free(pe, (kind, "tok", tb))
                at = 0
                for tile in tiles:
                    rows = tile.shape[0]
                    last = pe.transpose(bank[0:c1 - c0, at:at + rows], tile[:, c0:c1], ident[0:rows, 0:rows])
                    at += rows
                last.then_inc(fill_sem((kind, "tok", tb)), 1)

        def attention(pe, kind, scores, values, dv, prepare):
            units = prompt_units(HEADS[kind])
            for i in range(len(units) + 2):
                if i < len(units):
                    qb, h = units[i]
                    dst = bank_free(pe, (kind, "S", i))[:, 0:keys(kind, qb)]
                    scores(pe, qb, h, dst).then_inc(fill_sem((kind, "S", i)), 1)
                if 1 <= i <= len(units):
                    u = i - 1
                    emptied(pe, (kind, "S", u))
                    n = keys(kind, units[u][0])
                    transposes(pe, (kind, "PT", u), [(eg[:, u % 2, b:b + P], b) for b in range(0, n, P)])
                if i >= 2:
                    u = i - 2
                    qb, h = units[u]
                    emptied(pe, (kind, "PT", u))
                    name = (kind, "O", qb)
                    dst = bank_free(pe, name) if h == 0 else bank_of(name)
                    nb = keys(kind, qb) // P
                    for b in range(nb):
                        last = pe.matmul(dst[:, h * dv:(h + 1) * dv], PT[:, u % 2, b * P:(b + 1) * P],
                                         values(b, h), start=b == 0, stop=b == nb - 1)
                    last.then_inc(fill_sem(name), 1)
                if i in PREPARED[kind]:
                    prepare(PREPARED[kind][i])

        def sample_transposes(pe, kind, n_keys):
            Ps, _ = SBUF_P[kind]
            pe.wait_ge(sample_probs, SPROB[kind])
            for j, b0 in enumerate(range(0, n_keys, 512)):
                blocks = [(Ps[:, b:min(b + P, n_keys)], b - b0) for b in range(b0, min(b0 + 512, n_keys), P)]
                bank = bank_free(pe, (kind, "PT", j))
                for tile, at in blocks:
                    cols = tile.shape[1]
                    last = pe.transpose(bank[0:cols, at:at + P], tile, ident)
                last.then_inc(fill_sem((kind, "PT", j)), 1)
            emptied(pe, (kind, "PT", (n_keys - 1) // 512))

        def to_features(pe, kind):
            emptied(pe, (kind, "O", TB - 1))
            for f in range(4):
                transposes(pe, (kind, "feat", f),
                           [(O_TOK[kind][:, tb, P * f:P * f + P], P * tb) for tb in range(TB)])

        def branch(pe, b):
            for n in range(0, KT, 2):
                gemm(pe, ("gate", b, n), h_hi, h_lo)
                gemm(pe, ("gate", b, n + 1), h_hi, h_lo)
                if n == 0 and b < 2:
                    emptied(pe, (("fox", "mla")[b], "feat", 3))
                elif n == 0:
                    pe.wait_ge(r_lo_ready, 4)
                gemm(pe, ("br", b, n), r_hi, r_lo)
                gemm(pe, ("br", b, n + 1), r_hi, r_lo)

        def fox_cached_v(g):
            return R["fVc"] if g == 0 else S["fk_tok"][:, :, :].rearrange("p a (b c) -> p (a b) c", b=2)

        def chunks(name_banks):
            return list(zip(name_banks, (0, 512, 1024), (512, 1024, CACHED)))

        def pe_fox(pe):
            fq, fk = S["fq"], S["fk"]
            gemm(pe, ("ff", 0), h_hi, h_lo, wait_h=0)
            for n in range(4):
                gemm(pe, ("fq", n), h_hi, h_lo)
            pe.wait_ge(ff_vector, 2)
            for tb in range(TB + 1):
                c0, c1 = (P * tb, P * tb + P) if tb < TB else (SEQ, NT)
                name = ("flogf", tb)
                pe.matmul(bank_free(pe, name)[0:c1 - c0, 0:FOX_HEADS], S["flogT"][:, c0:c1],
                          ident[0:FOX_HEADS, 0:FOX_HEADS], start=True, stop=True).then_inc(fill_sem(name), 1)
            pe.wait_ge(DMA["clogf"], 16)
            for j in range(2):
                name = ("clogf", j)
                bank = bank_free(pe, name)
                for b in range(4):
                    last = pe.matmul(bank[0:FOX_HEADS, P * b:P * b + P], S["clogf"][:, 4 * j + b, :], ident,
                                     start=True, stop=True)
                last.then_inc(fill_sem(name), 1)
            for n in range(4):
                gemm(pe, ("fk", n), h_hi, h_lo)
            gemm(pe, ("fv", 0), h_hi, h_lo)
            emptied(pe, ("fk", 3))
            tokens(pe, "fk", [fk[:, n, :] for n in range(4)])
            for n in range(1, 4):
                gemm(pe, ("fv", n), h_hi, h_lo)
            emptied(pe, ("fv", 3))
            tokens(pe, "fv", [R["fvT"][:, n, :] for n in range(4)])
            pe.wait_ge(ncum_ready, 1)
            emptied(pe, ("fv", "tok", TB))

            def scores(pe, qb, h, dst):
                n = dst.shape[1]
                pe.matmul(dst, head_rows[:, h:h + 1].to_broadcast([P, P]), M["ncum_parts"][:, 0:n],
                          start=True, stop=True)
                return pe.matmul(dst, fq[:, h, P * qb:P * qb + P], fk[:, h // 2, 0:n],
                                 start=False, stop=True, skip_group_check=True)

            def cached_keys(name):
                _, g, _, j = name
                f, half = j // 2, j % 2
                if j == 0:
                    pe.wait_ge(DMA["foxc"], 48 + 16 * g)
                transposes(pe, name, [(R["fKc"][:, 4 * half + b, P * f:P * f + P], P * b) for b in range(4)])

            attention(pe, "fox", scores, lambda b, h: S["fv_tok"][:, b, 64 * h:64 * h + 64], FOX_DIM, cached_keys)
            for g in range(2):
                kind = ("foxs", g)
                for j in (2, 3):
                    emptied(pe, ("foxs", g, "KT", j))
                for bank, c0, c1 in chunks(("A0", "A1", "T")):
                    dst = bank_free(pe, (kind, "S", bank))
                    pe.matmul(dst[:, 0:c1 - c0], SEL[:, P * g:P * g + P], M["ncums"][:, c0:c1],
                              start=True, stop=True)
                    for f in range(2):
                        k = R["fKT"][:, f, c0:c1] if c0 < PAST_LEN else fk[:, 2 * g + f, SEQ:NT]
                        q = S["fq_new"][:, :, :].rearrange("p h n -> p (h n)")
                        q = q[:, 64 * (2 * g + f):64 * (2 * g + f) + 64]
                        last = pe.matmul(dst[64 * f:64 * f + 64, 0:c1 - c0], q, k,
                                         start=False, stop=True, skip_group_check=True)
                    last.then_inc(fill_sem((kind, "S", bank)), 1)
                if g == 0:
                    for j in range(4):
                        cached_keys(("foxs", 1, "KT", j))
                sample_transposes(pe, kind, CACHED)
                dst = bank_free(pe, (kind, "PV"))
                PTs = R["fPTs"]
                for f in range(2):
                    out = dst[:, 64 * f:64 * f + 64]
                    for b in range(CB):
                        pe.matmul(out, fox_cached_v(g)[:, b, P * f:P * f + P], PTs[:, b, 64 * f:64 * f + 64],
                                  start=b == 0, stop=False)
                    c = 256 * g + P * f
                    last = pe.matmul(out, S["fv_s"][:, c:c + P], PTs[0:DEC_SEQ, CB, 64 * f:64 * f + 64],
                                     start=False, stop=True)
                last.then_inc(fill_sem((kind, "PV")), 1)
            to_features(pe, "fox")
            branch(pe, 0)

        def rot(pe, j, tile):
            for a in range(2):
                name = ("rot", j, a)
                pe.matmul(bank_free(pe, name)[:, 0:HALF], cst[:, K_ROT:K_ROT + P], tile[:, a * HALF:(a + 1) * HALF],
                          start=True, stop=True).then_inc(fill_sem(name), 1)

        def pe_mla(pe):
            ckv, kpe, wukv, qn, qpe = S["ckv"], R["kpe"], S["wukv"], S["qn"], S["qpe"]
            cq, kn, vm = S["cq"], S["kn"], S["vm"]
            for n in range(QT):
                gemm(pe, ("cq", n), h_hi, h_lo)
            for n in range(MT):
                gemm(pe, ("ckv", n), h_hi, h_lo)
                if n == 0:
                    stat(pe, 1)
            gemm(pe, ("kpe", 0), h_hi, h_lo)
            stat(pe, 2)
            emptied(pe, ("kpe", 0))
            rot(pe, 0, kpe)
            pe.wait_ge(cqn_ready, 1)
            pe.wait_ge(DMA["wuq"], 32 * QT)
            for n in range(6):
                name = ("qn", n) if n < 4 else ("qpe", n - 4)
                G = bank_free(pe, name)
                for a in range(2):
                    for k in range(QT):
                        w = S["wuqn"][:, k, n, :] if n < 4 else \
                            S["wuqp"][:, k, 2 * (n - 4):2 * (n - 4) + 2, :].rearrange("p a b -> p (a b)")
                        last = pe.matmul(G[:, a, 0:HALF], w, cq[:, k, a * HALF:(a + 1) * HALF],
                                         start=k == 0, stop=k == QT - 1)
                last.then_inc(fill_sem(name), 1)
            emptied(pe, ("qpe", 0))
            rot(pe, 1, qpe[:, 0, :])
            emptied(pe, ("qpe", 1))
            rot(pe, 2, qpe[:, 1, :])
            pe.wait_ge(rope_ready, 3)
            tokens(pe, "ckv", [ckv[:, 0, :], ckv[:, 1, :], kpe[0:MLA_ROPE, :]])
            pe.wait_ge(DMA["wukv"], 16)
            for h in range(4):
                G = bank_free(pe, ("kn", h))
                for c in range(MT):
                    last = pe.matmul(G[:, 0, :], wukv[:, c, 256 * h:256 * h + P], ckv[:, c, 0:SEQ],
                                     start=c == 0, stop=c == MT - 1)
                last.then_inc(fill_sem(("kn", h)), 1)
            for tb in range(TB):
                G = bank_free(pe, ("vm", tb))
                for c in range(MT):
                    wv = wukv[:, c, :].rearrange("p (h t d) -> p h t d", h=4, t=2)[:, :, 1, :]
                    last = pe.matmul(G[:, 0, :].rearrange("p (h d) -> p h d", h=4), ckv[:, c, P * tb:P * tb + P], wv,
                                     start=c == 0, stop=c == MT - 1)
                last.then_inc(fill_sem(("vm", tb)), 1)
            emptied(pe, ("kn", 3)), emptied(pe, ("vm", 3)), emptied(pe, ("vm", 2))

            def scores(pe, qb, h, dst):
                r, n = 64 * (h % 2), dst.shape[1]
                pe.matmul(dst, qn[:, h, P * qb:P * qb + P], kn[:, h, 0:n], start=True, stop=False)
                return pe.matmul(dst, qpe[r:r + 64, h // 2, P * qb:P * qb + P], kpe[r:r + 64, 0:n],
                                 start=False, stop=True)

            def latent(name):
                kind = name[1]
                if kind == "ckvT":
                    c, half = name[2] // 2, name[2] % 2
                    if name[2] == 0:
                        pe.wait_ge(DMA["mlac"], 48)
                    transposes(pe, name, [(R["ckvc"][:, 4 * half + b, P * c:P * c + P], P * b) for b in range(4)])
                elif kind == "kpeT":
                    transposes(pe, name, [(R["kpec"][:, 4 * name[2] + b, :], P * b) for b in range(4)])
                elif kind == "wukT":
                    transposes(pe, name, [(wukv[:, name[2], 256 * h:256 * h + P], P * h) for h in range(4)])
                else:
                    emptied(pe, ("mlas", "wukT", 0)), emptied(pe, ("mlas", "wukT", 1))
                    dst = bank_free(pe, name)
                    for c in range(MT):
                        for h in range(4):
                            last = pe.matmul(dst[:, P * c + 32 * h:P * c + 32 * h + 32],
                                             R["wukT"][:, h, P * c:P * c + P], qn[:, h, SEQ:NT], start=True, stop=True)
                    last.then_inc(fill_sem(name), 1)

            attention(pe, "mla", scores, lambda b, h: vm[:, b, P * h:P * h + P], MLA_V, latent)
            emptied(pe, ("mlas", "qabs"))
            for bank, c0, c1 in chunks(("A0", "A1", "T")):
                dst = bank_free(pe, ("mlas", "S", bank))
                old = c0 < PAST_LEN
                for c in range(MT):
                    k = R["ckvT"][:, c, c0:c1] if old else ckv[:, c, SEQ:NT]
                    pe.matmul(dst[:, 0:c1 - c0], R["qabs"][:, c, :], k, start=c == 0, stop=c == MT - 1)
                for j in range(4):
                    r = 64 * (j % 2)
                    k = R["kpeT"][r:r + 64, c0:c1] if old else kpe[r:r + 64, SEQ:NT]
                    last = pe.matmul(dst[32 * j:32 * j + 32, 0:c1 - c0], qpe[r:r + 64, j // 2, SEQ:NT], k,
                                     start=False, stop=True, skip_group_check=True)
                last.then_inc(fill_sem(("mlas", "S", bank)), 1)
            sample_transposes(pe, "mlas", CACHED)
            dst = bank_free(pe, ("mlas", "PV"))
            for c in range(MT):
                for b in range(CB):
                    pe.matmul(dst[:, P * c:P * c + P], R["ckvc"][:, b, P * c:P * c + P], S["msPT"][:, b, :],
                              start=b == 0, stop=False)
                last = pe.matmul(dst[:, P * c:P * c + P], S["ckv_s"][:, P * c:P * c + P],
                                 S["msPT"][0:DEC_SEQ, CB, :], start=False, stop=True)
            last.then_inc(fill_sem(("mlas", "PV")), 1)
            emptied(pe, ("mlas", "PV"))
            dst = bank_free(pe, ("mlas", "o"))
            for h in range(4):
                for c in range(MT):
                    last = pe.matmul(dst[:, 32 * h:32 * h + 32], wukv[:, c, 256 * h + P:256 * h + 2 * P],
                                     R["lat"][:, c, 32 * h:32 * h + 32], start=c == 0, stop=c == MT - 1)
            last.then_inc(fill_sem(("mlas", "o")), 1)
            to_features(pe, "mla")
            branch(pe, 1)

        def pe_hgrn(pe):
            hq, lc, hk = S["hq"], S["hf"], S["hk"]
            for kind in ("hf", "hg", "hq", "hi"):
                for n in range(4):
                    gemm(pe, (kind, n), h_hi, h_lo)
            emptied(pe, ("hi", 3)), emptied(pe, ("hi", 2))
            tokens(pe, "hi", [R["hviT"][:, n, :] for n in range(4)])
            emptied(pe, ("hi", "tok", TB)), emptied(pe, ("hi", "tok", TB - 1))
            def products(h, lv):
                name = ("hgA", h, lv)
                G = bank_free(pe, name)
                diagonal = lv == NL - 1
                if not diagonal:
                    i = h * len(LEVELS) + lv
                    pe.wait_ge(hl_scaled, i + 1)
                    q, k = eg[:, i % 2, :], acc_rs[:, i % 2, :]
                else:
                    q, k = hq[:, h, :], hk[:, h, :]
                for tb in range(TB):
                    last = pe.matmul(G[:, 0, P * tb:P * tb + P], k[:, P * tb:P * tb + P], q[:, P * tb:P * tb + P],
                                     start=True, stop=True)
                if diagonal or LEVELS[lv] < DEC_SEQ:
                    last = pe.matmul(G[0:DEC_SEQ, 1, 0:DEC_SEQ], k[:, SEQ:NT], q[:, SEQ:NT], start=True, stop=True)
                last.then_inc(fill_sem(name), 1)

            def state_updates(h):
                emptied(pe, ("hg", "kdTs", h)), emptied(pe, ("hg", "kdT", h))
                dst = bank_free(pe, ("hg", "U", h))
                for tb in range(TB):
                    last = pe.matmul(dst[:, P * tb:P * tb + P], R["hkdT"][:, tb, :], S["hv"][:, tb, P * h:P * h + P],
                                     start=True, stop=True)
                last.then_inc(fill_sem(("hg", "U", h)), 1)
                dst = bank_free(pe, ("hg", "Us", h))
                pe.matmul(dst[:, 0:P], R["hkdTs"][:, :], S["hv_s"][:, P * h:P * h + P], start=True, stop=True) \
                    .then_inc(fill_sem(("hg", "Us", h)), 1)

            def outputs(h):
                emptied(pe, ("hgA", h, NL - 1))
                emptied(pe, ("hg", "U", h))
                dst = bank_free(pe, ("hg", "O", h))
                for tb in range(TB):
                    out = dst[:, P * tb:P * tb + P]
                    last = pe.matmul(out, R["hAT"][:, h % 2, tb, :], S["hv"][:, tb, P * h:P * h + P],
                                     start=True, stop=tb == 0)
                    if tb:
                        last = pe.matmul(out, R["hqd"][:, P * tb:P * tb + P], R["hST"][:, tb - 1, :],
                                         start=False, stop=True)
                last.then_inc(fill_sem(("hg", "O", h)), 1)
                if h == 0:
                    pe.wait_ge(DMA["state"], 16)
                dst = bank_free(pe, ("hg", "Os", h))
                pe.matmul(dst[0:DEC_SEQ, 0:P], R["hATs"][:, h % 2, :], S["hv_s"][:, P * h:P * h + P],
                          start=True, stop=False)
                pe.matmul(dst[0:DEC_SEQ, 0:P], R["hqd"][:, SEQ:NT], R["hS0"][:, h, :], start=False, stop=True) \
                    .then_inc(fill_sem(("hg", "Os", h)), 1)

            for h in range(HG_HEADS + 1):
                for lv in range(NL):
                    if h < HG_HEADS:
                        products(h, lv)
                    if h and lv == HG_STEP_U:
                        state_updates(h - 1)
                    if h and lv == HG_STEP_O:
                        outputs(h - 1)
                if h < HG_HEADS:
                    pe.wait_ge(hd_scaled, h + 1)
                    kd = R["hkd"]
                    transposes(pe, ("hg", "kdT", h), [(kd[:, P * tb:P * tb + P], P * tb) for tb in range(TB)])
                    transposes(pe, ("hg", "kdTs", h), [(kd[:, SEQ:NT], 0)])
            for f in range(4):
                emptied(pe, ("hg", "O", f)), emptied(pe, ("hg", "Os", f))
                name = ("hg", "feat", f)
                G = bank_free(pe, name)
                for tb in range(TB):
                    pe.transpose(G[:, 0, P * tb:P * tb + P], R["ho_tok"][:, tb, P * f:P * f + P], ident)
                pe.transpose(G[:, 1, 0:DEC_SEQ], S["ho_s"][:, P * f:P * f + P], ident[0:DEC_SEQ, 0:DEC_SEQ]) \
                    .then_inc(fill_sem(name), 1)
            branch(pe, 2)

        def pe_layer(pe):
            stat(pe, 0)
            pe.wait_ge(DMA["vecs"], VECS)
            transposes(pe, ("vec",), [(vecs[0:V_ROWS, :], 0)])
            pe_fox(pe)
            pe_mla(pe)
            pe_hgrn(pe)
            pe.wait_ge(DMA["mem"], 16)

            def memory_transposes(j):
                transposes(pe, ("memT", j), [(S["mem_tok"][:, b, P * (2 * j + f):P * (2 * j + f) + P], 256 * f + P * b)
                                             for f in range(2) for b in range(MB)])

            def memory(kind, n):
                gemm(pe, (kind, n), R["m_hi"], R["m_lo"], cols=(0, N_MEM))

            for n in range(KT):
                if n % (KT // 2) == 0:
                    memory_transposes(4 * n // KT), memory_transposes(4 * n // KT + 1)
                gemm(pe, ("out", n), h_hi, h_lo, wait_h=KT if n == 0 else None)
            emptied(pe, ("memT", 3)), emptied(pe, ("memT", 2))
            memory("memk", 0)
            stat(pe, 3)
            for n in range(1, 4):
                memory("memk", n)
            memory("memv", 0), memory("memv", 1)
            stat(pe, 4)
            memory("memv", 2), memory("memv", 3)
            gemm(pe, ("xq", 0), h_hi, h_lo, wait_h=2 * KT)
            for kind, tile in (("memk", S["mkT"]), ("memv", S["mvT"])):
                emptied(pe, (kind, 3)), emptied(pe, (kind, 2))
                for b in range(MB):
                    transposes(pe, (kind, "tok", b), [(tile[:, n, P * b:P * b + P], P * n) for n in range(4)])
            for n in range(1, 4):
                gemm(pe, ("xq", n), h_hi, h_lo)
            xq = S["xq"]
            emptied(pe, ("memv", "tok", 1)), emptied(pe, ("memv", "tok", 0))
            emptied(pe, ("xq", 3)), emptied(pe, ("xq", 2))

            def scores(pe, qb, h, dst):
                return pe.matmul(dst, xq[:, h, P * qb:P * qb + P], S["mkT"][:, h, :], start=True, stop=True)

            def cached_memory(name):
                j = name[2]
                if j == 0:
                    pe.wait_ge(DMA["xsc"], 32)
                transposes(pe, name, [(S["xsK"][:, b, P * (2 * j + f):P * (2 * j + f) + P], 256 * f + P * b)
                                      for f in range(2) for b in range(MB)])

            attention(pe, "x", scores, lambda b, h: S["mv_tok"][:, b, P * h:P * h + P], X_DIM, cached_memory)
            emptied(pe, ("xs", "KT", 0)), emptied(pe, ("xs", "KT", 1))
            dst = bank_free(pe, ("xs", "S", "A0"))
            for j in range(4):
                last = pe.matmul(dst[32 * j:32 * j + 32, 0:N_MEM], xq[:, j, SEQ:NT], S["xsKT"][:, j, :],
                                 start=True, stop=True)
            last.then_inc(fill_sem(("xs", "S", "A0")), 1)
            sample_transposes(pe, "xs", N_MEM)
            dst = bank_free(pe, ("xs", "PV"))
            for j in range(4):
                for b in range(MB):
                    last = pe.matmul(dst[:, 32 * j:32 * j + 32], S["xsV"][:, b, P * j:P * j + P],
                                     S["xsPT"][:, b, 32 * j:32 * j + 32], start=b == 0, stop=b == MB - 1)
            last.then_inc(fill_sem(("xs", "PV")), 1)
            to_features(pe, "x")
            emptied(pe, ("x", "feat", 3))
            for n in range(KT):
                gemm(pe, ("xo", n), r_hi, r_lo)
            stat(pe, 5)
            stat(pe, 6)
            with pe.Fori(0, MLP_GROUPS) as g:
                for n in range(KT):
                    gemm(pe, ("up", n), h_hi, h_lo, plus_s=g * MLP_N, plus_t=g * (MLP_N // 2),
                         wait_h=3 * KT if n == 0 else None)
                for n in range(KT):
                    gemm(pe, ("down", n), r_hi, r_lo, plus_s=g * MLP_N, plus_t=g * (MLP_N // 2),
                         wait_r=4 + g * KT if n == 0 else None)
            stat(pe, 7)

        def act_code():
            n = [0]

            def chain(ins):
                ins.then_inc(scalar_chain, 1)
                n[0] += 1

            def wait_chain(act):
                act.wait_ge(scalar_chain, n[0])

            copy = nc.scalar.copy

            def exp(out, in_, **kw):
                return nc.scalar.activation(out, in_, ACT.Exp, **kw)

            def rs_of(act, k, features):
                for a in range(2):
                    name = ("stat", k, a)
                    filled(act, name)
                    nc.scalar.activation(acc[:, a * HALF:(a + 1) * HALF], bank_of(name)[:, 0:HALF], ACT.Ln,
                                         bias=eps[:, 0:1], scale=1.0 / features).then_inc(empty_sem(name), 1)
                emptied(act, ("stat", k, 1)), emptied(act, ("stat", k, 0))
                exp(rs, acc, scale=-0.5).then_inc(rs_ready, 1)

            def h_high(act, base, tiles=range(KT)):
                for t in tiles:
                    act.wait_ge(h32_ready, base + t + 1)
                    copy(h_hi[:, t, :], sq[:, t, :]).then_inc(h_hi_ready, 1)

            def evacuate(act, name, out):
                filled(act, name)
                copy(out, g_tile(name, out.shape[0])).then_inc(empty_sem(name), 1)

            def square_and_keep(act, name, sq_tile, keep):
                filled(act, name)
                nc.scalar.activation(both(sq_tile), g_tile(name), ACT.Square).then_inc(square_ready, 1)
                copy(both(keep), g_tile(name)).then_inc(empty_sem(name), 1)

            def keep_prepared(act, name):
                filled(act, name)
                bank, j = one_bank(bank_of(name)), name[-1]
                if name[0] == "foxs":
                    out = R["fKT"][:, j // 2, 512 * (j % 2):512 * (j % 2) + 512]
                elif name[0] == "xs":
                    out, bank = S["xsKT"][:, 2 * j:2 * j + 2, :], bank.rearrange("p (f n) -> p f n", f=2)
                elif name[1] == "ckvT":
                    out = R["ckvT"][:, j // 2, 512 * (j % 2):512 * (j % 2) + 512]
                elif name[1] == "kpeT":
                    out = R["kpeT"][:, 512 * j:512 * j + 512]
                elif name[1] == "wukT":
                    out, bank = R["wukT"][:, :, P * j:P * j + P], bank.rearrange("p (h c) -> p h c", h=4)
                else:
                    out, bank = R["qabs"][:, :, :], bank[:, 0:256].rearrange("p (c n) -> p c n", c=2)
                copy(out, bank).then_inc(empty_sem(name), 1)

            def attention(act, kind):
                units = prompt_units(HEADS[kind])
                for i in range(len(units) + 3):
                    if i < len(units):
                        nk = keys(kind, units[i][0])
                        act.wait_ge(row_max, RMAX[kind] + i + 1)
                        if i >= 2:
                            filled(act, (kind, "PT", i - 2))
                        exp(eg[:, i % 2, 0:nk], bank_of((kind, "S", i))[:, 0:nk], bias=negmax[:, i:i + 1],
                            scale=SCALE[kind], accum_out=rsum[:, i:i + 1]).then_inc(empty_sem((kind, "S", i)), 1)
                    if i - 1 in PREPARED[kind]:
                        keep_prepared(act, PREPARED[kind][i - 1])
                    if 1 <= i <= len(units):
                        u = i - 1
                        nk = keys(kind, units[u][0])
                        filled(act, (kind, "PT", u))
                        if u >= 2:
                            qb, h = units[u - 2]
                            filled(act, (kind, "O", qb), part=h + 1)
                        copy(PT[:, u % 2, 0:nk], one_bank(bank_of((kind, "PT", u)))[:, 0:nk]) \
                            .then_inc(empty_sem((kind, "PT", u)), 1)

            def sample(act, kind, n_keys, o_out, prepared=()):
                Ps, PTs = SBUF_P[kind]
                act.wait_ge(row_max, RMAX[kind] + 1)
                for j, c0 in enumerate(range(0, n_keys, 512)):
                    c1 = min(c0 + 512, n_keys)
                    name = (kind, "S", ("A0", "A1", "T")[j])
                    exp(Ps[:, c0:c1], SCORES[:, c0:c1], bias=negmax[:, 63:64], scale=SCALE[kind],
                        accum_out=rsum[:, 60 + j:61 + j]).then_inc(empty_sem(name), 1)
                for name in prepared:
                    keep_prepared(act, name)
                for j, c0 in enumerate(range(0, n_keys, 512)):
                    name = (kind, "PT", j)
                    filled(act, name)
                    nb = (min(c0 + 512, n_keys) - c0) // P
                    if nb:
                        copy(PTs[:, 4 * j:4 * j + nb, :], bank_of(name)[:, 0:nb * P].rearrange("p (b c) -> p b c", b=nb)) \
                            .then_inc(empty_sem(name), 1)
                    else:
                        copy(PTs[0:DEC_SEQ, 4 * j, :], bank_of(name)[0:DEC_SEQ, 0:P]).then_inc(empty_sem(name), 1)
                name = (kind, "PV")
                filled(act, name)
                if kind[0] == "foxs":
                    pv = bank_of(name)[:, 0:P].rearrange("p (f j n) -> p f j n", f=2, j=2)
                    chain(copy(o_out[0:64], pv[0:64, :, 0, :]))
                    copy(o_out[64:P], pv[64:P, :, 1, :]).then_inc(empty_sem(name), 1)
                    return
                n_cols = o_out.shape[1] * o_out.shape[2]
                copy(o_out, bank_of(name)[:, 0:n_cols].rearrange("p (a b) -> p a b", a=o_out.shape[1])) \
                    .then_inc(empty_sem(name), 1)

            def o_high(act, kind):
                copy(r_hi[:, 0:4, SEQ:NT], O_S[kind][:, :, :]).then_inc(o_hi_ready, 1)
                for f in range(4):
                    name = (kind, "feat", f)
                    filled(act, name)
                    copy(r_hi[:, f, 0:SEQ], bank_of(name)).then_inc(o_hi_ready, 1)

            def gates(act, b):
                for m in range(KT):
                    filled(act, ("gate", b, m))
                    if m >= 2:
                        emptied(act, ("br", b, m - 2))
                    exp(both(eg[:, m % 2, :]), g_tile(("gate", b, m)), scale=-1.0) \
                        .then_inc(empty_sem(("gate", b, m)), 1)

            def store(act, name, l, prompt, sample, key="out"):
                if prompt is not None:
                    dst = O["p_" + name][bass.ds(l, 1), 0]
                    dst = dst.rearrange("a s h d -> (a s) (h d)") if len(dst.shape) == 4 else \
                        dst.rearrange("a s c -> (a s) c")
                    act.dma_start(dst.rearrange("(b p) c -> p b c", p=P), prompt).then_inc(DMA[key], 16)
                if sample is not None:
                    dst = O["s_" + name][bass.ds(l, 1), 0]
                    dst = dst.rearrange("a s h d -> (a s) (h d)") if len(dst.shape) == 4 else \
                        dst.rearrange("a s c -> (a s) c")
                    act.dma_start(dst, sample).then_inc(DMA[key], 16)

            def act_lb(act):
                act.wait_ge(hz_vector, 1)
                exp(small[:, 8:16], small[:, 0:8]).then_inc(hz_scalar, 1)

            def cached(name, l, c0, c1):
                src = layer_of(name, l)[:, 0]
                src = src.rearrange("a s h d -> (a s) (h d)") if len(src.shape) == 4 else \
                    src.rearrange("a s c -> (a s) c")
                return src[:, c0:c1].rearrange("(b p) c -> p b c", p=P)

            def act_fox(act, l):
                name = ("ff", 0)
                filled(act, name)
                act.wait_ge(DMA["vecs"], VECS)
                nc.scalar.activation(both(S["flogT"][:, :]), g_tile(name, FOX_HEADS), ACT.Identity,
                                     bias=bfox[:, 0:1]).then_inc(empty_sem(name), 1)
                act.wait_ge(ff_vector, 1)
                chain(exp(eg[0:FOX_HEADS, 0, :], eg[0:FOX_HEADS, 0, :], scale=-1.0))
                wait_chain(act)
                nc.scalar.activation(eg[0:FOX_HEADS, 1, :], eg[0:FOX_HEADS, 0, :], ACT.Ln, bias=1.0) \
                    .then_inc(ff_scalar, 1)
                for m in range(4):
                    filled(act, ("fq", m))
                    for j in range(2):
                        r = slice(64 * j, 64 * j + 64)
                        ins = nc.scalar.activation(both(S["fq"][r, 2 * m + j, :]), g_tile(("fq", m))[r], ACT.Copy,
                                                   scale=FOX_DIM ** -0.5)
                        ins.then_inc(empty_sem(("fq", m)), 1) if j else chain(ins)
                emptied(act, ("flogf", TB)), emptied(act, ("flogf", TB - 1))
                store(act, "fox_logf", l, S["flogf"][:, 0:TB, :], S["flogf"][0:DEC_SEQ, TB, :], "v_out")
                for m in range(4):
                    evacuate(act, ("fk", m), both(S["fk"][:, m, :]))
                for m in range(4):
                    evacuate(act, ("fv", m), both(R["fvT"][:, m, :]))
                emptied(act, ("fk", "tok", TB)), emptied(act, ("fk", "tok", TB - 1))
                store(act, "fox_k", l, S["fk_tok"][:, :, :], M["fk_s"][:, :], "k_out")
                emptied(act, ("fv", "tok", TB)), emptied(act, ("fv", "tok", TB - 1))
                store(act, "fox_v", l, S["fv_tok"][:, :, :], S["fv_s"][:, :], "v_out")
                load(act, R["fKc"][:, :, :], cached("cache_fox_k", l, 0, 256), "foxc")
                load(act, R["fVc"][:, :, :], cached("cache_fox_v", l, 0, 256), "foxc")
                act.wait_ge(DMA["k_out"], 32)
                load(act, fox_cached_v(1), cached("cache_fox_v", l, 256, 512), "foxc")
                attention(act, "fox")
                load(act, R["fKc"][:, :, :], cached("cache_fox_k", l, 256, 512), "foxc")
                for g in range(2):
                    sample(act, ("foxs", g), CACHED, S["foS"][:, 2 * g:2 * g + 2, :],
                           [("foxs", 1, "KT", j) for j in range(4)] if g == 0 else [])
                emptied(act, (("foxs", 1), "PV"))
                o_high(act, "fox")
                emptied(act, ("fox", "feat", 3))
                act.wait_ge(DMA["v_out"], 64)
                for k in range(QT):
                    uq = layer_of("w_mla_uq", l).rearrange("a r (h c) -> (a r) h c", h=4)[P * k:P * k + P]
                    load(act, S["wuqn"][:, k, :, :], uq[:, :, 0:MLA_NOPE], "wuq")
                    load(act, S["wuqp"][:, k, :, :], uq[:, :, MLA_NOPE:], "wuq")
                load(act, S["wukv"][:, :, :], layer_of("w_mla_ukv", l).rearrange("a r c -> (a r) c")
                     .rearrange("(k p) c -> p k c", p=P), "wukv")
                gates(act, 0)

            def act_mla(act, l):
                for m in range(QT):
                    square_and_keep(act, ("cq", m), S["msq"][:, m, :], S["cq"][:, m, :])
                act.wait_ge(square_sum_ready, 2)
                for m in range(MT):
                    square_and_keep(act, ("ckv", m), S["msq"][:, m, :], S["ckv"][:, m, :])
                    if m == 0:
                        rs_of(act, 1, MLA_Q_RANK)
                emptied(act, ("br", 0, KT - 1))
                emptied(act, ("br", 0, KT - 2))
                evacuate(act, ("kpe", 0), both(R["kpe"][:, :]))
                load(act, R["ckvc"][:, :, :], cached("cache_mla_ckv", l, 0, 256), "mlac")
                kp = R["kpec"][:, :, :].rearrange("p b (t c) -> p b t c", t=2)
                for t in range(2):
                    load(act, kp[:, :, t, :], cached("cache_mla_kpe", l, 0, 64), "mlac")
                rs_of(act, 2, MLA_KV_RANK)
                for m in range(6):
                    name = ("qn", m) if m < 4 else ("qpe", m - 4)
                    evacuate(act, name, both(S["qn"][:, m, :] if m < 4 else S["qpe"][:, m - 4, :]))
                for kind, tile in (("kn", S["kn"]), ("vm", S["vm"])):
                    for m in range(4):
                        filled(act, (kind, m))
                        copy(tile[:, m, :], bank_of((kind, m))[:, 0, :]).then_inc(empty_sem((kind, m)), 1)
                emptied(act, ("ckv", "tok", TB)), emptied(act, ("ckv", "tok", TB - 1))
                o = S["mo_tok"]
                store(act, "mla_ckv", l, o[:, :, 0:256], S["ckv_s"][:, 0:256], "ckv_out")
                store(act, "mla_kpe", l, o[:, :, 256:320], S["ckv_s"][:, 256:320], "ckv_out")
                attention(act, "mla")
                sample(act, "mlas", CACHED, R["lat"][:, :, :])
                name = ("mlas", "o")
                filled(act, name)
                copy(S["moS"][:, :, :], bank_of(name)[:, 0:P].rearrange("p (h n) -> p h n", h=4)) \
                    .then_inc(empty_sem(name), 1)
                emptied(act, name)
                o_high(act, "mla")
                gates(act, 1)

            def act_hgrn(act, l):
                hf, hk, hE = S["hf"], S["hk"], S["hE"]
                emptied(act, ("mla", "feat", 3))
                act.wait_ge(DMA["ckv_out"], 64)
                for m in range(4):
                    evacuate(act, ("hf", m), both(hf[:, m, :]))

                def other(kind, m):
                    if kind == "hq":
                        evacuate(act, ("hq", m), both(S["hq"][:, m, :]))
                    elif kind == "hi":
                        if m == 0:
                            emptied(act, ("br", 1, KT - 1)), emptied(act, ("br", 1, KT - 2))
                        evacuate(act, ("hi", m), both(R["hviT"][:, m, :]))
                    else:
                        filled(act, ("hg", m))
                        exp(both(S["hg"][:, m, :]), g_tile(("hg", m)), scale=-1.0).then_inc(empty_sem(("hg", m)), 1)

                others = [(kind, m) for kind in ("hg", "hq", "hi") for m in range(4)]
                ta, tb_, tc, td, te = eg[:, 0, :], eg[:, 1, :], acc, rs, hE[:, 0, :]
                for h in range(HG_HEADS):
                    act.wait_ge(hz_vector, 2 + 3 * h)
                    chain(exp(ta, ta, scale=-1.0))
                    wait_chain(act)
                    chain(nc.scalar.activation(tb_, ta, ACT.Ln, bias=1.0))
                    exp(tc, tc).then_inc(hz_scalar, 1)
                    other(*others[3 * h])
                    act.wait_ge(hz_vector, 3 + 3 * h)
                    chain(nc.scalar.activation(tc, tc, ACT.Ln))
                    chain(nc.scalar.activation(td, td, ACT.Ln))
                    exp(hk[:, h, :], te, scale=-1.0).then_inc(hz_scalar, 1)
                    other(*others[3 * h + 1])
                    other(*others[3 * h + 2])
                load(act, R["hS0"][:, :, :], layer_of("state_hgrn", l)[:, 0].rearrange("a h c v -> (a h) c v")
                     .rearrange("h c v -> c h v"), "state")

                def keep_kd(h):
                    name = ("hg", "kdT", h)
                    filled(act, name)
                    copy(R["hkdT"][:, :, :], bank_of(name).rearrange("p (b c) -> p b c", b=TB)) \
                        .then_inc(empty_sem(name), 1)
                    name = ("hg", "kdTs", h)
                    filled(act, name)
                    copy(R["hkdTs"][:, :], bank_of(name)[0:DEC_SEQ, 0:P]).then_inc(empty_sem(name), 1)

                def output_blocks(h):
                    prompt, new = ("hg", "O", h), ("hg", "Os", h)
                    return [(bank_of(prompt)[:, P * tb:P * tb + P], P) for tb in range(TB)] + \
                        [(bank_of(new)[0:DEC_SEQ, 0:P], DEC_SEQ)]

                def output_squares(h):
                    filled(act, ("hg", "O", h)), filled(act, ("hg", "Os", h))
                    for tb, (o, rows) in enumerate(output_blocks(h)):
                        chain(nc.scalar.activation(R["hsq"][0:rows, :], o, ACT.Square,
                                                   accum_out=small[0:rows, tb:tb + 1]))
                        wait_chain(act)

                def output_scales(h):
                    for func, kw in ((ACT.Ln, lambda r: dict(bias=eps[0:r, 0:1], scale=1.0 / HG_DIM)),
                                     (ACT.Exp, lambda r: dict(scale=-0.5))):
                        wait_chain(act)
                        for rows, c0, c1 in ((P, 0, TB), (DEC_SEQ, TB, TB + 1)):
                            rms = small[0:rows, c0:c1]
                            chain(nc.scalar.activation(rms, rms, func, **kw(rows)))

                def keep_outputs(h):
                    wait_chain(act)
                    for tb, (o, rows) in enumerate(output_blocks(h)):
                        out = R["ho_tok"][:, tb, P * h:P * h + P] if tb < TB else S["ho_s"][:, P * h:P * h + P]
                        ins = nc.scalar.activation(out, o, ACT.Copy, scale=small[0:rows, tb:tb + 1])
                        if tb < TB - 1:
                            chain(ins)
                        else:
                            ins.then_inc(empty_sem(("hg", "O" if tb < TB else "Os", h)), 1)

                for h in range(HG_HEADS):
                    for lv, half in enumerate(LEVELS):
                        i = h * len(LEVELS) + lv
                        n_tok = SEQ if 2 * half > DEC_SEQ else NT
                        e = hE[:, i % 2, 0:n_tok].rearrange("p (b w) -> p b w", w=2 * half)
                        act.wait_ge(hl_diff, i + 1)
                        chain(exp(e[:, :, half:], e[:, :, half:]))
                        exp(e[:, :, 0:half], e[:, :, 0:half], scale=-1.0).then_inc(hl_exp, 1)
                        if h and lv == 1:
                            keep_kd(h - 1)
                        if h and lv == 4:
                            output_squares(h - 1)
                        if h and lv == 5:
                            output_scales(h - 1)
                        if h and lv == 6:
                            keep_outputs(h - 1)
                        if lv == 5:
                            act.wait_ge(hd_diff, h + 1)
                            chain(exp(R["hqd"][:, :], hf[:, h, :]))
                            chain(exp(R["hkd"][:, :], R["hkd"][:, :], scale=-1.0))
                            lcp = hf[:, h, 0:SEQ].rearrange("p (b w) -> p b w", w=P)
                            chain(exp(small[:, 16:16 + TB], lcp[:, :, P - 1]))
                            exp(small[:, 16 + TB:17 + TB], hf[:, h, NT - 1:NT]).then_inc(hd_exp, 1)
                keep_kd(HG_HEADS - 1)
                output_squares(HG_HEADS - 1), output_scales(HG_HEADS - 1)
                keep_outputs(HG_HEADS - 1)
                emptied(act, ("hg", "Us", HG_HEADS - 1))
                src = R["hSf"][:, :, :]
                act.dma_start(O["p_hgrn_state"][bass.ds(l, 1), 0].rearrange("a h c v -> (a h) c v")
                              .rearrange("h c v -> c h v"), src).then_inc(DMA["out"], 16)
                act.dma_start(O["s_hgrn_state"][bass.ds(l, 1), 0].rearrange("a h c v -> (a h) c v")
                              .rearrange("h c v -> c h v"), R["hS0"][:, :, :]).then_inc(DMA["out"], 16)
                for f in range(4):
                    emptied(act, ("hg", "feat", f))
                    copy(r_hi[:, f, :], hE[:, f % 2, :]).then_inc(r_hi_ready, 1)
                act.wait_ge(r_lo_ready, 4)
                load(act, S["mem_tok"][:, :, :], A["mem_prompt"][0].rearrange("(b p) c -> p b c", p=P), "mem")
                load(act, S["xsK"][:, :, :], cached("cache_mem_k", l, 0, 512), "xsc")
                load(act, S["xsV"][:, :, :], cached("cache_mem_v", l, 0, 512), "xsc")
                gates(act, 2)

            def act_cross(act, l):
                filled(act, ("gate", 2, KT - 1))
                for m in range(KT):
                    emptied(act, ("br", 2, m))
                    copy(h_hi[:, m, :], U[:, m, :]).then_inc(h_hi_ready, 1)

                def memory_high(j):
                    name = ("memT", j)
                    filled(act, name)
                    copy(R["m_hi"][:, 2 * j:2 * j + 2, :], bank_of(name).rearrange("p (f n) -> p f n", f=2)) \
                        .then_inc(o_hi_ready, 1)

                def memory(kind, m):
                    tile = S["mkT"] if kind == "memk" else S["mvT"]
                    filled(act, (kind, m))
                    copy(tile[:, m, :], bank_of((kind, m))[:, 0, 0:N_MEM]).then_inc(empty_sem((kind, m)), 1)

                for m in range(KT):
                    if m % (KT // 2) == 0:
                        memory_high(4 * m // KT), memory_high(4 * m // KT + 1)
                    square_and_keep(act, ("out", m), sq[:, m, :], U[:, m, :])
                rs_of(act, 3, D_MODEL)
                memory("memk", 0), memory("memk", 1)
                x_squares(act, 4, 0, range(0, KT // 2))
                memory("memk", 2)
                x_squares(act, 4, 0, range(KT // 2, KT))
                memory("memk", 3), memory("memv", 0), memory("memv", 1)
                rs_of(act, 4, D_MODEL)
                h_high(act, KT, range(0, 2))
                memory("memv", 2)
                h_high(act, KT, range(2, 4))
                memory("memv", 3)
                h_high(act, KT, range(4, KT))
                for kind, tile in (("mem_k", S["mk_tok"]), ("mem_v", S["mv_tok"])):
                    emptied(act, (kind.replace("_", ""), "tok", 1)), emptied(act, (kind.replace("_", ""), "tok", 0))
                    store(act, kind, l, tile[:, :, :], None, "mem_out")
                for m in range(4):
                    evacuate(act, ("xq", m), both(S["xq"][:, m, :]))
                attention(act, "x")
                sample(act, "xs", N_MEM, S["xoS"][:, :, :])
                emptied(act, ("xs", "PV"))
                o_high(act, "x")
                emptied(act, ("x", "feat", 3))
                act.wait_ge(DMA["mem_out"], 32)
                for m in range(KT):
                    square_and_keep(act, ("xo", m), S["sqx"][:, m, :], U[:, m, :])
                rs_of(act, 5, D_MODEL)
                x_squares(act, 6, KT)
                rs_of(act, 6, D_MODEL)
                h_high(act, 2 * KT)

            def x_squares(act, k, base, tiles=range(KT)):
                for t in tiles:
                    act.wait_ge(x_ready, base + t + 1)
                    nc.scalar.activation(sq[:, t, :], x[:, t, :], ACT.Square).then_inc(square_ready, 1)

            def act_mlp(act):
                with act.Fori(0, MLP_GROUPS) as g:
                    plus = g * (MLP_N // 2)
                    for m in range(KT):
                        name = ("up", m)
                        filled(act, name, plus=plus)
                        if m >= 2:
                            act.wait_ge(r32_ready, 1 + g * KT + m - 1)
                        else:
                            act.wait_ge(r32_ready, 1 + g * KT)
                        nc.scalar.activation(both(S["t1"][:, m % 2, :]), g_tile(name), ACT.Relu) \
                            .then_inc(empty_sem(name), 1)
                        if m >= 1:
                            act.wait_ge(r32_ready, 1 + g * KT + m)
                            copy(r_hi[:, m - 1, :], S["t2"][:, (m - 1) % 2, :]).then_inc(r_hi_ready, 1)
                    act.wait_ge(r32_ready, 1 + g * KT + KT)
                    copy(r_hi[:, KT - 1, :], S["t2"][:, (KT - 1) % 2, :]).then_inc(r_hi_ready, 1)
                for t in range(KT):
                    act.wait_ge(u_ready, 1)
                    nc.scalar.activation(sq[:, t, :], U[:, t, :], ACT.Square).then_inc(square_ready, 1)
                rs_of(act, 7, D_MODEL)

            def layer(act, l):
                n[0] = 0
                for t in range(KT):
                    nc.scalar.activation(sq[:, t, :], x[:, t, :], ACT.Square).then_inc(square_ready, 1)
                rs_of(act, 0, D_MODEL)
                h_high(act, 0)
                act_lb(act)
                act_fox(act, l)
                act_mla(act, l)
                act_hgrn(act, l)
                act_cross(act, l)
                act_mlp(act)
                wait_chain(act)

            return layer

        def dve_code():
            n = [0]
            V = nc.vector

            def step(v, ins):
                n[0] += 1
                ins.then_inc(vector_chain, 1)
                v.wait_ge(vector_chain, n[0])

            def square_sum(v, k, tiles):
                base = SQ0[k]
                for t in range(1, NORMS[k]):
                    v.wait_ge(square_ready, base + t + 1)
                    first = tiles[:, 0, :] if t == 1 else acc
                    ins = V.tensor_tensor(acc, first, tiles[:, t, :], ALU.add)
                    if t < NORMS[k] - 1:
                        step(v, ins)
                    else:
                        ins.then_inc(square_sum_ready, 1)

            def low(v, t, base, src):
                v.wait_ge(h_hi_ready, base + t + 1)
                V.tensor_tensor(h_lo[:, t, :], src[:, t, :], h_hi[:, t, :].bitcast(F32), ALU.subtract) \
                    .then_inc(h_lo_ready, 1)

            def post(v, k, gcol, tmp):
                v.wait_ge(rs_ready, k + 1)
                own = KT if k not in POOL_POSTS else POOL_FROM
                for t in range(own + 1):
                    if t < own:
                        n[0] += 1
                        V.scalar_tensor_tensor(tmp[:, t, :], U[:, t, :], gT[:, gcol + t:gcol + t + 1], rs,
                                               ALU.mult, ALU.mult).then_inc(vector_chain, 1)
                    if t:
                        v.wait_ge(vector_chain, n[0] - 1 if t < own else n[0])
                        V.tensor_tensor(x[:, t - 1, :], x[:, t - 1, :], tmp[:, t - 1, :], ALU.add).then_inc(x_ready, 1)
                for t in range(own, KT):
                    v.wait_ge(pool_products, POOL_POSTS[k] + t - own + 1)
                    V.scalar_tensor_tensor(x[:, t, :], tmp[:, t, :], gT[:, gcol + t:gcol + t + 1], x[:, t, :],
                                           ALU.mult, ALU.add).then_inc(x_ready, 1)

            def to_tokens(v, kind, prompt, sample, cols):
                for tb in range(TB + 1):
                    name = (kind, "tok", tb)
                    filled(v, name)
                    dst = prompt[:, tb, 0:cols] if tb < TB else sample[:, 0:cols]
                    V.tensor_copy(dst, bank_of(name)[0:dst.shape[0], 0:cols]).then_inc(empty_sem(name), 1)

            def attention(v, kind, mask, dv):
                heads = HEADS[kind]
                units = prompt_units(heads)

                def outputs(qb):
                    name = (kind, "O", qb)
                    filled(v, name)
                    inv = rinv[:, qb * heads:(qb + 1) * heads]
                    step(v, V.reciprocal(inv, rsum[:, qb * heads:(qb + 1) * heads]))
                    V.tensor_tensor(O_TOK[kind][:, qb, :].rearrange("p (h d) -> p h d", h=heads),
                                    bank_of(name).rearrange("p (h d) -> p h d", h=heads),
                                    inv.unsqueeze(2).to_broadcast([P, heads, dv]), ALU.mult) \
                        .then_inc(empty_sem(name), 1)

                for i, (qb, h) in enumerate(units):
                    name = (kind, "S", i)
                    filled(v, name)
                    bank, nk = bank_of(name), keys(kind, qb)
                    if mask is not None:
                        diag = bank[:, nk - P:nk]
                        step(v, V.tensor_tensor(diag, diag, mask, ALU.add))
                    ins = V.tensor_reduce(negmax[:, i:i + 1], bank[:, 0:nk], AX.X, ALU.max, negate=True)
                    if SCALE[kind] != 1.0:
                        step(v, ins)
                        ins = V.tensor_scalar_mul(negmax[:, i:i + 1], negmax[:, i:i + 1], SCALE[kind])
                    ins.then_inc(row_max, 1)
                    if h == 1 and qb:
                        outputs(qb - 1)
                outputs(TB - 1)

            def sample(v, kind, n_keys, masked):
                banks = ("A0", "A1", "T")[:-(-n_keys // 512)]
                for b in banks:
                    filled(v, (kind, "S", b))
                if masked:
                    new = SCORES[:, PAST_LEN:CACHED]
                    step(v, V.tensor_tensor(new, new, cst[:, K_SAMPLE:K_SAMPLE + DEC_SEQ], ALU.add))
                ins = V.tensor_reduce(negmax[:, 63:64], SCORES[:, 0:n_keys], AX.X, ALU.max, negate=True)
                if SCALE[kind] != 1.0:
                    step(v, ins)
                    ins = V.tensor_scalar_mul(negmax[:, 63:64], negmax[:, 63:64], SCALE[kind])
                ins.then_inc(row_max, 1)
                for b in banks:
                    emptied(v, (kind, "S", b))
                step(v, V.tensor_reduce(rinv[:, 62:63], rsum[:, 60:60 + len(banks)], AX.X, ALU.add))
                step(v, V.reciprocal(rinv[:, 63:64], rinv[:, 62:63]))
                Ps = SBUF_P[kind][0]
                V.tensor_scalar_mul(Ps[:, 0:n_keys], Ps[:, 0:n_keys], rinv[:, 63:64]).then_inc(sample_probs, 1)

            def o_low(v, kind):
                v.wait_ge(o_hi_ready, OHI[kind] + 1)
                step(v, V.tensor_tensor(r_lo[:, 0:4, SEQ:NT], O_S[kind][:, :, :], r_hi[:, 0:4, SEQ:NT].bitcast(F32),
                                        ALU.subtract))
                for f in range(4):
                    name = (kind, "feat", f)
                    v.wait_ge(o_hi_ready, OHI[kind] + f + 2)
                    V.tensor_tensor(r_lo[:, f, 0:SEQ], bank_of(name), r_hi[:, f, 0:SEQ].bitcast(F32), ALU.subtract) \
                        .then_inc(empty_sem(name), 1)

            def merge(v, b):
                for m in range(KT):
                    e = eg[:, m % 2, :]
                    emptied(v, ("gate", b, m))
                    step(v, V.tensor_scalar_add(e, e, 1.0))
                    step(v, V.reciprocal(e, e))
                    name = ("br", b, m)
                    filled(v, name)
                    if b == 0:
                        V.tensor_tensor(both(U[:, m, :]), g_tile(name), both(e), ALU.mult).then_inc(empty_sem(name), 1)
                    else:
                        step(v, V.tensor_tensor(both(e), g_tile(name), both(e), ALU.mult))
                        V.tensor_tensor(U[:, m, :], U[:, m, :], e, ALU.add).then_inc(empty_sem(name), 1)
                    if b == 2 and m == KT - 2:
                        for t in range(KT - 4):
                            low(v, t, KT, U)

            def vectors(v):
                name = ("vec",)
                filled(v, name)
                V.tensor_copy(gT[:, 0:V_ROWS], bank_of(name)[:, 0:V_ROWS]).then_inc(empty_sem(name), 1)
                emptied(v, name)

            def lower_bound(v):
                l0, l1 = gT[:, V_LB:V_LB + 4], gT[:, V_LB + 4:V_LB + 8]
                step(v, V.tensor_tensor(small[:, 16:20], l0, l1, ALU.max))
                step(v, V.tensor_tensor(small[:, 0:4], l0, small[:, 16:20], ALU.subtract))
                V.tensor_tensor(small[:, 4:8], l1, small[:, 16:20], ALU.subtract).then_inc(hz_vector, 1)
                v.wait_ge(hz_scalar, 1)
                step(v, V.tensor_tensor(small[:, 16:20], small[:, 8:12], small[:, 12:16], ALU.add))
                step(v, V.reciprocal(small[:, 20:24], small[:, 16:20]))
                step(v, V.tensor_tensor(small[:, 8:12], small[:, 8:12], small[:, 20:24], ALU.mult))
                step(v, V.tensor_tensor(small[:, 12:16], small[:, 12:16], small[:, 20:24], ALU.mult))
                step(v, V.tensor_scalar(small[:, 16:20], small[:, 8:12], lbsel[:, 0:1], None, ALU.mult))
                step(v, V.scalar_tensor_tensor(small[:, 24:28], small[:, 12:16], lbsel[:, 1:2], small[:, 16:20],
                                               ALU.mult, ALU.add))
                step(v, V.tensor_scalar(small[:, 28:32], small[:, 24:28], -1.0, 1.0, ALU.mult, ALU.add))

            def dve_fox(v):
                e0, e1, flog = eg[0:FOX_HEADS, 0, :], eg[0:FOX_HEADS, 1, :], S["flogT"][:, :]
                step(v, V.memset(M["ncum_parts"][:, :].bitcast(F32), 0.0))
                emptied(v, ("ff", 0))
                V.scalar_tensor_tensor(e0, flog, -1.0, flog, ALU.mult, ALU.max).then_inc(ff_vector, 1)
                v.wait_ge(ff_scalar, 1)
                V.scalar_tensor_tensor(flog, flog, 0.0, e1, ALU.min, ALU.subtract).then_inc(ff_vector, 1)
                for tb in range(TB + 1):
                    rows = P if tb < TB else DEC_SEQ
                    name = ("flogf", tb)
                    filled(v, name)
                    V.tensor_copy(S["flogf"][0:rows, tb, :], bank_of(name)[0:rows, 0:FOX_HEADS]) \
                        .then_inc(empty_sem(name), 1)
                v.wait_ge(ff_vector, 2)
                step(v, V.memset(e0, 1.0))
                parts, ncums = M["ncum_parts"], M["ncums"]
                step(v, V.tensor_tensor_scan(e1[:, 0:SEQ], e0[:, 0:SEQ], flog[:, 0:SEQ], 0.0, ALU.mult, ALU.subtract))
                high = parts[0:FOX_HEADS, :]
                step(v, V.tensor_copy(high, e1[:, 0:SEQ]))
                step(v, V.tensor_tensor(parts[LOW_ROWS:LOW_ROWS + FOX_HEADS, :], e1[:, 0:SEQ], high.bitcast(F32),
                                        ALU.subtract))
                for j in range(2):
                    name = ("clogf", j)
                    filled(v, name)
                    init = 0.0 if j == 0 else ncums[:, 511:512]
                    V.tensor_tensor_scan(ncums[:, 512 * j:512 * j + 512], e0[:, 0:512], bank_of(name)[0:FOX_HEADS, :],
                                         init, ALU.mult, ALU.subtract).then_inc(empty_sem(name), 1)
                    emptied(v, name)
                V.tensor_tensor_scan(ncums[:, PAST_LEN:CACHED], e0[:, 0:DEC_SEQ], flog[:, SEQ:NT],
                                     ncums[:, PAST_LEN - 1:PAST_LEN], ALU.mult, ALU.subtract).then_inc(ncum_ready, 1)
                for j in range(2):
                    r = slice(64 - 64 * j, 128 - 64 * j)
                    step(v, V.memset(S["fq"][r, :, :].rearrange("p (m t) n -> p m t n", t=2)[:, :, j, :], 0.0))
                emptied(v, ("fq", 3)), emptied(v, ("fq", 2))
                step(v, V.tensor_copy(S["fq_new"][:, :, :], S["fq"][:, :, SEQ:NT]))
                to_tokens(v, "fk", S["fk_tok"], M["fk_s"], 512)
                to_tokens(v, "fv", S["fv_tok"], S["fv_s"], 512)
                attention(v, "fox", cst[:, K_CAUSAL:K_CAUSAL + P], FOX_DIM)
                for g in range(2):
                    sample(v, ("foxs", g), CACHED, True)
                o_low(v, "fox")
                merge(v, 0)

            def rope(v, j, tile):
                t = eg[:, 0, :]
                for a in range(2):
                    name = ("rot", j, a)
                    c = slice(a * HALF, (a + 1) * HALF)
                    filled(v, name)
                    V.tensor_tensor(t[:, c], bank_of(name)[:, 0:HALF], SIN[:, c], ALU.mult).then_inc(empty_sem(name), 1)
                    emptied(v, name)
                step(v, V.tensor_tensor(tile, tile, COS, ALU.mult))
                V.tensor_tensor(tile, tile, t, ALU.add).then_inc(rope_ready, 1)
                v.wait_ge(rope_ready, j + 1)

            def dve_mla(v):
                cq, ckv = S["cq"], S["ckv"]
                for k, nt, tile, col in ((1, QT, cq, V_CQ), (2, MT, ckv, V_CKV)):
                    square_sum(v, k, S["msq"])
                    v.wait_ge(rs_ready, k + 1)
                    for t in range(nt):
                        ins = V.scalar_tensor_tensor(tile[:, t, :], tile[:, t, :], gT[:, col + t:col + t + 1], rs,
                                                     ALU.mult, ALU.mult)
                        if k == 1 and t == nt - 1:
                            ins.then_inc(cqn_ready, 1)
                        else:
                            step(v, ins)
                rope(v, 0, R["kpe"][:, :])
                rope(v, 1, S["qpe"][:, 0, :])
                rope(v, 2, S["qpe"][:, 1, :])
                to_tokens(v, "ckv", S["mo_tok"], S["ckv_s"], 320)
                v.wait_ge(DMA["ckv_out"], 64)
                attention(v, "mla", cst[:, K_CHUNK:K_CHUNK + P], MLA_V)
                sample(v, "mlas", CACHED, False)
                o_low(v, "mla")
                merge(v, 1)

            def dve_hgrn(v):
                hq, hf, hk, hg, hE = S["hq"], S["hf"], S["hk"], S["hg"], S["hE"]
                ta, tb_, tc, td, te = eg[:, 0, :], eg[:, 1, :], acc, rs, hE[:, 0, :]
                for h in range(HG_HEADS):
                    z = hf[:, h, :]
                    emptied(v, ("hf", h))
                    step(v, V.scalar_tensor_tensor(ta, z, -1.0, z, ALU.mult, ALU.max))
                    V.tensor_scalar(tc, z, -1.0, EXP_CLIP, ALU.mult, ALU.min).then_inc(hz_vector, 1)
                    v.wait_ge(hz_scalar, 2 + 2 * h)
                    lb, one_less = small[:, 24 + h:25 + h], small[:, 28 + h:29 + h]
                    step(v, V.tensor_scalar(tc, tc, lb, 1.0, ALU.mult, ALU.add))
                    step(v, V.tensor_scalar(td, tc, SMALL, 1.0, ALU.mult, ALU.max))
                    step(v, V.tensor_scalar_min(tc, tc, BIG))
                    V.scalar_tensor_tensor(te, z, 0.0, tb_, ALU.max, ALU.add).then_inc(hz_vector, 1)
                    v.wait_ge(hz_scalar, 3 + 2 * h)
                    step(v, V.tensor_scalar(hk[:, h, :], hk[:, h, :], one_less, None, ALU.mult))
                    step(v, V.scalar_tensor_tensor(z, z, 0.0, tb_, ALU.min, ALU.subtract))
                    step(v, V.tensor_tensor(z, z, tc, ALU.add))
                    step(v, V.tensor_tensor(z, z, td, ALU.add))
                    V.tensor_tensor_scan(te, cst[:, K_RESET:K_RESET + NT], z, 0.0, ALU.mult, ALU.add) \
                        .then_inc(hz_vector, 1)
                    v.wait_ge(hz_vector, 4 + 3 * h)
                    step(v, V.tensor_copy(z, te))
                    for m in ((), (0,), (1, 2), (3,))[h]:
                        emptied(v, ("hg", m))
                        step(v, V.tensor_scalar_add(hg[:, m, :], hg[:, m, :], 1.0))
                        step(v, V.reciprocal(hg[:, m, :], hg[:, m, :]))
                AT, ATs = R["hAT"], R["hATs"]
                items = [(h, lv) for h in range(HG_HEADS) for lv in range(len(LEVELS))]

                def scale(i):
                    h, lv = items[i]
                    half = LEVELS[lv]
                    v.wait_ge(hl_exp, i + 1)
                    if i >= 2:
                        filled(v, ("hgA", *items[i - 2]))
                    e = level_view(hE[:, i % 2, :], lv)
                    V.tensor_tensor(level_view(eg[:, i % 2, :], lv)[:, :, half:],
                                    level_view(hq[:, h, :], lv)[:, :, half:], e[:, :, half:], ALU.mult)
                    V.tensor_tensor(level_view(acc_rs[:, i % 2, :], lv)[:, :, 0:half], level_view(hk[:, h, :], lv)[:, :, 0:half],
                                    e[:, :, 0:half], ALU.mult).then_inc(hl_scaled, 1)

                def choose(h, lv):
                    name = ("hgA", h, lv)
                    filled(v, name)
                    if lv:
                        emptied(v, ("hgA", h, lv - 1))
                    G = bank_of(name)
                    mask = masks[:, lv, :].unsqueeze(1).to_broadcast([P, TB, P])
                    ins = V.copy_predicated(AT[:, h % 2, :, :], mask, G[:, 0, :].rearrange("p (b t) -> p b t", b=TB))
                    if lv == NL - 1 or LEVELS[lv] < DEC_SEQ:
                        ins = V.copy_predicated(ATs[:, h % 2, :], masks[0:DEC_SEQ, lv, 0:DEC_SEQ],
                                                G[0:DEC_SEQ, 1, 0:DEC_SEQ])
                    ins.then_inc(empty_sem(name), 1)

                def decay_differences(h):
                    kd, lc = R["hkd"], hf[:, h, :]
                    if h:
                        filled(v, ("hg", "kdT", h - 1)), filled(v, ("hg", "kdTs", h - 1))
                    ends = lc[:, 0:SEQ].rearrange("p (b w) -> p b w", w=P)
                    V.tensor_tensor(kd[:, 0:SEQ].rearrange("p (b w) -> p b w", w=P), ends,
                                    ends[:, :, P - 1:P].to_broadcast([P, TB, P]), ALU.subtract)
                    V.tensor_scalar(kd[:, SEQ:NT], lc[:, SEQ:NT], lc[:, NT - 1:NT], None, ALU.subtract) \
                        .then_inc(hd_diff, 1)

                def decay_scale(h):
                    v.wait_ge(hd_exp, h + 1)
                    V.tensor_tensor(R["hqd"][:, :], hq[:, h, :], R["hqd"][:, :], ALU.mult)
                    V.tensor_tensor(R["hkd"][:, :], hk[:, h, :], R["hkd"][:, :], ALU.mult).then_inc(hd_scaled, 1)

                def states(h):
                    name = ("hg", "U", h)
                    filled(v, name)
                    bank, ST = bank_of(name), R["hST"]
                    step(v, V.tensor_copy(ST[:, 0, :], bank[:, 0:P]))
                    for tb in range(1, TB - 1):
                        step(v, V.scalar_tensor_tensor(ST[:, tb, :], ST[:, tb - 1, :], small[:, 16 + tb:17 + tb],
                                                       bank[:, P * tb:P * tb + P], ALU.mult, ALU.add))
                    V.scalar_tensor_tensor(R["hSf"][:, h, :], ST[:, TB - 2, :], small[:, 15 + TB:16 + TB],
                                           bank[:, P * (TB - 1):P * TB], ALU.mult, ALU.add) \
                        .then_inc(empty_sem(name), 1)

                def new_state(h):
                    filled(v, ("hg", "Os", h))
                    name = ("hg", "Us", h)
                    filled(v, name)
                    V.scalar_tensor_tensor(R["hS0"][:, h, :], R["hS0"][:, h, :], small[:, 16 + TB:17 + TB],
                                           bank_of(name)[:, 0:P], ALU.mult, ALU.add).then_inc(empty_sem(name), 1)

                hg_difference(V, 0), hg_difference(V, 1)
                to_tokens(v, "hi", S["hv"], S["hv_s"], 512)
                v.wait_ge(zeros_ready, 4)
                for i, (h, lv) in enumerate(items):
                    scale(i)
                    if lv:
                        choose(h, lv - 1)
                    elif h:
                        choose(h - 1, len(LEVELS) - 1)
                        choose(h - 1, NL - 1)
                    if h and lv == HG_STEP_U + 1:
                        states(h - 1)
                    if h and lv == HG_STEP_O + 1:
                        new_state(h - 1)
                    if lv == 4:
                        decay_differences(h)
                    if lv == len(LEVELS) - 1:
                        decay_scale(h)
                h = HG_HEADS - 1
                choose(h, len(LEVELS) - 1)
                choose(h, NL - 1)
                states(h)
                new_state(h)
                emptied(v, ("hg", "Us", h))
                for f in range(5):
                    if f < 4:
                        name = ("hg", "feat", f)
                        filled(v, name)
                        if f >= 2:
                            v.wait_ge(r_lo_ready, f - 1)
                        V.scalar_tensor_tensor(hE[:, f % 2, :], bank_of(name).rearrange("p a n -> p (a n)")[:, 0:NT],
                                               gT[:, V_HG:V_HG + 1], hg[:, f, :], ALU.mult, ALU.mult) \
                            .then_inc(empty_sem(name), 1)
                    if f:
                        t = f - 1
                        v.wait_ge(r_hi_ready, t + 1)
                        if t == 0:
                            v.wait_ge(DMA["out"], 32)
                        V.tensor_tensor(r_lo[:, t, :], hE[:, t % 2, :], r_hi[:, t, :].bitcast(F32), ALU.subtract) \
                            .then_inc(r_lo_ready, 1)
                merge(v, 2)

            def dve_cross(v):
                for t in range(KT - 4, KT):
                    low(v, t, KT, U)
                for j in range(4):
                    name = ("memT", j)
                    v.wait_ge(o_hi_ready, 11 + j)
                    V.tensor_tensor(R["m_lo"][:, 2 * j:2 * j + 2, :], bank_of(name).rearrange("p (f n) -> p f n", f=2),
                                    R["m_hi"][:, 2 * j:2 * j + 2, :].bitcast(F32), ALU.subtract) \
                        .then_inc(empty_sem(name), 1)
                square_sum(v, 3, sq)
                post(v, 3, V_NORM + KT, sq)
                square_sum(v, 4, sq)
                h_pre(v, 4, 2 * KT, V_NORM + 2 * KT)
                for kind, tile in (("memk", S["mk_tok"]), ("memv", S["mv_tok"])):
                    for b in range(MB):
                        name = (kind, "tok", b)
                        filled(v, name)
                        V.tensor_copy(tile[:, b, :], bank_of(name)).then_inc(empty_sem(name), 1)
                attention(v, "x", None, X_DIM)
                sample(v, "xs", N_MEM, False)
                o_low(v, "x")
                square_sum(v, 5, S["sqx"])
                post(v, 5, V_NORM + 3 * KT, S["sqx"])
                h_pre(v, 6, 3 * KT, V_NORM + 4 * KT)

            def h_pre(v, k, base, gcol):
                v.wait_ge(rs_ready, k + 1)
                for t in range(KT + 1):
                    if t < KT:
                        V.scalar_tensor_tensor(sq[:, t, :], x[:, t, :], gT[:, gcol + t:gcol + t + 1], rs,
                                               ALU.mult, ALU.mult).then_inc(h32_ready, 1)
                    if t:
                        low(v, t - 1, base, sq)

            def dve_mlp(v):
                V.engine_nop().then_inc(r32_ready, 1)
                for t in range(KT):
                    step(v, V.memset(U[:, t, :], 0.0))
                with v.Fori(0, MLP_GROUPS) as g:
                    plus = g * (MLP_N // 2)
                    for m in range(KT):
                        name = ("up", m)
                        emptied(v, name, plus=plus)
                        t2 = S["t2"][:, m % 2, :]
                        if m >= 2:
                            v.wait_ge(r_lo_ready, 4 + g * KT + m - 1)
                        V.tensor_tensor(t2, S["t1"][:, m % 2, :], S["t1"][:, m % 2, :], ALU.mult).then_inc(r32_ready, 1)
                        v.wait_ge(r_hi_ready, 4 + g * KT + m + 1)
                        V.tensor_tensor(r_lo[:, m, :], t2, r_hi[:, m, :].bitcast(F32), ALU.subtract) \
                            .then_inc(r_lo_ready, 1)
                    for m in range(KT):
                        name = ("down", m)
                        filled(v, name, plus=plus)
                        V.tensor_tensor(both(U[:, m, :]), both(U[:, m, :]), g_tile(name), ALU.add) \
                            .then_inc(empty_sem(name), 1)
                    emptied(v, ("down", KT - 1), plus=plus), emptied(v, ("down", KT - 2), plus=plus)
                V.engine_nop().then_inc(u_ready, 1)
                square_sum(v, 7, sq)
                post(v, 7, V_NORM + 5 * KT, sq)
                v.wait_ge(x_ready, 3 * KT)

            def layer(v):
                n[0] = 0
                square_sum(v, 0, sq)
                vectors(v)
                h_pre(v, 0, 0, V_NORM)
                lower_bound(v)
                dve_fox(v)
                dve_mla(v)
                dve_hgrn(v)
                dve_cross(v)
                dve_mlp(v)

            return layer

        ends_in, ends_out = plan_ends("in"), plan_ends("out")
        block = ctx.enter_context(nc.Block())

        @block.sync
        def _(sp):
            sp.dma_start(cst[:, :], A["constants"]).then_inc(consts_loaded, 16)
            sp.dma_start(R["mask32"][:, :, :], A["level_masks"]).then_inc(consts_loaded, 16)
            end_of_phase_sp(sp)
            with sp.Fori(0, DEPTH) as l:
                sp_layer(sp, l)
                end_of_phase_sp(sp)
            t = ends_out
            for c in range(2):
                for tb in range(TB + 1):
                    emptied(sp, ("y", c * (TB + 1) + tb), t=t)
            sp.dma_start(O["y_prompt"][0].rearrange("(b p) c -> p b c", p=P), S["x_tok"][:, :, :]) \
                .then_inc(DMA["y_out"], 16)
            sp.dma_start(O["y_sample"][0], S["xs_tok"][:, :]).then_inc(DMA["y_out"], 16)
            sp.wait_ge(DMA["y_out"], 32)

        @block.gpsimd
        def _(pool):
            end_of_phase(pool, 1)
            with pool.Fori(0, DEPTH) as l:
                pool_layer(pool)
                end_of_phase(pool, l + 2)

        @block.tensor
        def _(pe):
            pe.wait_ge(consts_loaded, 32)
            pe.wait_ge(DMA["mem"], 32)
            for f in range(KT):
                transposes(pe, ("x", f), [(S["x_tok"][:, tb, P * f:P * f + P], P * tb) for tb in range(TB)], t=ends_in)
                transposes(pe, ("xs", f), [(S["xs_tok"][:, P * f:P * f + P], 0)], t=ends_in)
            end_of_phase(pe, 1)
            with pe.Fori(0, DEPTH) as l:
                pe_layer(pe)
                end_of_phase(pe, l + 2)
            for c in range(2):
                for tb in range(TB + 1):
                    c0, c1 = (P * tb, P * tb + P) if tb < TB else (SEQ, NT)
                    name = ("y", c * (TB + 1) + tb)
                    bank = bank_free(pe, name, t=ends_out)
                    for f in range(4):
                        last = pe.transpose(bank[0:c1 - c0, P * f:P * f + P], x[:, 4 * c + f, c0:c1], ident)
                    last.then_inc(fill_sem(name, ends_out), 1)

        @block.scalar
        def _(act):
            act.preload_act_table_set("natural_log_exp_and_others")
            act.dma_start(S["x_tok"][:, :, :], A["x_prompt"][0].rearrange("(b p) c -> p b c", p=P)) \
                .then_inc(DMA["mem"], 16)
            act.dma_start(S["xs_tok"][:, :], A["x_sample"][0]).then_inc(DMA["mem"], 16)
            end_of_phase(act, 1)
            layer = act_code()
            with act.Fori(0, DEPTH) as l:
                layer(act, l)
                end_of_phase(act, l + 2)

        @block.vector
        def _(v):
            nc.vector.memset(eps[:, :], EPS).then_inc(vector_chain, 1)
            nc.vector.memset(zero[:, :], 0.0).then_inc(vector_chain, 1)
            v.wait_ge(consts_loaded, 32)
            nc.vector.tensor_copy(masks[:, :, :], R["mask32"][:, :, :]).then_inc(vector_chain, 1)
            nc.vector.tensor_copy(head_rows[:, :], cst[:, K_HEAD:K_HEAD + FOX_HEADS]).then_inc(vector_chain, 1)
            for f in range(KT):
                for name, dst in ((("x", f), x[:, f, 0:SEQ]), (("xs", f), x[:, f, SEQ:NT])):
                    filled(v, name, t=ends_in)
                    nc.vector.tensor_copy(dst, bank_of(name, ends_in)[:, 0:dst.shape[1]]) \
                        .then_inc(empty_sem(name, ends_in), 1)
            emptied(v, ("x", KT - 1), t=ends_in), emptied(v, ("xs", KT - 1), t=ends_in)
            end_of_phase(v, 1)
            layer = dve_code()
            with v.Fori(0, DEPTH) as l:
                layer(v)
                end_of_phase(v, l + 2)
            for c in range(2):
                for tb in range(TB + 1):
                    name = ("y", c * (TB + 1) + tb)
                    filled(v, name, t=ends_out)
                    dst = S["x_tok"][:, tb, 512 * c:512 * c + 512] if tb < TB else S["xs_tok"][:, 512 * c:512 * c + 512]
                    nc.vector.tensor_copy(dst, bank_of(name, ends_out)[0:dst.shape[0], :]) \
                        .then_inc(empty_sem(name, ends_out), 1)


_INS = ["x_prompt", "x_sample", "cache_fox_k", "cache_fox_v", "cache_fox_logf", "cache_mla_ckv", "cache_mla_kpe",
        "state_hgrn", "cache_mem_k", "cache_mem_v", "mem_prompt", "w_in", "b_fox", "g_mla_q", "w_mla_uq",
        "g_mla_kv", "w_mla_ukv", "g_hgrn_out", "lb_hgrn", "w_branch", "w_out", "w_xq", "w_mem_k", "w_mem_v",
        "w_xo", "w_up", "w_down", "g_norm"]
_OUTS = {
    "y_prompt": (1, SEQ, D_MODEL), "y_sample": (1, DEC_SEQ, D_MODEL),
    "p_fox_k": (DEPTH, 1, SEQ, FOX_HEADS, FOX_DIM), "p_fox_v": (DEPTH, 1, SEQ, FOX_HEADS, FOX_DIM),
    "p_fox_logf": (DEPTH, 1, SEQ, FOX_HEADS), "p_mla_ckv": (DEPTH, 1, SEQ, MLA_KV_RANK),
    "p_mla_kpe": (DEPTH, 1, SEQ, MLA_ROPE), "p_hgrn_state": (DEPTH, 1, HG_HEADS, HG_DIM, HG_DIM),
    "p_mem_k": (DEPTH, 1, N_MEM, X_HEADS, X_DIM), "p_mem_v": (DEPTH, 1, N_MEM, X_HEADS, X_DIM),
    "s_fox_k": (DEPTH, 1, DEC_SEQ, FOX_HEADS, FOX_DIM), "s_fox_v": (DEPTH, 1, DEC_SEQ, FOX_HEADS, FOX_DIM),
    "s_fox_logf": (DEPTH, 1, DEC_SEQ, FOX_HEADS), "s_mla_ckv": (DEPTH, 1, DEC_SEQ, MLA_KV_RANK),
    "s_mla_kpe": (DEPTH, 1, DEC_SEQ, MLA_ROPE), "s_hgrn_state": (DEPTH, 1, HG_HEADS, HG_DIM, HG_DIM),
}


def shape_constants():
    c = np.zeros((P, K_END), np.float32)
    i = np.arange(P)
    c[:, K_ID:K_ID + P] = np.eye(P)
    c[:, K_ONES:K_ONES + P] = 1.0
    c[:, K_CAUSAL:K_CAUSAL + P] = np.where(i[:, None] >= i[None, :], 0.0, NEG_BIG)
    c[:, K_CHUNK:K_CHUNK + P] = np.where(i[:, None] // CHUNK >= i[None, :] // CHUNK, 0.0, NEG_BIG)
    j = np.arange(DEC_SEQ)
    c[:, K_SAMPLE:K_SAMPLE + DEC_SEQ] = np.where((i % DEC_SEQ)[:, None] >= j[None, :], 0.0, NEG_BIG)
    half = MLA_ROPE // 2
    for m in range(P):
        if m % MLA_ROPE < half:
            c[m + half, K_ROT + m] = -1.0
        else:
            c[m - half, K_ROT + m] = 1.0
    freq = np.float32(ROPE_THETA) ** (-np.arange(half, dtype=np.float32) / np.float32(half))
    pos = np.concatenate([np.arange(SEQ), PAST_LEN + np.arange(DEC_SEQ)]).astype(np.float32)
    ang = (pos[None, :] * freq[:, None]).astype(np.float32)
    c[:, K_COS:K_COS + NT] = np.tile(np.cos(ang), (P // half, 1))
    c[:, K_SIN:K_SIN + NT] = np.tile(np.sin(ang), (P // half, 1))
    c[:, K_RESET:K_RESET + NT] = (np.arange(NT) % P != 0)
    for g in range(2):
        for h in range(4):
            c[4 * g + h, K_SEL + P * g + 32 * h:K_SEL + P * g + 32 * h + 32] = 1.0
    for h in range(FOX_HEADS):
        c[[h, LOW_ROWS + h], K_HEAD + h] = 1.0
    masks = np.zeros((P, NL, P), np.float32)
    s, t = i[:, None], i[None, :]
    for n, w in enumerate(LEVELS):
        masks[:, n, :] = (s // (2 * w) == t // (2 * w)) & (s % (2 * w) < w) & (t % (2 * w) >= w)
    masks[:, NL - 1, :] = s == t
    select = np.zeros((DEPTH, P, DEPTH), np.float32)
    for l in range(DEPTH):
        select[l, :, 1:l + 1] = 1.0
    return {"constants": c, "level_masks": masks, "lb_select": select}


def kernel(**inputs):
    import numpy as _np
    import concourse.bacc as _bacc
    from concourse import mybir as _mybir
    from concourse.bass_utils import run_bass_kernel_spmd as _run

    nc = _bacc.Bacc("TRN2", target_bir_lowering=False, num_devices=1)
    arrays, A, O = {}, {}, {}
    given = {n: _np.ascontiguousarray(inputs[n]) for n in _INS}
    given.update(shape_constants())
    for name, a in given.items():
        arrays[f"in_{name}"] = a
        A[name] = nc.dram_tensor(f"in_{name}", a.shape, _mybir.dt.from_np(a.dtype), kind="ExternalInput").ap()
    for name, shape in _OUTS.items():
        O[name] = nc.dram_tensor(f"out_{name}", shape, _mybir.dt.float32, kind="ExternalOutput").ap()
    hybrid_encoder(nc, A, O)
    r = _run(nc, [arrays], core_ids=[0])
    return tuple(r.results[0][f"out_{name}"] for name in _OUTS)
```
